# Optimizing a Trainium2 kernel written in Bass

```python
import math
import jax
import jax.numpy as jnp
from jax import lax
import numpy as np

D_MODEL = 1024
BATCH = 1
SEQ = 1024
DEPTH = 2
DEC_BATCH = 8
DEC_SEQ = 8
PAST_LEN = 256
PAGE_SIZE = 128

MI_HEADS = 4
MI_DQK = 64
MI_DV = 128
MI_CHUNK = 64
GD_HEADS = 4
GD_DK = 128
GD_DV = 128
GD_CONV = 4
GD_CHUNK = 64
NSA_HEADS = 8
NSA_KV_HEADS = 2
HEAD_DIM = 64
CMP_BLOCK = 32
CMP_STRIDE = CMP_BLOCK // 2
CMP_HIDDEN = 256
SEL_BLOCK = 64
SEL_TOPN = 16
WINDOW = 512
FORCE_SCORE = 1e4
FOX_HEADS = 8
Q_BLOCK = 128
N_BUCKETS = 32
MAX_DISTANCE = 128
D_FF = 4 * D_MODEL
EPS = 1e-6
NEG_BIG = -1e30
N_EVEN = (DEPTH + 1) // 2
N_ODD = DEPTH // 2

MI_QKW = MI_HEADS * MI_DQK
MI_VW = MI_HEADS * MI_DV
GD_KW = GD_HEADS * GD_DK
GD_VW = GD_HEADS * GD_DV
GD_CONV_CH = 2 * GD_KW + GD_VW
EVEN_SPLITS = (MI_QKW, MI_QKW, MI_VW, MI_VW, MI_HEADS, MI_HEADS,
               GD_KW, GD_KW, GD_VW, GD_VW, GD_HEADS, GD_HEADS)
EVEN_MIX = MI_VW + GD_VW
NSA_KVW = NSA_KV_HEADS * HEAD_DIM
ODD_SPLITS = (NSA_HEADS * HEAD_DIM, 6 * NSA_KVW, 3 * NSA_HEADS,
              FOX_HEADS * HEAD_DIM, FOX_HEADS * HEAD_DIM, FOX_HEADS * HEAD_DIM, FOX_HEADS)
ODD_MIX = (NSA_HEADS + FOX_HEADS) * HEAD_DIM

kernel_name = 'hybrid_mlstm_gdn_nsa_fox_step'

def rmsnorm(x, g):
    xf = x.astype(jnp.float32)
    return (xf * lax.rsqrt(jnp.mean(xf * xf, axis=-1, keepdims=True) + EPS) * g).astype(x.dtype)

def _split(a, sizes):
    return jnp.split(a, np.cumsum(sizes)[:-1].tolist(), axis=-1)

def l2norm(x):
    return x * lax.rsqrt(jnp.sum(x * x, axis=-1, keepdims=True) + EPS)

def masked_softmax(logits, mask):
    lg = jnp.where(mask, logits.astype(jnp.float32), NEG_BIG)
    p = jnp.exp(lg - jnp.max(lg, axis=-1, keepdims=True)) * mask
    return p / jnp.maximum(jnp.sum(p, axis=-1, keepdims=True), 1e-30)

def t5_bucket(dist):
    n = jnp.maximum(dist, 0)
    exact = N_BUCKETS // 2
    nf = jnp.maximum(n, 1).astype(jnp.float32)
    large = exact + (jnp.log(nf / exact) / math.log(MAX_DISTANCE / exact)
                     * (N_BUCKETS - exact)).astype(jnp.int32)
    return jnp.where(n < exact, n, jnp.minimum(large, N_BUCKETS - 1))

def causal_conv(x, buf, w):
    T = x.shape[1]
    xp = jnp.concatenate([buf, x], axis=1)
    y = sum(xp[:, j:j + T] * w[j] for j in range(GD_CONV))
    return jax.nn.silu(y), xp[:, -(GD_CONV - 1):]

def mlstm_chunked(q, k, v, log_i, log_f, c0, n0, m0):
    B, T, H, _ = q.shape
    L = math.gcd(T, MI_CHUNK)
    nc = T // L
    tri = jnp.tril(jnp.ones((L, L), dtype=bool))

    def chunks(a):
        return jnp.moveaxis(a.reshape(B, nc, L, *a.shape[2:]), 1, 0)

    def step(carry, inp):
        c, n, m = carry
        qc, kc, vc, lic, lfc = inp
        b = jnp.cumsum(lfc, axis=1)
        d = jnp.where(tri[None, :, :, None],
                      b[:, :, None, :] - b[:, None, :, :] + lic[:, None, :, :], -jnp.inf)
        inter = b + m[:, None, :]
        m_t = jnp.maximum(inter, jnp.max(d, axis=2))
        s = jnp.einsum('bthd,bshd->btsh', qc, kc) * jnp.exp(d - m_t[:, :, None, :])
        a_inter = jnp.exp(inter - m_t)
        num = jnp.einsum('btsh,bshv->bthv', s, vc) + a_inter[..., None] * jnp.einsum('bthd,bhdv->bthv', qc, c)
        den = jnp.sum(s, axis=2) + a_inter * jnp.einsum('bthd,bhd->bth', qc, n)
        h = num / jnp.maximum(jnp.abs(den), jnp.exp(-m_t))[..., None]
        b_last = b[:, -1]
        g = b_last[:, None, :] - b + lic
        m_new = jnp.maximum(b_last + m, jnp.max(g, axis=1))
        a_prev = jnp.exp(b_last + m - m_new)
        wgt = jnp.exp(g - m_new[:, None, :])
        c = a_prev[:, :, None, None] * c + jnp.einsum('bsh,bshd,bshv->bhdv', wgt, kc, vc)
        n = a_prev[:, :, None] * n + jnp.einsum('bsh,bshd->bhd', wgt, kc)
        return (c, n, m_new), h

    (c, n, m), h = lax.scan(step, (c0, n0, m0), tuple(chunks(a) for a in (q, k, v, log_i, log_f)))
    return jnp.moveaxis(h, 0, 1).reshape(B, T, H, v.shape[-1]), c, n, m

def gated_delta_chunked(q, k, v, g, beta, s0):
    B, T, H, DK = q.shape
    DV = v.shape[-1]
    L = math.gcd(T, GD_CHUNK)
    nc = T // L

    def ch(a):
        return jnp.swapaxes(a.reshape(B, nc, L, *a.shape[2:]), 2, 3)

    q, k, v, g, beta = (ch(a) for a in (q, k, v, g, beta))
    gc = jnp.cumsum(g, axis=-1)
    idx = jnp.arange(L)
    incl = idx[:, None] >= idx[None, :]
    strict = idx[:, None] > idx[None, :]
    dec_incl = jnp.exp(jnp.where(incl, gc[..., :, None] - gc[..., None, :], -jnp.inf))
    dec_strict = jnp.where(strict, dec_incl, 0.0)
    kb = k * beta[..., None]
    a = jnp.einsum('bchtd,bchsd->bchts', kb, k) * dec_strict + jnp.eye(L, dtype=jnp.float32)
    rhs = jnp.concatenate([v * beta[..., None], kb * jnp.exp(gc)[..., None]], axis=-1)
    sol = lax.linalg.triangular_solve(a, rhs, left_side=True, lower=True)
    u, w = sol[..., :DV], sol[..., DV:]
    attn = jnp.einsum('bchtd,bchsd->bchts', q, k) * dec_incl
    q_dec = q * jnp.exp(gc)[..., None]
    g_last = gc[..., -1]
    k_dec = k * jnp.exp(g_last[..., None] - gc)[..., None]

    def step(s, inp):
        u_c, w_c, at_c, qd_c, kd_c, gl_c = inp
        v_new = u_c - jnp.einsum('bhld,bhdv->bhlv', w_c, s)
        o = jnp.einsum('bhld,bhdv->bhlv', qd_c, s) + jnp.einsum('bhts,bhsv->bhtv', at_c, v_new)
        s = jnp.exp(gl_c)[..., None, None] * s + jnp.einsum('bhld,bhlv->bhdv', kd_c, v_new)
        return s, o

    xs = tuple(jnp.moveaxis(t, 1, 0) for t in (u, w, attn, q_dec, k_dec, g_last))
    s, o = lax.scan(step, s0, xs)
    return jnp.transpose(o, (1, 0, 3, 2, 4)).reshape(B, T, H, DV), s

def even_mixer(h, w_in, w_out, b_i, b_f, mi_norm, conv_w, a_log, dt_bias, gd_norm, past):
    B, T, _ = h.shape
    f32 = jnp.float32
    mq, mk, mv, mo, mi, mf, gq, gk, gv, gz, gb, ga = _split((h @ w_in).astype(f32), EVEN_SPLITS)
    if past is None:
        c0 = jnp.zeros((B, MI_HEADS, MI_DQK, MI_DV), f32)
        n0 = jnp.zeros((B, MI_HEADS, MI_DQK), f32)
        m0 = jnp.zeros((B, MI_HEADS), f32)
        s0 = jnp.zeros((B, GD_HEADS, GD_DK, GD_DV), f32)
        conv0 = jnp.zeros((B, GD_CONV - 1, GD_CONV_CH), f32)
    else:
        c0, n0, m0, s0, conv0 = (a.astype(f32) for a in past)
    hm, c1, n1, m1 = mlstm_chunked(
        mq.reshape(B, T, MI_HEADS, MI_DQK),
        mk.reshape(B, T, MI_HEADS, MI_DQK) * MI_DQK ** -0.5,
        mv.reshape(B, T, MI_HEADS, MI_DV),
        mi + b_i, jax.nn.log_sigmoid(mf + b_f), c0, n0, m0)
    hm = rmsnorm(hm, mi_norm.reshape(MI_HEADS, MI_DV)).reshape(B, T, MI_VW) * jax.nn.sigmoid(mo)
    conv_out, conv1 = causal_conv(jnp.concatenate([gq, gk, gv], axis=-1), conv0, conv_w)
    cq, ck, cv = _split(conv_out, (GD_KW, GD_KW, GD_VW))
    cq = l2norm(cq.reshape(B, T, GD_HEADS, GD_DK)) * GD_DK ** -0.5
    ck = l2norm(ck.reshape(B, T, GD_HEADS, GD_DK))
    g = -jnp.exp(a_log) * jax.nn.softplus(ga + dt_bias)
    og, s1 = gated_delta_chunked(cq, ck, cv.reshape(B, T, GD_HEADS, GD_DV), g, jax.nn.sigmoid(gb), s0)
    og = rmsnorm(og, gd_norm) * jax.nn.silu(gz.reshape(B, T, GD_HEADS, GD_DV))
    y = jnp.concatenate([hm, og.reshape(B, T, GD_VW)], axis=-1).astype(h.dtype) @ w_out
    dt = h.dtype
    return y, (c1.astype(dt), n1.astype(dt), m1.astype(dt), s1.astype(dt), conv1.astype(dt))

def compress(kf, pos_emb, w1, w2):
    B, Tp, G, D = kf.shape
    c = kf.reshape(B, Tp // CMP_STRIDE, CMP_STRIDE, G, D)
    blocks = jnp.concatenate([c[:, :-1], c[:, 1:]], axis=2) + pos_emb[:, None, :]
    nc = blocks.shape[1]
    flat = jnp.moveaxis(blocks, 3, 2).reshape(B, nc, G, CMP_BLOCK * D)
    return jax.nn.silu(flat @ w1) @ w2

def selection_overlap(nc, ns):
    c_start = np.arange(nc)[:, None] * CMP_STRIDE
    s_start = np.arange(ns)[None, :] * SEL_BLOCK
    return ((c_start < s_start + SEL_BLOCK) & (c_start + CMP_BLOCK > s_start)).astype(np.float32)

def nsa_attend(q, q_pos, gates, kc, vc, c_end, ksel, vsel, kw, vw, w_pos, rel_bias, sel_map):
    B, Lq, G, R, D = q.shape
    scale = D ** -0.5
    tbl = rel_bias.reshape(N_BUCKETS, G, R)
    dist_c = q_pos[:, None] - c_end[None, :]
    bias_c = jnp.moveaxis(tbl[t5_bucket(dist_c)], (2, 3), (0, 1))
    pc = masked_softmax(jnp.einsum('bqgrd,bngd->bgrqn', q, kc) * scale + bias_c, dist_c >= 0)
    o_c = jnp.einsum('bgrqn,bngd->bqgrd', pc, vc)
    ns = ksel.shape[2]
    ps = jnp.einsum('bgrqn,ns->bgqs', pc, sel_map)
    blk = jnp.arange(ns)
    cur = q_pos // SEL_BLOCK
    visible = blk[None, :] * SEL_BLOCK <= q_pos[:, None]
    forced = (blk[None, :] == 0) | (blk[None, :] == cur[:, None]) | (blk[None, :] == cur[:, None] - 1)
    score = jnp.where(forced, FORCE_SCORE, jnp.where(visible, ps, -1.0))
    n_top = min(SEL_TOPN, ns)
    _, idx = lax.top_k(score, n_top)
    pick = jax.vmap(jax.vmap(lambda kb, ib: kb[ib]))
    ks = pick(ksel, idx).reshape(B, G, Lq, n_top * SEL_BLOCK, D)
    vs = pick(vsel, idx).reshape(B, G, Lq, n_top * SEL_BLOCK, D)
    pos_s = (idx[..., None] * SEL_BLOCK + jnp.arange(SEL_BLOCK)).reshape(B, G, Lq, n_top * SEL_BLOCK)
    dist_s = q_pos[None, None, :, None] - pos_s
    tbl_g = jnp.transpose(tbl, (1, 0, 2))
    bias_s = jnp.moveaxis(tbl_g[jnp.arange(G)[None, :, None, None], t5_bucket(dist_s)], -1, 2)
    p_s = masked_softmax(jnp.einsum('bqgrd,bgqkd->bgrqk', q, ks) * scale + bias_s, (dist_s >= 0)[:, :, None])
    o_s = jnp.einsum('bgrqk,bgqkd->bqgrd', p_s, vs)
    dist_w = q_pos[:, None] - w_pos[None, :]
    mask_w = (dist_w >= 0) & (dist_w < WINDOW) & (w_pos[None, :] >= 0)
    bias_w = jnp.moveaxis(tbl[t5_bucket(dist_w)], (2, 3), (0, 1))
    p_w = masked_softmax(jnp.einsum('bqgrd,bkgd->bgrqk', q, kw) * scale + bias_w, mask_w)
    o_w = jnp.einsum('bgrqk,bkgd->bqgrd', p_w, vw)
    return gates[..., 0:1] * o_c + gates[..., 1:2] * o_s + gates[..., 2:3] * o_w

def fox_attend(q, F_q, q_pos, k, v, F_k, k_pos):
    logits = (jnp.einsum('bqhd,bkhd->bhqk', q, k).astype(jnp.float32) * HEAD_DIM ** -0.5
              + jnp.moveaxis(F_q, 2, 1)[..., None] - jnp.moveaxis(F_k, 2, 1)[:, :, None, :])
    p = masked_softmax(logits, k_pos[None, :] <= q_pos[:, None])
    return jnp.einsum('bhqk,bkhd->bqhd', p, v)

def odd_mixer(h, w_in, w_out, cmp_pos, cmp_w1, cmp_w2, fox_b_f, rel_bias, w_buf, past):
    B, T, _ = h.shape
    G, R, D = NSA_KV_HEADS, NSA_HEADS // NSA_KV_HEADS, HEAD_DIM
    nq, nkv, ngate, fq, fk, fv, ff = _split(h @ w_in, ODD_SPLITS)
    q = nq.reshape(B, T, G, R, D)
    kv = nkv.reshape(B, T, 6, G, D)
    gates = jax.nn.sigmoid(ngate.astype(jnp.float32)).reshape(B, T, G, R, 3)
    fq = fq.reshape(B, T, FOX_HEADS, D)
    new_fox = jnp.stack([fk.reshape(B, T, FOX_HEADS, D), fv.reshape(B, T, FOX_HEADS, D)], axis=2)
    logf = jax.nn.log_sigmoid((ff + fox_b_f).astype(jnp.float32))
    new_nsa = kv[:, :, :4]
    new_win = kv[:, :, 4:]
    if past is None:
        start = 0
        nsa_full, fox_full, logf_full = new_nsa, new_fox, logf
        win_prev = jnp.zeros((B, WINDOW, 2, G, D), h.dtype)
    else:
        nsa_past, win_prev, fox_past, logf_past = past
        start = nsa_past.shape[1]
        nsa_full = jnp.concatenate([nsa_past.astype(h.dtype), new_nsa], axis=1)
        fox_full = jnp.concatenate([fox_past.astype(h.dtype), new_fox], axis=1)
        logf_full = jnp.concatenate([logf_past.astype(jnp.float32), logf], axis=1)
    win_all = jnp.concatenate([win_prev.astype(h.dtype), new_win], axis=1)
    wp = win_all.shape[1] - T
    new_win_state = win_all[:, -w_buf:]
    Tk = nsa_full.shape[1]
    Tp = -(-Tk // SEL_BLOCK) * SEL_BLOCK
    nsa_pad = jnp.pad(nsa_full, ((0, 0), (0, Tp - Tk), (0, 0), (0, 0), (0, 0)))
    kc = compress(nsa_pad[:, :, 0], cmp_pos[0], cmp_w1[0], cmp_w2[0])
    vc = compress(nsa_pad[:, :, 1], cmp_pos[1], cmp_w1[1], cmp_w2[1])
    nc = kc.shape[1]
    ns = Tp // SEL_BLOCK
    c_end = jnp.arange(nc) * CMP_STRIDE + (CMP_BLOCK - 1)
    ksel = jnp.transpose(nsa_pad[:, :, 2].reshape(B, ns, SEL_BLOCK, G, D), (0, 3, 1, 2, 4))
    vsel = jnp.transpose(nsa_pad[:, :, 3].reshape(B, ns, SEL_BLOCK, G, D), (0, 3, 1, 2, 4))
    sel_map = jnp.asarray(selection_overlap(nc, ns))
    fk_full, fv_full = fox_full[:, :, 0], fox_full[:, :, 1]
    F_full = jnp.cumsum(logf_full, axis=1)
    F_q = F_full[:, start:]
    k_pos = jnp.arange(Tk)
    if past is None:
        qb = math.gcd(T, Q_BLOCK)

        def block(i):
            qs = i * qb
            sl = lambda a: lax.dynamic_slice_in_dim(a, qs, qb, axis=1)
            qp = qs + jnp.arange(qb)
            wk = lax.dynamic_slice_in_dim(win_all, qs, qb + WINDOW, axis=1)
            wpos = qs - WINDOW + jnp.arange(qb + WINDOW)
            o_n = nsa_attend(sl(q), qp, sl(gates), kc, vc, c_end, ksel, vsel,
                             wk[:, :, 0], wk[:, :, 1], wpos, rel_bias, sel_map)
            o_f = fox_attend(sl(fq), sl(F_q), qp, fk_full, fv_full, F_full, k_pos)
            return o_n, o_f

        o_n, o_f = lax.map(block, jnp.arange(T // qb))
        o_n = jnp.moveaxis(o_n, 0, 1).reshape(B, T, NSA_HEADS * D)
        o_f = jnp.moveaxis(o_f, 0, 1).reshape(B, T, FOX_HEADS * D)
    else:
        q_pos = start + jnp.arange(T)
        w_pos = start - wp + jnp.arange(wp + T)
        o_n = nsa_attend(q, q_pos, gates, kc, vc, c_end, ksel, vsel, win_all[:, :, 0], win_all[:, :, 1],
                         w_pos, rel_bias, sel_map).reshape(B, T, NSA_HEADS * D)
        o_f = fox_attend(fq, F_q, q_pos, fk_full, fv_full, F_full, k_pos).reshape(B, T, FOX_HEADS * D)
    y = jnp.concatenate([o_n, o_f], axis=-1).astype(h.dtype) @ w_out
    return y, (new_nsa, new_win_state, new_fox, logf.astype(h.dtype))

def gather_pages(pool, page_table):
    g = pool[page_table]
    return g.reshape(page_table.shape[0], -1, *pool.shape[2:])

def trunk(x, past, page_table, p, w_buf):
    new = [[] for _ in range(9)]
    ie = 0
    io = 0
    for layer in range(DEPTH):
        hn = rmsnorm(x, p['norm_mix'][layer])
        if layer % 2 == 0:
            st = None if past is None else (past['mc'][ie], past['mn'][ie], past['mm'][ie],
                                            past['gs'][ie], past['gc'][ie])
            y, ns = even_mixer(hn, p['w_in_even'][ie], p['w_out_even'][ie], p['mi_b_i'][ie], p['mi_b_f'][ie],
                               p['mi_norm'][ie], p['gd_conv_w'][ie], p['gd_a_log'][ie], p['gd_dt_bias'][ie],
                               p['gd_norm'][ie], st)
            for lst, a in zip(new[:5], ns):
                lst.append(a)
            ie += 1
        else:
            st = None if past is None else (gather_pages(past['nsa_kv'][io], page_table), past['nsa_win'][io],
                                            gather_pages(past['fox_kv'][io], page_table),
                                            gather_pages(past['fox_logf'][io], page_table))
            y, ns = odd_mixer(hn, p['w_in_odd'][io], p['w_out_odd'][io], p['nsa_cmp_pos'][io],
                              p['nsa_cmp_w1'][io], p['nsa_cmp_w2'][io], p['fox_b_f'][io], p['rel_bias'],
                              w_buf, st)
            for lst, a in zip(new[5:], ns):
                lst.append(a)
            io += 1
        x = x + y
        hn = rmsnorm(x, p['norm_mlp'][layer])
        u = jnp.maximum(hn @ p['w_up'][layer], 0)
        x = x + (u * u) @ p['w_down'][layer]
    return rmsnorm(x, p['norm_final']), tuple(jnp.stack(lst) for lst in new)

def setup_inputs(seed: int = 0) -> dict:
    key = jax.random.key(seed)
    keys = iter(jax.random.split(key, 48))

    def nrm(shape, scale):
        return jax.random.normal(next(keys), shape, jnp.float32) * scale

    n_pages = PAST_LEN // PAGE_SIZE
    n_pool = (DEC_BATCH * n_pages * 5 + 3) // 4
    w_buf = min(WINDOW, PAST_LEN)
    G, HD = NSA_KV_HEADS, HEAD_DIM
    inp = {}
    inp['x_prompt'] = nrm((BATCH, SEQ, D_MODEL), 1.0)
    inp['x_sample'] = nrm((DEC_BATCH, DEC_SEQ, D_MODEL), 1.0)
    inp['state_mlstm_c'] = nrm((N_EVEN, DEC_BATCH, MI_HEADS, MI_DQK, MI_DV), 0.1)
    inp['state_mlstm_n'] = nrm((N_EVEN, DEC_BATCH, MI_HEADS, MI_DQK), 0.1)
    inp['state_mlstm_m'] = nrm((N_EVEN, DEC_BATCH, MI_HEADS), 1.0)
    inp['state_gdn_s'] = nrm((N_EVEN, DEC_BATCH, GD_HEADS, GD_DK, GD_DV), 0.1)
    inp['state_gdn_conv'] = nrm((N_EVEN, DEC_BATCH, GD_CONV - 1, GD_CONV_CH), 1.0)
    inp['cache_nsa_kv'] = nrm((N_ODD, n_pool, PAGE_SIZE, 4, G, HD), 1.0)
    inp['state_nsa_win'] = nrm((N_ODD, DEC_BATCH, w_buf, 2, G, HD), 1.0)
    inp['cache_fox_kv'] = nrm((N_ODD, n_pool, PAGE_SIZE, 2, FOX_HEADS, HD), 1.0)
    inp['cache_fox_logf'] = jax.nn.log_sigmoid(3.0 + nrm((N_ODD, n_pool, PAGE_SIZE, FOX_HEADS), 0.5))
    perm = jax.random.permutation(next(keys), n_pool)
    inp['page_table'] = perm[:DEC_BATCH * n_pages].reshape(DEC_BATCH, n_pages).astype(jnp.int32)
    inp['norm_mix'] = 1.0 + nrm((DEPTH, D_MODEL), 0.05)
    inp['norm_mlp'] = 1.0 + nrm((DEPTH, D_MODEL), 0.05)
    inp['norm_final'] = 1.0 + nrm((D_MODEL,), 0.05)
    inp['w_up'] = nrm((DEPTH, D_MODEL, D_FF), D_MODEL ** -0.5)
    inp['w_down'] = nrm((DEPTH, D_FF, D_MODEL), D_FF ** -0.5)
    inp['w_in_even'] = nrm((N_EVEN, D_MODEL, sum(EVEN_SPLITS)), D_MODEL ** -0.5)
    inp['w_out_even'] = nrm((N_EVEN, EVEN_MIX, D_MODEL), EVEN_MIX ** -0.5)
    inp['mi_b_i'] = nrm((N_EVEN, MI_HEADS), 0.1)
    inp['mi_b_f'] = 3.0 + nrm((N_EVEN, MI_HEADS), 0.5)
    inp['mi_norm'] = 1.0 + nrm((N_EVEN, MI_VW), 0.05)
    inp['gd_conv_w'] = nrm((N_EVEN, GD_CONV, GD_CONV_CH), GD_CONV ** -0.5)
    inp['gd_a_log'] = jnp.log(jax.random.uniform(next(keys), (N_EVEN, GD_HEADS), jnp.float32, 1.0, 16.0))
    dt = jnp.exp(jax.random.uniform(next(keys), (N_EVEN, GD_HEADS), jnp.float32,
                                    math.log(1e-3), math.log(1e-1)))
    inp['gd_dt_bias'] = dt + jnp.log(-jnp.expm1(-dt))
    inp['gd_norm'] = 1.0 + nrm((N_EVEN, GD_DV), 0.05)
    inp['w_in_odd'] = nrm((N_ODD, D_MODEL, sum(ODD_SPLITS)), D_MODEL ** -0.5)
    inp['w_out_odd'] = nrm((N_ODD, ODD_MIX, D_MODEL), ODD_MIX ** -0.5)
    inp['nsa_cmp_pos'] = nrm((N_ODD, 2, CMP_BLOCK, HD), 0.1)
    inp['nsa_cmp_w1'] = nrm((N_ODD, 2, CMP_BLOCK * HD, CMP_HIDDEN), (CMP_BLOCK * HD) ** -0.5)
    inp['nsa_cmp_w2'] = nrm((N_ODD, 2, CMP_HIDDEN, HD), CMP_HIDDEN ** -0.5)
    inp['fox_b_f'] = 3.0 + nrm((N_ODD, FOX_HEADS), 0.5)
    inp['rel_bias'] = nrm((N_BUCKETS, NSA_HEADS), 0.5)
    return inp

def reference(x_prompt, x_sample, state_mlstm_c, state_mlstm_n, state_mlstm_m, state_gdn_s, state_gdn_conv,
              cache_nsa_kv, state_nsa_win, cache_fox_kv, cache_fox_logf, page_table,
              norm_mix, norm_mlp, norm_final, w_up, w_down,
              w_in_even, w_out_even, mi_b_i, mi_b_f, mi_norm, gd_conv_w, gd_a_log, gd_dt_bias, gd_norm,
              w_in_odd, w_out_odd, nsa_cmp_pos, nsa_cmp_w1, nsa_cmp_w2, fox_b_f, rel_bias):
    params = dict(norm_mix=norm_mix, norm_mlp=norm_mlp, norm_final=norm_final, w_up=w_up, w_down=w_down,
                  w_in_even=w_in_even, w_out_even=w_out_even, mi_b_i=mi_b_i, mi_b_f=mi_b_f, mi_norm=mi_norm,
                  gd_conv_w=gd_conv_w, gd_a_log=gd_a_log, gd_dt_bias=gd_dt_bias, gd_norm=gd_norm,
                  w_in_odd=w_in_odd, w_out_odd=w_out_odd, nsa_cmp_pos=nsa_cmp_pos, nsa_cmp_w1=nsa_cmp_w1,
                  nsa_cmp_w2=nsa_cmp_w2, fox_b_f=fox_b_f, rel_bias=rel_bias)
    w_buf = state_nsa_win.shape[2]
    y_prompt, (p_mc, p_mn, p_mm, p_gs, p_gc, p_nkv, p_nwin, p_fkv, p_flogf) = trunk(
        x_prompt, None, None, params, w_buf)
    past = dict(mc=state_mlstm_c, mn=state_mlstm_n, mm=state_mlstm_m, gs=state_gdn_s, gc=state_gdn_conv,
                nsa_kv=cache_nsa_kv, nsa_win=state_nsa_win, fox_kv=cache_fox_kv, fox_logf=cache_fox_logf)
    y_sample, (s_mc, s_mn, s_mm, s_gs, s_gc, s_nkv, s_nwin, s_fkv, s_flogf) = trunk(
        x_sample, past, page_table, params, w_buf)
    return (y_prompt, y_sample,
            p_mc, p_mn, p_mm, p_gs, p_gc, p_nkv, p_nwin, p_fkv, p_flogf,
            s_mc, s_mn, s_mm, s_gs, s_gc, s_nkv, s_nwin, s_fkv, s_flogf)


_drawn_inputs = setup_inputs


def setup_inputs(seed=0):
    import zlib

    import numpy as np

    out = dict(_drawn_inputs(seed))
    spreads = {}
    factors = {'cache_fox_logf': 28.038,
     'mi_norm': 3.015,
     'gd_norm': 2.751,
     'nsa_cmp_pos': 4.319,
     'rel_bias': 2.977}
    for name, (base, spread) in spreads.items():
        noise = np.random.default_rng([zlib.crc32(name.encode()), seed]).standard_normal(out[name].shape)
        drawn = base * np.exp(spread * noise) if base else spread * noise
        out[name] = jnp.asarray(drawn.astype(out[name].dtype))
    for name, factor in factors.items():
        out[name] = (out[name] * factor).astype(out[name].dtype)
    return out
```

```python
from contextlib import ExitStack, contextmanager

import numpy as np
import concourse.bass as bass
from concourse import mybir

F32 = mybir.dt.float32
I32 = mybir.dt.int32
ALU = mybir.AluOpType
ACT = mybir.ActivationFunctionType
AX = mybir.AxisListType.X

P = 128
DM = 1024
KT = DM // P
NPROMPT = 1024
NB, NT = 8, 8
NS = NB * NT
TOK = NPROMPT + NS
CH = 364
TP = 3 * CH
NC = NPROMPT // P
DFF = 4 * DM
EPS = 1e-6
NEG = -1e30
PAST = 256
TK = PAST + NT
NPOOL = 20
WIN = 512
H = 8
HD = 64


class Steps:

    def __init__(self, handle, values):
        self.sem, self.values, self.count, self.first = handle, values, 0, not values
        self.seen = {}

    def mark(self, name, by=1):
        assert name not in self.seen, name
        self.count += by
        self.seen[name] = self.count
        return by

    def at(self, name):
        return 1 if self.first else self.values[name]


class Program:

    def __init__(self, nc, values):
        self.nc, self.values, self.found = nc, values, {}

    @contextmanager
    def stage(self, name, steps=(), sems=()):
        nc = self.nc
        all_ = {}
        for s in steps:
            all_[s] = Steps(nc.alloc_semaphore(name=f"{name}_{s}"), self.values.get((name, s), {}))
        for s in sems:
            all_[s] = nc.alloc_semaphore(name=f"{name}_{s}")
        with nc.Block(no_gpsimd_drain=False) as block:
            yield block, all_
        for s in steps:
            self.found[(name, s)] = all_[s].seen
        nc.clear_and_free_semaphores([v.sem if isinstance(v, Steps) else v for v in all_.values()])
        nc.all_engine_barrier()


class Arena:

    def __init__(self, *buffers):
        self.free = [[b, 0] for b in buffers]

    def __call__(self, shape):
        p, dims = shape[0], shape[1:]
        n = int(np.prod(dims))
        for f in self.free:
            if f[1] + n <= f[0].shape[1]:
                ap = f[0][0:p, f[1]:f[1] + n]
                f[1] += n + n % 2
                if len(dims) > 1:
                    names = " ".join("abc"[:len(dims)])
                    ap = ap.rearrange(f"p ({names}) -> p {names}", **dict(zip("abc", dims[:-1])))
                return ap
        raise ValueError(f"no room for {shape}")


def bank(ps, n):
    return ps[:, 512 * n:512 * (n + 1)]


def stream(pr, name, ps, wslots, iters, tiles, loads=()):
    nc = pr.nc
    nb = len(tiles)
    assert nb % 4 == 0
    pres = [n for n, t in enumerate(tiles) if t.get("pre")]
    M = [t.get("m", P) for t in tiles]

    def over(e):
        class One:
            def __enter__(self):
                return 0

            def __exit__(self, *a):
                return False
        return e.Fori(0, iters) if iters > 1 else One()

    sems = ["w0", "w1", "w2", "w3", "product", "set0_free", "set1_free", "pre_done"]
    with pr.stage(name, sems=sems) as (block, s):
        view = [ps[:, 1536 * k:1536 * (k + 1)].rearrange("p (c n) -> p c n", n=512)[:, :, 0:CH] for k in (0, 1)]
        free = [s["set0_free"], s["set1_free"]]

        @block.sync
        def _(sp):
            with over(sp) as i:
                for n, t in enumerate(tiles):
                    sp.wait_ge(s["product"], i * nb + n + 1)
                    sp.dma_start(wslots[:, n % 4, :, 0:M[n]], t["w"](i).rearrange("(k p) m -> p k m", p=P)) \
                        .then_inc(s[f"w{n % 4}"], 16)

        @block.tensor
        def _(pe):
            pe.sem_inc(s["product"], 4)
            with over(pe) as i:
                for n, t in enumerate(tiles):
                    pe.wait_ge(s[f"w{n % 4}"], i * (4 * nb) + 16 * (n // 4 + 1))
                    pe.wait_ge(free[n % 2], i * (nb // 2) + n // 2 + 1)
                    if t.get("need"):
                        for k in (0, 1):
                            pe.wait_ge(free[k], i * (nb // 2) + (t["need"] + 1 - k) // 2 + 1)
                    for k in range(KT):
                        for c in range(3):
                            mm = pe.matmul(view[n % 2][0:M[n], c, :], wslots[:, n % 4, k, 0:M[n]],
                                           t["x"][:, k, CH * c:CH * (c + 1)], start=(k == 0), stop=(k == KT - 1))
                    mm.then_inc(s["product"], 1)

        @block.scalar
        def _(act):
            act.sem_inc(s["set0_free"], 1)
            act.sem_inc(s["set1_free"], 1)
            with over(act) as i:
                for n, t in enumerate(tiles):
                    if t.get("pre") or t["by"] == "act":
                        act.wait_ge(s["product"], i * nb + n + 5)
                    if t.get("pre"):
                        t["pre"](nc.scalar, i, view[n % 2][0:M[n]]).then_inc(s["pre_done"], 1)
                    if t["by"] == "act":
                        t["epi"](nc.scalar, i, view[n % 2][0:M[n]]).then_inc(free[n % 2], 1)

        @block.vector
        def _(dve):
            with over(dve) as i:
                for n, t in enumerate(tiles):
                    if t["by"] == "dve":
                        dve.wait_ge(s["product"], i * nb + n + 5)
                        if t.get("pre"):
                            dve.wait_ge(s["pre_done"], i * len(pres) + pres.index(n) + 1)
                        t["epi"](nc.vector, i, view[n % 2][0:M[n]]).then_inc(free[n % 2], 1)


def v3(ap):
    return ap.rearrange("p (c n) -> p c n", n=CH)


def rmsnorm(pr, name, xT, hn, tmp, rms, g_dram, ones, ps):
    nc = pr.nc
    with ExitStack() as c:
        gcol = c.enter_context(nc.sbuf_tensor(f"{name}_g", [P, KT], F32))
        with pr.stage(name, steps=["pe", "act", "dve"], sems=["g"]) as (block, s):
            pe_, act_, dve_ = s["pe"], s["act"], s["dve"]
            sums = ps[:, 0:1536].rearrange("p (c n) -> p c n", n=512)[:, :, 0:CH]

            @block.sync
            def _(sp):
                sp.dma_start(gcol[:], g_dram.rearrange("(k p) -> p k", p=P),
                             allow_slow_non_contiguous=True).then_inc(s["g"], 16)

            @block.scalar
            def _(act):
                for k in range(KT):
                    nc.scalar.activation(hn[:, k, :], xT[:, k, :], ACT.Square).then_inc(act_.sem, act_.mark(("sq", k)))
                act.wait_ge(dve_.sem, dve_.at("mean"))
                nc.scalar.activation(rms, rms, ACT.Sqrt).then_inc(act_.sem, act_.mark("root"))

            @block.tensor
            def _(pe):
                for k in range(KT):
                    pe.wait_ge(act_.sem, act_.at(("sq", k)))
                    for j in range(3):
                        mm = pe.matmul(sums[:, j, :], ones[:], hn[:, k, CH * j:CH * (j + 1)],
                                       start=(k == 0), stop=(k == KT - 1))
                mm.then_inc(pe_.sem, pe_.mark("sum"))

            @block.vector
            def _(dve):
                dve.wait_ge(pe_.sem, pe_.at("sum"))
                nc.vector.tensor_scalar(v3(rms), sums, 1.0 / DM, EPS, ALU.mult, ALU.add) \
                    .then_inc(dve_.sem, dve_.mark("mean"))
                dve.wait_ge(act_.sem, act_.at("root"))
                nc.vector.reciprocal(tmp, rms).then_inc(dve_.sem, dve_.mark("rstd"))
                dve.wait_ge(dve_.sem, dve_.at("rstd"))
                dve.wait_ge(s["g"], 16)
                for k in range(KT):
                    nc.vector.scalar_tensor_tensor(out=hn[:, k, :], in0=xT[:, k, :], scalar=gcol[:, k:k + 1],
                                                   in1=tmp, op0=ALU.mult, op1=ALU.mult) \
                        .then_inc(dve_.sem, dve_.mark(("hn", k)))


def token_rows(i):
    return P if i < NC else NS


def load_x(pr, I, xT, ident, ps):
    nc = pr.nc
    with ExitStack() as c:
        xin = c.enter_context(nc.sbuf_tensor("xin", [P, 2, DM], F32))
        with pr.stage("loadx", steps=["pe", "act", "dve"], sems=["x0", "x1"]) as (block, s):
            pe_, act_, dve_ = s["pe"], s["act"], s["dve"]

            @block.sync
            def _(sp):
                for i in range(NC + 1):
                    if i >= 2:
                        sp.wait_ge(pe_.sem, pe_.at(("turned", i - 2)))
                    src = I["x_prompt"][0, P * i:P * (i + 1), :] if i < NC else \
                        I["x_sample"].rearrange("b t d -> (b t) d")
                    sp.dma_start(xin[0:token_rows(i), i % 2, :], src).then_inc(s[f"x{i % 2}"], 16)

            @block.tensor
            def _(pe):
                for i in range(NC + 1):
                    r = token_rows(i)
                    pe.wait_ge(s[f"x{i % 2}"], 16 * (i // 2 + 1))
                    if i >= 2:
                        pe.wait_ge(act_.sem, act_.at(("x", i - 2)))
                        pe.wait_ge(dve_.sem, dve_.at(("x", i - 2)))
                    for k in range(KT):
                        t = pe.transpose(bank(ps, 2 * (i % 2) + k // 4)[:, P * (k % 4):P * (k % 4) + r],
                                         xin[0:r, i % 2, P * k:P * (k + 1)], ident[0:r, 0:r])
                    t.then_inc(pe_.sem, pe_.mark(("turned", i)))

            def half(e, st, b):
                if b:
                    nc.vector.memset(xT[:, :, TOK:TP], 0.0).then_inc(st.sem, st.mark("pad"))
                for i in range(NC + 1):
                    r = token_rows(i)
                    e.wait_ge(pe_.sem, pe_.at(("turned", i)))
                    src = bank(ps, 2 * (i % 2) + b).rearrange("p (k t) -> p k t", k=4)[:, :, 0:r]
                    dst = xT[:, 4 * b:4 * b + 4, P * i:P * i + r]
                    op = nc.vector.tensor_copy(dst, src) if b else nc.scalar.activation(dst, src, ACT.Copy)
                    op.then_inc(st.sem, st.mark(("x", i)))

            @block.scalar
            def _(act):
                half(act, act_, 0)

            @block.vector
            def _(dve):
                half(dve, dve_, 1)


def even_gates(pr, I, O, C, zg, GC, RT, arena, ps):
    nc = pr.nc
    Q = [slice(32 * q, 32 * q + 4) for q in range(4)]
    with ExitStack() as c:
        def sb(n, shape):
            return c.enter_context(nc.sbuf_tensor("eg_" + n, shape, F32))
        bias, al = sb("bias", [P, 1]), sb("al", [4, 1])
        z, l1, colr = zg, arena([P, TP]), arena([P, TP])
        rows = {n: arena([4, TP]) for n in ("li", "lf", "b", "m", "mp", "beta", "g", "gc", "t3", "t4")}
        rows["t1"], rows["t2"] = rows["mp"], rows["m"]
        m0 = sb("m0", [4, NB])
        mout = sb("mout", [4, 1 + NB])
        with pr.stage("evengates", steps=["pe", "act", "dve"], sems=["ld", "st"]) as (block, s):
            pe_, act_, dve_ = s["pe"], s["act"], s["dve"]

            @block.sync
            def _(sp):
                sp.wait_ge(dve_.sem, dve_.at("zero"))
                for q, n in ((0, "mi_b_i"), (1, "mi_b_f"), (3, "gd_dt_bias")):
                    sp.dma_start(bias[Q[q], :], I[n].rearrange("a h -> h a")).then_inc(s["ld"], 16)
                sp.dma_start(al[:], I["gd_a_log"].rearrange("a h -> h a")).then_inc(s["ld"], 16)
                sp.dma_start(m0[:], I["state_mlstm_m"][0].rearrange("b h -> h b"),
                             allow_slow_non_contiguous=True).then_inc(s["ld"], 16)
                sp.wait_ge(dve_.sem, dve_.at("m_out"))
                sp.dma_start(O["p_mlstm_m"].rearrange("a b h -> (b h) a"), mout[:, 0:1]).then_inc(s["st"], 16)
                sp.dma_start(O["s_mlstm_m"][0].rearrange("b h -> h b"), mout[:, 1:1 + NB],
                             allow_slow_non_contiguous=True).then_inc(s["st"], 16)
                sp.wait_ge(s["st"], 32)

            @block.scalar
            def _(act):
                act.wait_ge(dve_.sem, dve_.at("z"))
                nc.scalar.activation(l1[:], z[:], ACT.Abs).then_inc(act_.sem, act_.mark("abs"))
                act.wait_ge(act_.sem, act_.at("abs"))
                nc.scalar.activation(l1[:], l1[:], ACT.Exp, scale=-1.0).then_inc(act_.sem, act_.mark("e"))
                act.wait_ge(act_.sem, act_.at("e"))
                nc.scalar.activation(l1[:], l1[:], ACT.Ln, bias=1.0).then_inc(act_.sem, act_.mark("l1"))
                act.wait_ge(s["ld"], 80)
                nc.scalar.activation(al[:], al[:], ACT.Exp).then_inc(act_.sem, act_.mark("al"))
                nc.scalar.activation(rows["beta"][:], z[Q[2], :], ACT.Sigmoid).then_inc(act_.sem, act_.mark("beta"))
                act.wait_ge(dve_.sem, dve_.at("t3"))
                nc.scalar.activation(RT[Q[1], :], rows["t3"][:], ACT.Exp).then_inc(act_.sem, act_.mark("ainter"))
                nc.scalar.activation(RT[Q[2], :], rows["m"][:], ACT.Exp, scale=-1.0).then_inc(act_.sem, act_.mark("em"))
                act.wait_ge(dve_.sem, dve_.at("gc"))
                nc.scalar.activation(rows["t4"][:], rows["gc"][:], ACT.Exp).then_inc(act_.sem, act_.mark("egc"))

            @block.vector
            def _(dve):
                def step(name, ins):
                    ins.then_inc(dve_.sem, dve_.mark(name))

                def need(name):
                    dve.wait_ge(dve_.sem, dve_.at(name))
                V = nc.vector
                R = rows
                step("zero", V.memset(bias[:], 0.0))
                step("zero2", V.memset(RT[:], 0.0))
                step("zero3", V.memset(colr[:], 0.0))
                dve.wait_ge(s["ld"], 80)
                need("zero")
                step("z", V.tensor_scalar(z[:], zg[:], bias[:, 0:1], None, ALU.add))
                need("z")
                step("li", V.tensor_copy(R["li"][:], z[Q[0], :]))
                step("zf", V.tensor_copy(R["lf"][:], z[Q[1], :]))
                step("zg", V.tensor_copy(R["g"][:], z[Q[3], :]))
                dve.wait_ge(act_.sem, act_.at("l1"))
                step("l1f", V.tensor_copy(R["t1"][:], l1[Q[1], :]))
                step("l1g", V.tensor_copy(R["t2"][:], l1[Q[3], :]))
                need("l1g")
                step("lf", V.scalar_tensor_tensor(out=R["lf"][:], in0=R["lf"][:], scalar=0.0, in1=R["t1"][:],
                                                  op0=ALU.min, op1=ALU.subtract))
                step("sp", V.scalar_tensor_tensor(out=R["g"][:], in0=R["g"][:], scalar=0.0, in1=R["t2"][:],
                                                  op0=ALU.max, op1=ALU.add))
                dve.wait_ge(act_.sem, act_.at("al"))
                need("sp")
                step("g", V.tensor_scalar(R["g"][:], R["g"][:], al[:, 0:1], -1.0, ALU.mult, ALU.mult))
                need("lf")
                step("b", V.tensor_tensor_scan(R["b"][:], C["keep"][0:4, :], R["lf"][:], 0.0, ALU.mult, ALU.add))
                need("g")
                step("gc", V.tensor_tensor_scan(R["gc"][:], C["keep"][0:4, :], R["g"][:], 0.0, ALU.mult, ALU.add))
                step("m_p", V.tensor_tensor_scan(R["m"][:, 0:NPROMPT], R["lf"][:, 0:NPROMPT], R["li"][:, 0:NPROMPT],
                                                 0.0, ALU.add, ALU.max))
                for b in range(NB):
                    w = slice(NPROMPT + NT * b, NPROMPT + NT * (b + 1))
                    step(("m_s", b), V.tensor_tensor_scan(R["m"][:, w], R["lf"][:, w], R["li"][:, w],
                                                          m0[:, b:b + 1], ALU.add, ALU.max))
                step("m_pad", V.memset(R["m"][:, TOK:TP], 0.0))
                step("mp0", V.memset(R["mp"][:], 0.0))
                need("m_pad")
                need("mp0")
                ends = R["m"][:, P - 1:P * (NC - 1):P].rearrange("h (c o) -> h c o", o=1)
                step("mp1", V.tensor_copy(R["mp"][:, P:NPROMPT].rearrange("h (c t) -> h c t", t=P),
                                          ends.broadcast_to([4, NC - 1, P])))
                step("mp2", V.tensor_copy(R["mp"][:, NPROMPT:TOK].rearrange("h (b t) -> h b t", t=NT),
                                          m0[:].rearrange("h (b o) -> h b o", o=1).broadcast_to([4, NB, NT])))
                step("r1", V.tensor_tensor(RT[Q[0], :], R["b"][:], R["m"][:], ALU.subtract))
                step("r1b", V.tensor_tensor(R["t3"][:], R["b"][:], R["m"][:], ALU.subtract))
                need("r1b")
                step("t3", V.tensor_tensor(R["t3"][:], R["t3"][:], R["mp"][:], ALU.add))
                step("rgc", V.tensor_copy(RT[Q[3], :], R["gc"][:]))
                step("mo1", V.tensor_copy(mout[:, 0:1], R["m"][:, NPROMPT - 1:NPROMPT]))
                step("m_out", V.tensor_copy(mout[:, 1:1 + NB], R["m"][:, NPROMPT + NT - 1:TOK:NT]))
                step("c1", V.tensor_tensor(colr[Q[0], :], R["li"][:], R["b"][:], ALU.subtract))
                step("c2", V.tensor_scalar(colr[Q[1], :], R["gc"][:], -1.0, None, ALU.mult))
                dve.wait_ge(act_.sem, act_.at("egc"))
                step("c3", V.tensor_copy(colr[Q[2], :], R["beta"][:]))
                step("c4", V.tensor_tensor(colr[Q[3], :], R["beta"][:], R["t4"][:], ALU.mult))
                for i in range(NC + 1):
                    r = token_rows(i)
                    dve.wait_ge(pe_.sem, pe_.at(("turn", i)))
                    step(("GC", i), V.tensor_copy(GC[0:r, i, :], bank(ps, i % 8)[0:r, 0:P]))

            @block.tensor
            def _(pe):
                pe.wait_ge(dve_.sem, dve_.at("c4"))
                for i in range(NC + 1):
                    r = token_rows(i)
                    if i == 8:
                        pe.wait_ge(dve_.sem, dve_.at(("GC", 0)))
                    pe.transpose(bank(ps, i % 8)[0:r, 0:P], colr[:, P * i:P * i + r], C["ident"][:]) \
                        .then_inc(pe_.sem, pe_.mark(("turn", i)))


def gate_product(pr, I, C, hn, zg, wg, ps):
    nc = pr.nc
    starts = [1536, 1540, 3592, 3596]
    with pr.stage("gatemm", steps=["pe", "dve"], sems=["ld"]) as (block, s):
        pe_, dve_ = s["pe"], s["dve"]
        acc = ps[:, 0:1536].rearrange("p (c n) -> p c n", n=512)[:, :, 0:CH]

        @block.sync
        def _(sp):
            sp.wait_ge(dve_.sem, dve_.at("zero"))
            for q, c0 in enumerate(starts):
                sp.dma_start(wg[:, :, 32 * q:32 * q + 4],
                             I["w_in_even"][0, :, c0:c0 + 4].rearrange("(k p) m -> p k m", p=P),
                             allow_slow_non_contiguous=True).then_inc(s["ld"], 16)

        @block.tensor
        def _(pe):
            pe.wait_ge(s["ld"], 64)
            for k in range(KT):
                for j in range(3):
                    mm = pe.matmul(acc[:, j, :], wg[:, k, :], hn[:, k, CH * j:CH * (j + 1)],
                                   start=(k == 0), stop=(k == KT - 1))
            mm.then_inc(pe_.sem, pe_.mark("z"))

        @block.vector
        def _(dve):
            nc.vector.memset(wg[:], 0.0).then_inc(dve_.sem, dve_.mark("zero"))
            dve.wait_ge(pe_.sem, pe_.at("z"))
            nc.vector.tensor_copy(v3(zg[:]), acc).then_inc(dve_.sem, dve_.mark("zg"))


def conv(pr, I, O, C, Z, arena, ps):
    nc = pr.nc
    T = 12
    with ExitStack() as c:
        def sb(n, shape):
            return arena(shape)
        hist_in, hist, wrow, wcol = sb("hi", [24, T * P]), sb("h", [P, T, 24]), sb("wr", [4, T * P]), sb("wc", [P, T, 4])
        last, lastT = sb("last", [P, T, 27]), sb("lastT", [27, T * P])
        y, xs = sb("y", [P, 2, TP]), sb("xs", [P, 2, NB, 11])
        rr = sb("rr", [P, TP])
        with pr.stage("conv", steps=["pe", "act", "dve"], sems=["ld", "st"]) as (block, s):
            pe_, act_, dve_ = s["pe"], s["act"], s["dve"]
            hp = bank(ps, 0)[:, 0:T * 24].rearrange("p (j n) -> p j n", n=24)
            wp = bank(ps, 1)[:, 0:T * 4].rearrange("p (j n) -> p j n", n=4)
            lp = bank(ps, 2)
            acc = ps[:, 1536:3072].rearrange("p (c n) -> p c n", n=512)[:, :, 0:CH]

            @block.sync
            def _(sp):
                sp.dma_start(hist_in[:], I["state_gdn_conv"][0].rearrange("b j c -> (b j) c")).then_inc(s["ld"], 16)
                sp.dma_start(wrow[:], I["gd_conv_w"][0]).then_inc(s["ld"], 16)
                sp.wait_ge(dve_.sem, dve_.at(("lastT", 2)))
                sp.dma_start(O["p_gdn_conv"][0, 0], lastT[0:3, :]).then_inc(s["st"], 16)
                sp.dma_start(O["s_gdn_conv"][0].rearrange("b j c -> (b j) c"), lastT[3:27, :]).then_inc(s["st"], 16)
                sp.wait_ge(s["st"], 32)

            @block.tensor
            def _(pe):
                pe.wait_ge(s["ld"], 32)
                for j in range(T):
                    pe.transpose(hp[:, j, :], hist_in[:, P * j:P * (j + 1)], C["ident"][0:24, 0:24])
                    t = pe.transpose(wp[:, j, :], wrow[:, P * j:P * (j + 1)], C["ident"][0:4, 0:4])
                t.then_inc(pe_.sem, pe_.mark("hist"))
                pe.wait_ge(dve_.sem, dve_.at("last"))
                for q in range(3):
                    if q:
                        pe.wait_ge(dve_.sem, dve_.at(("lastT", q - 1)))
                    for j in range(4 * q, 4 * q + 4):
                        t = pe.transpose(lp[0:27, P * (j - 4 * q):P * (j - 4 * q + 1)], last[:, j, :], C["ident"][:])
                    t.then_inc(pe_.sem, pe_.mark(("lastT", q)))
                for j in range(8):
                    pe.wait_ge(act_.sem, act_.at(("sq", j)))
                    if j:
                        pe.wait_ge(dve_.sem, dve_.at(("ss", j - 1)))
                    for k in range(3):
                        mm = pe.matmul(acc[:, k, :], C["ones"][:], y[:, j % 2, CH * k:CH * (k + 1)], start=True, stop=True)
                    mm.then_inc(pe_.sem, pe_.mark(("ss", j)))

            @block.vector
            def _(dve):
                V = nc.vector

                def step(name, ins):
                    ins.then_inc(dve_.sem, dve_.mark(name))

                def need(name):
                    dve.wait_ge(dve_.sem, dve_.at(name))
                dve.wait_ge(pe_.sem, pe_.at("hist"))
                step("hist", V.tensor_copy(hist[:], hp))
                step("wcol", V.tensor_copy(wcol[:], wp))
                step("last0", V.tensor_copy(last[:, :, 0:3], Z[:, 8:20, NPROMPT - 3:NPROMPT]))
                for j in range(3):
                    step(("last1", j), V.tensor_copy(last[:, :, 3 + j:27:3], Z[:, 8:20, NPROMPT + 5 + j:TOK:NT]))
                step("last", V.memset(rr[:, 0:1], 0.0))
                for q in range(3):
                    dve.wait_ge(pe_.sem, pe_.at(("lastT", q)))
                    step(("lastT", q), V.tensor_copy(lastT[:, 512 * q:512 * (q + 1)], lp[0:27, :]))
                need("wcol")
                for j in range(T):
                    z, b = Z[:, 8 + j, :], j % 2
                    ys = y[:, b, NPROMPT:TOK].rearrange("p (b t) -> p b t", t=NT)
                    zs = z[:, NPROMPT:TOK].rearrange("p (b t) -> p b t", t=NT)
                    if j >= 2:
                        dve.wait_ge(act_.sem, act_.at(("silu", j - 2)))
                    step(("xs0", j), V.tensor_copy(xs[:, b, :, 0:3], hist[:, j, :].rearrange("p (b t) -> p b t", t=3)))
                    step(("xs1", j), V.tensor_copy(xs[:, b, :, 3:11], zs))
                    step(("y3", j), V.tensor_scalar(y[:, b, :], z, wcol[:, j, 3:4], None, ALU.mult))
                    for d in (1, 2, 3):
                        need(("y3", j) if d == 1 else (f"y{d - 1}s", j))
                        w = wcol[:, j, 3 - d:4 - d]
                        step((f"y{d}p", j), V.scalar_tensor_tensor(
                            out=y[:, b, d:NPROMPT], in0=z[:, 0:NPROMPT - d], scalar=w, in1=y[:, b, d:NPROMPT],
                            op0=ALU.mult, op1=ALU.add))
                        step((f"y{d}s", j), V.scalar_tensor_tensor(
                            out=ys, in0=xs[:, b, :, 3 - d:11 - d], scalar=w, in1=ys, op0=ALU.mult, op1=ALU.add))
                for j in range(8):
                    dve.wait_ge(pe_.sem, pe_.at(("ss", j)))
                    if j:
                        need(("n", j - 1))
                    step(("ss", j), V.tensor_scalar(v3(rr[:]), acc, EPS, float(P) if j < 4 else 1.0, ALU.add, ALU.mult))
                    dve.wait_ge(act_.sem, act_.at(("root", j)))
                    step(("rec", j), V.reciprocal(rr[:], rr[:]))
                    need(("rec", j))
                    step(("n", j), V.tensor_tensor(Z[:, 8 + j, :], Z[:, 8 + j, :], rr[:], ALU.mult))

            @block.scalar
            def _(act):
                for j in range(T):
                    act.wait_ge(dve_.sem, dve_.at(("y3s", j)))
                    nc.scalar.activation(Z[:, 8 + j, :], y[:, j % 2, :], ACT.Silu).then_inc(act_.sem, act_.mark(("silu", j)))
                act.wait_ge(act_.sem, act_.at(("silu", T - 1)))
                for j in range(8):
                    if j >= 2:
                        act.wait_ge(pe_.sem, pe_.at(("ss", j - 2)))
                    nc.scalar.activation(y[:, j % 2, :], Z[:, 8 + j, :], ACT.Square).then_inc(act_.sem, act_.mark(("sq", j)))
                    if j >= 1:
                        act.wait_ge(dve_.sem, dve_.at(("ss", j - 1)))
                        nc.scalar.activation(rr[:], rr[:], ACT.Sqrt).then_inc(act_.sem, act_.mark(("root", j - 1)))
                act.wait_ge(dve_.sem, dve_.at(("ss", 7)))
                nc.scalar.activation(rr[:], rr[:], ACT.Sqrt).then_inc(act_.sem, act_.mark(("root", 7)))


def mlstm(pr, I, O, C, Z, GC, RT, arena, ps):
    nc = pr.nc
    with ExitStack() as c:
        def sb(n, shape):
            return arena(shape)
        Cs = sb("C", [P, 2, 129])
        Cb = sb("Cb", [P, 1 + NB, 2, 129])
        nbc = sb("nbc", [P, 2, P])
        nbs = sb("nbs", [P, NB, 2, P])
        kt, vt = sb("kt", [P, 4, 64]), sb("vt", [P, 4, 129])
        dt, pt, kw, qa = sb("dt", [P, 4, P]), sb("pt", [P, 4, P]), sb("kw", [P, 4, 64]), sb("qa", [P, 4, P])
        qz = sb("qz", [P, 4, P])
        ab, den, eb = sb("ab", [P, 4, P]), sb("den", [P, 4, P]), sb("eb", [P, 4, P])
        kwb = sb("kwb", [NS, 2, 4, 64])

        def b4(n):
            return bank(ps, n).rearrange("p (h t) -> p h t", h=4)
        ST, RB, AB, EB, TR, NUM, DEN, CU = (b4(n) for n in range(8))
        with pr.stage("mlstm", steps=["pe", "act", "dve"], sems=["ld", "st"]) as (block, s):
            pe_, act_, dve_ = s["pe"], s["act"], s["dve"]

            def cols(i):
                return slice(P * i, P * i + token_rows(i))

            def hp(h):
                return slice(64 * (h % 2), 64 * (h % 2) + 64)

            @block.sync
            def _(sp):
                for x in range(2):
                    sl = slice(64 * x, 64 * x + 64)
                    for b in range(NB):
                        sp.dma_start(Cb[sl, 1 + b, :, 0:P], I["state_mlstm_c"][0, b].rearrange("(y x) d v -> x d y v", x=2)[x]) \
                            .then_inc(s["ld"], 16)
                    for y in range(2):
                        sp.dma_start(Cb[sl, 1:, y, P:P + 1], I["state_mlstm_n"][0, :, 2 * y + x, :].rearrange("b (d o) -> d b o", o=1),
                                     allow_slow_non_contiguous=True).then_inc(s["ld"], 16)
                sp.wait_ge(dve_.sem, dve_.at(("C", NC - 1, 3)))
                for x in range(2):
                    sl = slice(64 * x, 64 * x + 64)
                    sp.dma_start(O["p_mlstm_c"][0, 0].rearrange("(y x) d v -> x d y v", x=2)[x], Cs[sl, :, 0:P]).then_inc(s["st"], 16)
                    sp.dma_start(O["p_mlstm_n"][0, 0].rearrange("(y x) (d o) -> x d y o", x=2, o=1)[x], Cs[sl, :, P:P + 1],
                                 allow_slow_non_contiguous=True).then_inc(s["st"], 16)
                sp.wait_ge(dve_.sem, dve_.at(("Cb", NB - 1, 3)))
                for x in range(2):
                    sl = slice(64 * x, 64 * x + 64)
                    for b in range(NB):
                        sp.dma_start(O["s_mlstm_c"][0, b].rearrange("(y x) d v -> x d y v", x=2)[x], Cb[sl, 1 + b, :, 0:P]) \
                            .then_inc(s["st"], 16)
                    for y in range(2):
                        sp.dma_start(O["s_mlstm_n"][0, :, 2 * y + x, :].rearrange("b (d o) -> d b o", o=1), Cb[sl, 1:, y, P:P + 1],
                                     allow_slow_non_contiguous=True).then_inc(s["st"], 16)
                sp.wait_ge(s["st"], 16 * (4 + 20))

            @block.tensor
            def _(pe):
                def need(st, name):
                    pe.wait_ge(st.sem, st.at(name))

                def bcast(q, dst, i, r):
                    for h in range(4):
                        mm = pe.matmul(dst[:, h, 0:r], C["sel"][:, 4 * q + h, :], RT[:, cols(i)], start=True, stop=True)
                    return mm

                for i in range(NC + 1):
                    r = token_rows(i)
                    if i:
                        need(act_, ("kt", i - 1))
                        need(dve_, ("ab", i - 1))
                        need(dve_, ("pt", i - 1))
                        need(act_, ("eb", i - 1))
                        need(dve_, ("D", i - 1))
                        need(act_, ("vt", i - 1))
                        need(dve_, ("C", i - 1, 3))
                    need(dve_, ("qz", i))
                    for h in range(4):
                        if h % 2 == 0:
                            t = pe.transpose(TR.rearrange("p h t -> p (h t)")[0:r, 64 * h:64 * h + P], Z[:, 2 + h // 2, cols(i)], C["ident"][:])
                        pe.matmul(ST[0:r, h, 0:r], Z[:, 2 + h // 2, cols(i)], qz[:, h, 0:r], start=True, stop=True)
                    bcast(0, RB, i, r).then_inc(pe_.sem, pe_.mark(("RB", i)))
                    bcast(1, AB, i, r).then_inc(pe_.sem, pe_.mark(("AB", i)))
                    bcast(2, EB, i, r).then_inc(pe_.sem, pe_.mark(("EB", i)))
                    for h in range(4):
                        t = pe.transpose(CU[0:r, h, :], Z[:, 4 + h, cols(i)], C["ident"][:])
                    t.then_inc(pe_.sem, pe_.mark(("VT", i)))
                    need(dve_, ("pt", i))
                    need(act_, ("vt", i))
                    need(dve_, ("qa", i))
                    if i:
                        need(dve_, ("h", i - 1))
                        need(dve_, ("den", i - 1))
                    last = i == NC
                    need(dve_, ("nbs",) if last else ("nbc", i))
                    for h in range(4):
                        pe.matmul(NUM[:, h, 0:r], vt[0:r, h, 0:P], pt[0:r, h, 0:r], start=True, stop=(i == 0))
                        if not last and i:
                            pe.matmul(NUM[:, h, 0:r], Cs[:, h // 2, 0:P], qa[:, h, 0:r], start=False, stop=True)
                        for b in range(NB if last else 0):
                            w = slice(NT * b, NT * (b + 1))
                            pe.matmul(NUM[:, h, w], Cb[:, 1 + b, h // 2, 0:P], qa[:, h, w], start=False, stop=(b == NB - 1))
                    for h in range(4):
                        mm = pe.matmul(DEN[:, h, 0:r], C["ones"][0:r, :], pt[0:r, h, 0:r], start=True, stop=(i == 0))
                        if not last and i:
                            mm = pe.matmul(DEN[:, h, 0:r], nbc[:, h // 2, :], qa[:, h, 0:r], start=False, stop=True)
                        for b in range(NB if last else 0):
                            w = slice(NT * b, NT * (b + 1))
                            mm = pe.matmul(DEN[:, h, w], nbs[:, b, h // 2, :], qa[:, h, w], start=False, stop=(b == NB - 1))
                    mm.then_inc(pe_.sem, pe_.mark(("ND", i)))
                    if not last:
                        need(dve_, ("kw", i))
                        for h in range(4):
                            bk = CU if h < 2 else TR
                            mm = pe.matmul(bk.rearrange("p h t -> p (h t)")[hp(h), 0:129], kw[0:r, h, :], vt[0:r, h, :], start=True, stop=True)
                        mm.then_inc(pe_.sem, pe_.mark(("CU", i)))
                    for b in range(NB if last else 0):
                        need(dve_, ("kwb", b))
                        if b:
                            need(dve_, ("Cb", b - 1, 3))
                        for h in range(4):
                            bk = CU if h < 2 else TR
                            mm = pe.matmul(bk.rearrange("p h t -> p (h t)")[hp(h), 0:129], kwb[:, b % 2, h, :], vt[0:NS, h, :], start=True, stop=True)
                        mm.then_inc(pe_.sem, pe_.mark(("CUb", b)))

            @block.scalar
            def _(act):
                def need(st, name):
                    act.wait_ge(st.sem, st.at(name))
                for i in range(NC + 1):
                    r = token_rows(i)
                    need(pe_, ("RB", i))
                    if i:
                        need(pe_, ("CU", i - 1))
                    nc.scalar.activation(kt[0:r], TR.rearrange("p h t -> p (h t)")[0:r, 0:256].rearrange("p (h d) -> p h d", h=4), ACT.Copy) \
                        .then_inc(act_.sem, act_.mark(("kt", i)))
                    need(dve_, ("D", i))
                    for h in range(4):
                        ins = nc.scalar.activation(dt[0:r, h, 0:r], dt[0:r, h, 0:r], ACT.Exp, bias=GC[0:r, i, h:h + 1])
                    ins.then_inc(act_.sem, act_.mark(("dt", i)))
                    need(pe_, ("VT", i))
                    if i == 0:
                        need(dve_, ("ones_col"))
                    nc.scalar.activation(vt[0:r, :, 0:P], CU[0:r], ACT.Copy).then_inc(act_.sem, act_.mark(("vt", i)))
                    need(pe_, ("EB", i))
                    nc.scalar.activation(eb[:, :, 0:r], EB[:, :, 0:r], ACT.Copy).then_inc(act_.sem, act_.mark(("eb", i)))
                    need(pe_, ("ND", i))
                    nc.scalar.activation(den[:, :, 0:r], DEN[:, :, 0:r], ACT.Abs).then_inc(act_.sem, act_.mark(("absden", i)))

            @block.vector
            def _(dve):
                V = nc.vector

                def step(name, ins):
                    ins.then_inc(dve_.sem, dve_.mark(name))

                def need(st, name):
                    dve.wait_ge(st.sem, st.at(name))
                step("ones_col", V.memset(vt[:, :, P:P + 1], 1.0))
                step("qz_zero", V.memset(qz[:], 0.0))
                step("qa_zero", V.memset(qa[:], 0.0))
                need(dve_, "qa_zero")
                for i in range(NC + 1):
                    r = token_rows(i)
                    last = i == NC
                    if i:
                        need(pe_, ("AB", i - 1))
                    for x in range(2):
                        sl = slice(64 * x, 64 * x + 64)
                        step(("qz0", i) if x == 0 else ("qz", i), V.tensor_copy(qz[sl, x:4:2, 0:r], Z[sl, 0:2, cols(i)]))
                    mask = (C["maskS"] if last else C["maskP"])
                    need(pe_, ("RB", i))
                    if i:
                        need(pe_, ("ND", i - 1))
                        if not last or True:
                            need(dve_, ("kw", i - 1))
                    step(("D", i), V.tensor_tensor(dt[0:r, :, 0:r], RB[0:r, :, 0:r],
                                                   mask[0:r, 0:r].rearrange("p (o t) -> p o t", o=1).broadcast_to([r, 4, r]), ALU.add))
                    need(pe_, ("AB", i))
                    step(("ab", i), V.tensor_copy(ab[:, :, 0:r], AB[:, :, 0:r]))
                    need(dve_, ("ab", i))
                    if last:
                        dve.wait_ge(s["ld"], 16 * 20)
                        step(("nbs",), V.tensor_copy(nbs[:].rearrange("p b y v -> p (b y) v"),
                                                    Cb[:, 1:, :, P:P + 1].rearrange("p b y o -> p (b y) o").broadcast_to([P, 2 * NB, P])))
                    elif i:
                        need(dve_, ("C", i - 1, 3))
                        step(("nbc", i), V.tensor_copy(nbc[:], Cs[:, :, P:P + 1].broadcast_to([P, 2, P])))
                    else:
                        step(("nbc", i), V.memset(nbc[:], 0.0))
                    for x in range(2):
                        sl = slice(64 * x, 64 * x + 64)
                        ins = V.tensor_tensor(qa[sl, x:4:2, 0:r], Z[sl, 0:2, cols(i)], ab[sl, x:4:2, 0:r], ALU.mult)
                        step(("qa0", i) if x == 0 else ("qa", i), ins)
                    need(act_, ("dt", i))
                    step(("pt", i), V.scalar_tensor_tensor(out=pt[0:r, :, 0:r], in0=ST[0:r, :, 0:r], scalar=0.125,
                                                           in1=dt[0:r, :, 0:r], op0=ALU.mult, op1=ALU.mult))
                    if not last:
                        need(act_, ("kt", i))
                        for h in range(4):
                            ins = V.tensor_scalar(kw[0:r, h, :], kt[0:r, h, :], dt[0:r, h, P - 1:P], 0.125, ALU.mult, ALU.mult)
                        step(("kw", i), ins)
                    need(act_, ("absden", i))
                    need(act_, ("eb", i))
                    step(("den", i), V.tensor_tensor(den[:, :, 0:r], den[:, :, 0:r], eb[:, :, 0:r], ALU.max))
                    need(dve_, ("den", i))
                    step(("rden", i), V.reciprocal(den[:, :, 0:r], den[:, :, 0:r]))
                    need(dve_, ("rden", i))
                    step(("h", i), V.tensor_tensor(Z[:, 4:8, cols(i)], NUM[:, :, 0:r], den[:, :, 0:r], ALU.mult))
                    if not last:
                        need(pe_, ("CU", i))
                    for h in range(4 if not last else 0):
                        bk = (CU if h < 2 else TR).rearrange("p h t -> p (h t)")
                        if i == 0:
                            ins = V.tensor_copy(Cs[hp(h), h // 2, :], bk[hp(h), 0:129])
                        else:
                            ins = V.scalar_tensor_tensor(out=Cs[hp(h), h // 2, :], in0=Cs[hp(h), h // 2, :],
                                                         scalar=ab[hp(h), h, P - 1:P], in1=bk[hp(h), 0:129], op0=ALU.mult, op1=ALU.add)
                        step(("C", i, h), ins)
                    for b in range(NB if last else 0):
                        e = NT * b + NT - 1
                        if b >= 2:
                            need(pe_, ("CUb", b - 2))
                        if b == 0:
                            need(act_, ("kt", i))
                        for h in range(4):
                            ins = V.tensor_scalar(kwb[:, b % 2, h, :], kt[0:r, h, :], dt[0:r, h, e:e + 1], 0.125, ALU.mult, ALU.mult)
                        step(("kwb", b), ins)
                        need(pe_, ("CUb", b))
                        for h in range(4):
                            bk = (CU if h < 2 else TR).rearrange("p h t -> p (h t)")
                            step(("Cb", b, h), V.scalar_tensor_tensor(
                                out=Cb[hp(h), 1 + b, h // 2, :], in0=Cb[hp(h), 1 + b, h // 2, :],
                                scalar=ab[hp(h), h, e:e + 1], in1=bk[hp(h), 0:129], op0=ALU.mult, op1=ALU.add))


def deltanet(pr, I, O, C, Z, GC, RT, arena, ps):
    nc = pr.nc
    with ExitStack() as c:
        def sb(n, shape):
            return arena(shape)
        S = sb("S", [P, 4, P])
        Sb = sb("Sb", [P, NB * 4, P])
        names = ("dt", "mt", "at", "mm", "x", "xt", "t1", "bv", "kb", "kd", "nwt", "vn", "qd", "eg", "kk")
        T = {n: sb(n, [P, 4, P]) for n in names}
        kdb = sb("kdb", [NS, 2, 4, P])

        def b4(n):
            return bank(ps, n).rearrange("p (h t) -> p h t", h=4)
        KKT, QKT, GB, TK, TV, A1, A2, A3 = (b4(n) for n in range(8))
        with pr.stage("delta", steps=["pe", "act", "dve"], sems=["ld", "st"]) as (block, s):
            pe_, act_, dve_ = s["pe"], s["act"], s["dve"]

            def cols(i):
                return slice(P * i, P * i + token_rows(i))

            def levels(i):
                return 7 if i < NC else 3

            @block.sync
            def _(sp):
                sp.dma_start(Sb[:], I["state_gdn_s"][0].rearrange("b h k v -> k (b h) v")).then_inc(s["ld"], 16)
                sp.wait_ge(dve_.sem, dve_.at(("S", NC - 1)))
                sp.dma_start(O["p_gdn_s"][0, 0].rearrange("h k v -> k h v"), S[:]).then_inc(s["st"], 16)
                sp.wait_ge(dve_.sem, dve_.at(("Sb", NB - 1)))
                sp.dma_start(O["s_gdn_s"][0].rearrange("b h k v -> k (b h) v"), Sb[:]).then_inc(s["st"], 16)
                sp.wait_ge(s["st"], 32)

            @block.tensor
            def _(pe):
                def need(st, name):
                    pe.wait_ge(st.sem, st.at(name))

                for i in range(NC + 1):
                    r = token_rows(i)
                    last = i == NC
                    cc = cols(i)
                    if i:
                        need(dve_, ("O", i - 1))
                        need(dve_, ("S", i - 1))
                    for h in range(4):
                        pe.matmul(KKT[0:r, h, 0:r], Z[:, 12 + h, cc], Z[:, 12 + h, cc], start=True, stop=True)
                        pe.matmul(QKT[0:r, h, 0:r], Z[:, 12 + h, cc], Z[:, 8 + h, cc], start=True, stop=True)
                        pe.matmul(GB[:, h, 0:r], C["sel"][:, 12 + h, :], RT[:, cc], start=True, stop=True)
                        pe.transpose(TK[0:r, h, :], Z[:, 12 + h, cc], C["ident"][:])
                        mm = pe.transpose(TV[0:r, h, :], Z[:, 16 + h, cc], C["ident"][:])
                    mm.then_inc(pe_.sem, pe_.mark(("in", i)))
                    for l in range(levels(i)):
                        need(dve_, ("mm", i, l))
                        for h in range(4):
                            mm = pe.matmul(A1[0:r, h, 0:r], T["mm"][0:r, h, 0:r], T["x"][0:r, h, 0:r], start=True, stop=True)
                        mm.then_inc(pe_.sem, pe_.mark(("t1", i, l)))
                        need(dve_, ("t1", i, l))
                        for h in range(4):
                            mm = pe.matmul(A3[0:r, h, 0:r], T["t1"][0:r, h, 0:r], T["xt"][0:r, h, 0:r], start=True, stop=True)
                        mm.then_inc(pe_.sem, pe_.mark(("xt", i, l)))
                        if l < levels(i) - 1:
                            for h in range(4):
                                mm = pe.matmul(A2[0:r, h, 0:r], T["xt"][0:r, h, 0:r], T["t1"][0:r, h, 0:r], start=True, stop=True)
                            mm.then_inc(pe_.sem, pe_.mark(("x", i, l)))
                    need(dve_, ("xt", i, levels(i) - 1))
                    need(act_, ("kb", i))
                    for h in range(4):
                        mm = pe.matmul(A1[:, h, 0:r], T["kb"][0:r, h, :], T["xt"][0:r, h, 0:r], start=True, stop=True)
                    mm.then_inc(pe_.sem, pe_.mark(("wt", i)))
                    need(act_, ("nwt", i))
                    need(act_, ("bv", i))
                    if last:
                        pe.wait_ge(s["ld"], 16)
                        for h in range(4):
                            mm = pe.matmul(A2[:, h, 0:r], T["bv"][0:r, h, :], T["xt"][0:r, h, 0:r], start=True, stop=False)
                            for b in range(NB):
                                w = slice(NT * b, NT * (b + 1))
                                mm = pe.matmul(A2[:, h, w], Sb[:, 4 * b + h, :], T["nwt"][:, h, w], start=False, stop=(b == NB - 1))
                        mm.then_inc(pe_.sem, pe_.mark(("vnT", i)))
                        need(act_, ("vnT", i))
                        for h in range(4):
                            mm = pe.transpose(A1[0:r, h, :], T["mm"][:, h, 0:r], C["ident"][:])
                        mm.then_inc(pe_.sem, pe_.mark(("vn", i)))
                    else:
                        for h in range(4):
                            mm = pe.matmul(A2[0:r, h, :], T["xt"][0:r, h, 0:r], T["bv"][0:r, h, :], start=True, stop=(i == 0))
                            if i:
                                mm = pe.matmul(A2[0:r, h, :], T["nwt"][:, h, 0:r], S[:, h, :], start=False, stop=True)
                        mm.then_inc(pe_.sem, pe_.mark(("vn", i)))
                    need(act_, ("vn", i))
                    need(dve_, ("qd", i))
                    need(dve_, ("at", i))
                    for h in range(4):
                        mm = pe.matmul(A3[:, h, 0:r], T["vn"][0:r, h, :], T["at"][0:r, h, 0:r], start=True, stop=(i == 0))
                        if i and not last:
                            mm = pe.matmul(A3[:, h, 0:r], S[:, h, :], T["qd"][:, h, 0:r], start=False, stop=True)
                        for b in range(NB if last else 0):
                            w = slice(NT * b, NT * (b + 1))
                            mm = pe.matmul(A3[:, h, w], Sb[:, 4 * b + h, :], T["qd"][:, h, w], start=False, stop=(b == NB - 1))
                    mm.then_inc(pe_.sem, pe_.mark(("O", i)))
                    if not last:
                        need(dve_, ("kd", i))
                        for h in range(4):
                            mm = pe.matmul(A1[:, h, :], T["kd"][0:r, h, :], T["vn"][0:r, h, :], start=True, stop=True)
                        mm.then_inc(pe_.sem, pe_.mark(("SU", i)))
                    for b in range(NB if last else 0):
                        need(dve_, ("kdb", b))
                        if b:
                            need(dve_, ("Sb", b - 1))
                        for h in range(4):
                            mm = pe.matmul(A2[:, h, :], kdb[:, b % 2, h, :], T["vn"][0:r, h, :], start=True, stop=True)
                        mm.then_inc(pe_.sem, pe_.mark(("SUb", b)))

            @block.scalar
            def _(act):
                A = nc.scalar

                def need(st, name):
                    act.wait_ge(st.sem, st.at(name))

                def step(name, ins):
                    ins.then_inc(act_.sem, act_.mark(name))
                for i in range(NC + 1):
                    r = token_rows(i)
                    need(dve_, ("D", i))
                    for h in range(4):
                        ins = A.activation(T["dt"][0:r, h, 0:r], T["dt"][0:r, h, 0:r], ACT.Exp, bias=GC[0:r, i, 32 + h:33 + h])
                    step(("dt", i), ins)
                    step(("eg", i), A.activation(T["eg"][:, :, 0:r], GB[:, :, 0:r], ACT.Exp))
                    step(("kk", i), A.activation(T["kk"][0:r], TK[0:r], ACT.Copy))
                    for h in range(4):
                        ins = A.activation(T["bv"][0:r, h, :], TV[0:r, h, :], ACT.Copy, scale=GC[0:r, i, 64 + h:65 + h])
                    step(("bv", i), ins)
                    for h in range(4):
                        ins = A.activation(T["kb"][0:r, h, :], TK[0:r, h, :], ACT.Copy, scale=GC[0:r, i, 96 + h:97 + h])
                    step(("kb", i), ins)
                    need(pe_, ("wt", i))
                    step(("nwt", i), A.activation(T["nwt"][:, :, 0:r], A1[:, :, 0:r], ACT.Copy, scale=-1.0))
                    if i == NC:
                        need(pe_, ("vnT", i))
                        step(("vnT", i), A.activation(T["mm"][:, :, 0:r], A2[:, :, 0:r], ACT.Copy))
                        need(pe_, ("vn", i))
                        step(("vn", i), A.activation(T["vn"][0:r], A1[0:r], ACT.Copy))
                    else:
                        need(pe_, ("vn", i))
                        step(("vn", i), A.activation(T["vn"][0:r], A2[0:r], ACT.Copy))

            @block.vector
            def _(dve):
                V = nc.vector

                def step(name, ins):
                    ins.then_inc(dve_.sem, dve_.mark(name))

                def need(st, name):
                    dve.wait_ge(st.sem, st.at(name))

                def over_heads(m, r):
                    return m.rearrange("p (o t) -> p o t", o=1).broadcast_to([r, 4, r])
                for i in range(NC + 1):
                    r = token_rows(i)
                    last = i == NC
                    need(pe_, ("in", i))
                    if i:
                        need(pe_, ("SU", i - 1))
                    mask = C["maskS"] if last else C["maskP"]
                    step(("D", i), V.tensor_tensor(T["dt"][0:r, :, 0:r], GB[0:r, :, 0:r], over_heads(mask[0:r, 0:r], r), ALU.add))
                    idn = over_heads(C["ident"][0:r, 0:r], r)
                    step(("x0", i), V.tensor_copy(T["x"][0:r, :, 0:r], idn))
                    step(("xt0", i), V.tensor_copy(T["xt"][0:r, :, 0:r], idn))
                    need(act_, ("dt", i))
                    step(("mt", i), V.tensor_tensor(T["mt"][0:r, :, 0:r], KKT[0:r, :, 0:r], T["dt"][0:r, :, 0:r], ALU.mult))
                    step(("at", i), V.tensor_tensor(T["at"][0:r, :, 0:r], QKT[0:r, :, 0:r], T["dt"][0:r, :, 0:r], ALU.mult))
                    need(dve_, ("mt", i))
                    for l in range(levels(i)):
                        if l:
                            need(pe_, ("t1", i, l - 1))
                        step(("mm", i, l), V.tensor_tensor(T["mm"][0:r, :, 0:r], T["mt"][0:r, :, 0:r],
                                                           over_heads(C["level"][0:r, l, 0:r], r), ALU.mult))
                        need(pe_, ("t1", i, l))
                        beta = GC[0:r, i, 64:68].rearrange("p (h o) -> p h o", o=1).broadcast_to([r, 4, r])
                        step(("t1", i, l), V.tensor_tensor(T["t1"][0:r, :, 0:r], A1[0:r, :, 0:r], beta, ALU.mult))
                        if l == 0:
                            need(act_, ("eg", i))
                            step(("qd", i), V.tensor_tensor(T["qd"][:, :, 0:r], Z[:, 8:12, cols(i)], T["eg"][:, :, 0:r], ALU.mult))
                            if not last:
                                need(act_, ("kk", i))
                                step(("kd", i), V.tensor_tensor(T["kd"][0:r], T["kk"][0:r],
                                                               T["dt"][0:r, :, P - 1:P].broadcast_to([r, 4, P]), ALU.mult))
                        need(pe_, ("xt", i, l))
                        if l < levels(i) - 1:
                            need(pe_, ("x", i, l))
                            step(("x", i, l), V.tensor_tensor(T["x"][0:r, :, 0:r], T["x"][0:r, :, 0:r], A2[0:r, :, 0:r], ALU.subtract))
                        step(("xt", i, l), V.tensor_tensor(T["xt"][0:r, :, 0:r], T["xt"][0:r, :, 0:r], A3[0:r, :, 0:r], ALU.subtract))
                        need(dve_, ("xt", i, l))
                    need(pe_, ("O", i))
                    step(("O", i), V.tensor_copy(Z[:, 16:20, cols(i)], A3[:, :, 0:r]))
                    if not last:
                        need(pe_, ("SU", i))
                        if i == 0:
                            step(("S", i), V.tensor_copy(S[:], A1))
                        else:
                            for h in range(4):
                                ins = V.scalar_tensor_tensor(out=S[:, h, :], in0=S[:, h, :], scalar=T["eg"][:, h, P - 1:P],
                                                             in1=A1[:, h, :], op0=ALU.mult, op1=ALU.add)
                            step(("S", i), ins)
                    for b in range(NB if last else 0):
                        e = NT * b + NT - 1
                        if b >= 2:
                            need(pe_, ("SUb", b - 2))
                        step(("kdb", b), V.tensor_tensor(kdb[:, b % 2], T["kk"][0:r],
                                                         T["dt"][0:r, :, e:e + 1].broadcast_to([r, 4, P]), ALU.mult))
                        need(pe_, ("SUb", b))
                        for h in range(4):
                            ins = V.scalar_tensor_tensor(out=Sb[:, 4 * b + h, :], in0=Sb[:, 4 * b + h, :], scalar=T["eg"][:, h, e:e + 1],
                                                         in1=A2[:, h, :], op0=ALU.mult, op1=ALU.add)
                        step(("Sb", b), ins)


def head_norm(pr, I, C, Z, arena, ps):
    nc = pr.nc
    tiles = [4, 5, 6, 7, 16, 17, 18, 19]
    with ExitStack() as c:
        def sb(n, shape):
            return arena(shape)
        gam, sq, rr = sb("gam", [P, 5]), sb("sq", [P, 2, TP]), sb("rr", [P, TP])
        with pr.stage("headnorm", steps=["pe", "act", "dve"], sems=["ld"]) as (block, s):
            pe_, act_, dve_ = s["pe"], s["act"], s["dve"]
            acc = ps[:, 0:1536].rearrange("p (c n) -> p c n", n=512)[:, :, 0:CH]

            @block.sync
            def _(sp):
                sp.dma_start(gam[:, 0:4], I["mi_norm"][0].rearrange("(h v) -> v h", v=P), allow_slow_non_contiguous=True).then_inc(s["ld"], 16)
                sp.dma_start(gam[:, 4:5], I["gd_norm"].rearrange("a v -> v a")).then_inc(s["ld"], 16)

            @block.tensor
            def _(pe):
                for j in range(8):
                    pe.wait_ge(act_.sem, act_.at(("sq", j)))
                    if j:
                        pe.wait_ge(dve_.sem, dve_.at(("ss", j - 1)))
                    for k in range(3):
                        mm = pe.matmul(acc[:, k, :], C["ones"][:], sq[:, j % 2, CH * k:CH * (k + 1)], start=True, stop=True)
                    mm.then_inc(pe_.sem, pe_.mark(("ss", j)))

            @block.scalar
            def _(act):
                for j in range(8):
                    if j >= 2:
                        act.wait_ge(pe_.sem, pe_.at(("ss", j - 2)))
                    nc.scalar.activation(sq[:, j % 2, :], Z[:, tiles[j], :], ACT.Square).then_inc(act_.sem, act_.mark(("sq", j)))
                    act.wait_ge(dve_.sem, dve_.at(("ss", j)))
                    nc.scalar.activation(rr[:], rr[:], ACT.Sqrt).then_inc(act_.sem, act_.mark(("root", j)))

            @block.vector
            def _(dve):
                dve.wait_ge(s["ld"], 32)
                for j in range(8):
                    g = gam[:, min(j, 4):min(j, 4) + 1]
                    dve.wait_ge(pe_.sem, pe_.at(("ss", j)))
                    if j:
                        dve.wait_ge(dve_.sem, dve_.at(("n", j - 1)))
                    nc.vector.tensor_scalar(v3(rr[:]), acc, 1.0 / P, EPS, ALU.mult, ALU.add).then_inc(dve_.sem, dve_.mark(("ss", j)))
                    dve.wait_ge(act_.sem, act_.at(("root", j)))
                    nc.vector.reciprocal(rr[:], rr[:]).then_inc(dve_.sem, dve_.mark(("rec", j)))
                    dve.wait_ge(dve_.sem, dve_.at(("rec", j)))
                    nc.vector.scalar_tensor_tensor(out=Z[:, tiles[j], :], in0=Z[:, tiles[j], :], scalar=g, in1=rr[:],
                                                   op0=ALU.mult, op1=ALU.mult).then_inc(dve_.sem, dve_.mark(("n", j)))


def copy_to(dst_of):
    def epi(e, i, acc):
        dst = v3(dst_of(i))
        return e.tensor_copy(dst, acc) if e.__class__.__name__.find("Vector") >= 0 else e.activation(dst, acc, ACT.Copy)
    return epi


def mlp(pr, I, layer, xT, hn, u, rtmp, wslots, ps):
    nc = pr.nc
    wu, wd = I["w_up"][layer], I["w_down"][layer]
    tiles = []
    for n in range(8):
        def pre(e, i, acc, n=n):
            return e.activation(v3(rtmp[:, n % 2, :]), acc, ACT.Relu)

        def epi(e, i, acc, n=n):
            return nc.vector.tensor_tensor(v3(u[:, n, :]), v3(rtmp[:, n % 2, :]), v3(rtmp[:, n % 2, :]), ALU.mult)
        tiles.append(dict(w=lambda i, n=n: wu[:, bass.ds(i * DM + P * n, P)], x=hn, pre=pre, epi=epi, by="dve"))
    for n in range(8):
        def epi(e, i, acc, n=n):
            return nc.vector.tensor_tensor(v3(xT[:, n, :]), v3(xT[:, n, :]), acc, ALU.add)
        tiles.append(dict(w=lambda i, n=n: wd[bass.ds(i * DM, DM), P * n:P * (n + 1)], x=u, epi=epi, by="dve",
                          need=8 if n == 0 else None))
    stream(pr, f"mlp{layer}", ps, wslots, DFF // DM, tiles)


def residual_product(pr, name, w, mix, xT, wslots, ps):
    nc = pr.nc
    tiles = []
    for n in range(8):
        def epi(e, i, acc, n=n):
            return nc.vector.tensor_tensor(v3(xT[:, n, :]), v3(xT[:, n, :]), acc, ALU.add)
        tiles.append(dict(w=lambda i, n=n: w[:, P * n:P * (n + 1)], x=mix, epi=epi, by="dve"))
    stream(pr, name, ps, wslots, 1, tiles)


class Tiles:

    def __init__(self, z, which):
        self.z, self.which = z, which

    def __getitem__(self, key):
        p, k, t = key
        return self.z[p, self.which[k], t]


def move(pr, name, dst, src):
    with pr.stage(name, sems=["moved"]) as (block, s):
        @block.sync
        def _(sp):
            sp.dma_start(dst, src).then_inc(s["moved"], 16)
            sp.wait_ge(s["moved"], 16)


def layer0(pr, I, O, C, xT, hn, wslots, ps, dbg=None):
    nc = pr.nc
    with ExitStack() as c:
        Z = c.enter_context(nc.sbuf_tensor("Z", [P, 20, TP], F32))
        with ExitStack() as c2:
            zg = c.enter_context(nc.sbuf_tensor("zg", [P, TP], F32))
            spare = c.enter_context(nc.sbuf_tensor("spare", [P, TP], F32))
            GC = c.enter_context(nc.sbuf_tensor("GC", [P, NC + 1, P], F32))
            RT = c.enter_context(nc.sbuf_tensor("RT", [P, TP], F32))
            rmsnorm(pr, "norm0", xT, hn, zg[:], spare[:], I["norm_mix"][0], C["ones"], ps)
            saved = nc.dram_tensor("x_saved", [P, KT * TP], F32).ap()
            move(pr, "save_x", saved, xT[:].rearrange("p k t -> p (k t)"))

            def room():
                return Arena(xT[:].rearrange("p k t -> p (k t)"), wslots[:].rearrange("p a k m -> p (a k m)"), spare[:])
            w = I["w_in_even"][0]
            for name, c0, t0, panels in (("in0a", 0, 0, 2), ("in0b", 1544, 8, 3)):
                tiles = []
                for n in range(4):
                    def epi(e, i, acc, n=n, t0=t0):
                        dst = Z[:, bass.ds(4 * i + (t0 + n), 1), :].rearrange("p o (c n) -> p (o c) n", n=CH)
                        return nc.vector.tensor_copy(dst, acc) if n % 2 else nc.scalar.activation(dst, acc, ACT.Copy)
                    tiles.append(dict(w=lambda i, n=n, c0=c0: w[:, bass.ds(i * 512 + (c0 + P * n), P)], x=hn, epi=epi,
                                      by="dve" if n % 2 else "act"))
                stream(pr, name, ps, wslots, panels, tiles)
            gate_product(pr, I, C, hn, zg, wslots[:, 0], ps)
            even_gates(pr, I, O, C, zg, GC, RT, room(), ps)
        if dbg is not None and dbg(1, Z, GC, RT): return
        conv(pr, I, O, C, Z, room(), ps)
        if dbg is not None and dbg(2, Z, GC, RT): return
        mlstm(pr, I, O, C, Z, GC, RT, room(), ps)
        if dbg is not None and dbg(3, Z, GC, RT): return
        deltanet(pr, I, O, C, Z, GC, RT, room(), ps)
        head_norm(pr, I, C, Z, room(), ps)
        with ExitStack() as c2:
            gt = [zg[:], spare[:]]
            which = [4, 5, 6, 7, 16, 17, 18, 19]
            tiles = []
            for n in range(8):
                def pre(e, i, acc, n=n):
                    return e.activation(v3(gt[n % 2]), acc, ACT.Sigmoid if n < 4 else ACT.Silu)

                def epi(e, i, acc, n=n):
                    z = Z[:, which[n], :]
                    return nc.vector.tensor_tensor(z, z, gt[n % 2], ALU.mult)
                c0 = (1024 if n < 4 else 3080 - 512) + P * n
                tiles.append(dict(w=lambda i, c0=c0: w[:, c0:c0 + P], x=hn, pre=pre, epi=epi, by="dve"))
            stream(pr, "outgates", ps, wslots, 1, tiles)
        if dbg is not None and dbg(4, Z, GC, RT): return
        move(pr, "load_x_saved", xT[:].rearrange("p k t -> p (k t)"), saved)
        residual_product(pr, "wout0", I["w_out_even"][0], Tiles(Z, which), xT, wslots, ps)


KV0, WIN0, FQ0, FK0, FF0 = 512, 1024, 1304, 1816, 2840


def token_major(pr, I, O, W, hn, wslots, wide, stage_buf, gates, ps):
    nc = pr.nc
    w = I["w_in_odd"][0]
    panels = [(KV0, 512), (WIN0, 280), (FK0, 512), (FK0 + 512, 512)]
    flat = wslots[:].rearrange("p a k m -> p (a k m)").rearrange("p (k m) -> p k m", k=KT)
    wb = [flat, wide[:]]
    units = [(n, i) for n in range(4) for i in range(NC + 1)]
    NSL = 4
    with pr.stage("tokmajor", steps=["pe", "act", "dve"], sems=["w0", "w1", "gs", "hist"] + [f"out{k}" for k in range(NSL)]) as (block, s):
        pe_, act_, dve_ = s["pe"], s["act"], s["dve"]
        eng = lambda u: act_ if u % 2 == 0 else dve_
        stores = [0] * NSL
        sent = {}
        for u, (n, i) in enumerate(units):
            stores[u % NSL] += 2 if n == 1 and i in (6, 7, 8) else 1
            sent[u] = stores[u % NSL]

        @block.sync
        def _(sp):
            sp.dma_start(O["s_nsa_win"][0, :, 0:PAST - NT].rearrange("b j a g d -> b j (a g d)"),
                         I["state_nsa_win"][0, :, NT:PAST].rearrange("b j a g d -> b j (a g d)")).then_inc(s["hist"], 16)
            for n in range(2):
                c0, m = panels[n]
                sp.dma_start(wb[n % 2][:, :, 0:m], w[:, c0:c0 + m].rearrange("(k p) m -> p k m", p=P)).then_inc(s[f"w{n % 2}"], 16)
            for u, (n, i) in enumerate(units):
                if n >= 1 and i == 0 and n + 1 < 4:
                    c0, m = panels[n + 1]
                    sp.wait_ge(pe_.sem, pe_.at((n - 1, NC)))
                    sp.dma_start(wb[(n + 1) % 2][:, :, 0:m], w[:, c0:c0 + m].rearrange("(k p) m -> p k m", p=P)) \
                        .then_inc(s[f"w{(n + 1) % 2}"], 16)
                e = eng(u)
                sp.wait_ge(e.sem, e.at(("row", u)))
                r = token_rows(i)
                src = stage_buf[0:r, u % NSL, 0:(256 if n == 1 else 512)]
                so = s[f"out{u % NSL}"]
                rows = slice(P * i, P * i + r)
                if n == 0:
                    dst = O["p_nsa_kv"][0, 0, rows].rearrange("t a g d -> t (a g d)") if i < NC else \
                        O["s_nsa_kv"][0].rearrange("b t a g d -> (b t) (a g d)")
                elif n == 1:
                    dst = W["win"][rows]
                else:
                    dst = O["p_fox_kv"][0, 0, rows, n - 2].rearrange("t h d -> t (h d)") if i < NC else \
                        O["s_fox_kv"][0, :, :, n - 2].rearrange("b t h d -> (b t) (h d)")
                sp.dma_start(dst, src).then_inc(so, 16)
                if n == 1 and i in (6, 7):
                    sp.dma_start(O["p_nsa_win"][0, 0, P * (i - 6):P * (i - 5)].rearrange("j a g d -> j (a g d)"), src).then_inc(so, 16)
                if n == 1 and i == NC:
                    for b in range(1):
                        sp.dma_start(O["s_nsa_win"][0, :, PAST - NT:PAST].rearrange("b j a g d -> b j (a g d)"), src).then_inc(so, 16)
            sp.wait_ge(dve_.sem, dve_.at("gates_done"))
            sp.dma_start(W["gates"], gates[0:NS, NC, :]).then_inc(s["gs"], 16)
            sp.wait_ge(s["gs"], 16)
            sp.wait_ge(s["hist"], 16)
            for k in range(NSL):
                sp.wait_ge(s[f"out{k}"], 16 * stores[k])

        @block.tensor
        def _(pe):
            for u, (n, i) in enumerate(units):
                r, m = token_rows(i), panels[n][1]
                if i == 0:
                    pe.wait_ge(s[f"w{n % 2}"], 16 * (n // 2 + 1))
                if u >= 4:
                    e = eng(u - 4)
                    pe.wait_ge(e.sem, e.at(("read", u - 4)))
                for k in range(KT):
                    mm = pe.matmul(bank(ps, u % 4)[0:r, 0:m], hn[:, k, P * i:P * i + r], wb[n % 2][:, k, 0:m],
                                   start=(k == 0), stop=(k == KT - 1))
                mm.then_inc(pe_.sem, pe_.mark((n, i)))

        def half(e, st, par):
            for u, (n, i) in enumerate(units):
                if u % 2 != par:
                    continue
                r, m = token_rows(i), 256 if n == 1 else 512
                e.wait_ge(pe_.sem, pe_.at((n, i)))
                if u >= NSL:
                    e.wait_ge(s[f"out{u % NSL}"], 16 * sent[u - NSL])
                src = bank(ps, u % 4)[0:r]
                dst = stage_buf[0:r, u % NSL, 0:m]
                op = nc.vector.tensor_copy(dst, src[:, 0:m]) if par else nc.scalar.activation(dst, src[:, 0:m], ACT.Copy)
                op.then_inc(st.sem, st.mark(("row", u)))
                if n == 1:
                    dst, g = gates[0:r, i, :], src[:, 256:280]
                    op = nc.vector.tensor_copy(dst, g) if par else nc.scalar.activation(dst, g, ACT.Copy)
                    op.then_inc(st.sem, st.mark(("read", u)))
                else:
                    st.seen[("read", u)] = st.count

        @block.scalar
        def _(act):
            half(act, act_, 0)
            act.wait_ge(dve_.sem, dve_.at("gates_in"))
            nc.scalar.activation(gates[:], gates[:], ACT.Sigmoid).then_inc(act_.sem, act_.mark("gates"))

        @block.vector
        def _(dve):
            nc.vector.memset(gates[:, NC, :], 0.0).then_inc(dve_.sem, dve_.mark("gate_zero"))
            dve.wait_ge(dve_.sem, dve_.at("gate_zero"))
            half(dve, dve_, 1)
            dve.wait_ge(act_.sem, act_.at(("row", 34)))
            nc.vector.tensor_copy(gates[0:1, 0, 0:1], gates[0:1, 0, 0:1]).then_inc(dve_.sem, dve_.mark("gates_in"))
            dve.wait_ge(act_.sem, act_.at("gates"))
            nc.vector.tensor_scalar(gates[:, 0, 0:24:3], gates[:, 0, 0:24:3], W["rowvalid"][:, 0:1], None, ALU.mult) \
                .then_inc(dve_.sem, dve_.mark("gates_done"))


def fox_rows(pr, I, O, C, hn, F, FS, gS, W, arena, ps):
    nc = pr.nc
    wf, bf = arena([P, KT, 8]), arena([8, 1])
    z, e, lf = arena([8, TP]), arena([8, TP]), arena([8, TP])
    LT = arena([P, NC + 1, 8])
    L = arena([P, 2, NB, 8])
    FN = arena([NS, TK])
    with pr.stage("foxrows", steps=["pe", "act", "dve"], sems=["ld", "pages", "st", "new", "gs"]) as (block, s):
        pe_, act_, dve_ = s["pe"], s["act"], s["dve"]
        acc = ps[:, 0:1536].rearrange("p (c n) -> p c n", n=512)[0:8, :, 0:CH]

        @block.sync
        def _(sp):
            sp.dma_start(wf, I["w_in_odd"][0, :, FF0:FF0 + 8].rearrange("(k p) m -> p k m", p=P),
                         allow_slow_non_contiguous=True).then_inc(s["ld"], 16)
            sp.dma_start(bf, I["fox_b_f"].rearrange("a h -> h a")).then_inc(s["ld"], 16)
            for b in range(NB):
                for g in range(2):
                    page = sp.value_load(W["pages"][0:1, 2 * b + g:2 * b + g + 1], min_val=0, max_val=NPOOL - 1)
                    sp.dma_start(L[:, g, b, :], I["cache_fox_logf"][0, bass.ds(page, 1)].rearrange("o t h -> t (o h)")) \
                        .then_inc(s["pages"], 16)
            for h in range(H):
                sp.dma_start(gS[NT * h:NT * (h + 1)], W["gates"].rearrange("(b t) (h c) -> h t b c", t=NT, c=3)[h],
                             allow_slow_non_contiguous=True).then_inc(s["gs"], 16)
            sp.wait_ge(dve_.sem, dve_.at(("LT", NC)))
            sp.dma_start(O["p_fox_logf"][0, 0].rearrange("(i t) h -> t i h", t=P), LT[:, 0:NC, :]).then_inc(s["st"], 16)
            sp.dma_start(O["s_fox_logf"][0].rearrange("b t h -> (b t) h"), LT[0:NS, NC, :]).then_inc(s["st"], 16)
            sp.wait_ge(s["st"], 32)
            for b in range(NB):
                sp.dma_start(FN[NT * b:NT * (b + 1), PAST:TK], O["s_fox_logf"][0, b].rearrange("t h -> h t"),
                             allow_slow_non_contiguous=True).then_inc(s["new"], 16)
            sp.wait_ge(s["gs"], 16 * H)

        @block.tensor
        def _(pe):
            pe.wait_ge(s["ld"], 32)
            for k in range(KT):
                for j in range(3):
                    mm = pe.matmul(acc[:, j, :], wf[:, k, :], hn[:, k, CH * j:CH * (j + 1)], start=(k == 0), stop=(k == KT - 1))
            mm.then_inc(pe_.sem, pe_.mark("z"))
            pe.wait_ge(s["pages"], 16 * 2 * NB)
            for g in range(2):
                t = pe.transpose(bank(ps, 4)[0:NS, P * g:P * (g + 1)], L[:, g].rearrange("p b h -> p (b h)"), C["ident"][:])
            t.then_inc(pe_.sem, pe_.mark("past"))
            pe.wait_ge(dve_.sem, dve_.at("lf"))
            for i in range(NC + 1):
                r = token_rows(i)
                pe.transpose(bank(ps, 5)[0:r, 8 * i:8 * i + 8], lf[:, P * i:P * i + r], C["ident"][0:8, 0:8]) \
                    .then_inc(pe_.sem, pe_.mark(("LT", i)))

        @block.scalar
        def _(act):
            act.wait_ge(dve_.sem, dve_.at("z"))
            nc.scalar.activation(e, z, ACT.Abs).then_inc(act_.sem, act_.mark("abs"))
            act.wait_ge(act_.sem, act_.at("abs"))
            nc.scalar.activation(e, e, ACT.Exp, scale=-1.0).then_inc(act_.sem, act_.mark("exp"))
            act.wait_ge(act_.sem, act_.at("exp"))
            nc.scalar.activation(e, e, ACT.Ln, bias=1.0).then_inc(act_.sem, act_.mark("l1"))

        @block.vector
        def _(dve):
            V = nc.vector

            def step(name, ins):
                ins.then_inc(dve_.sem, dve_.mark(name))

            def need(name):
                dve.wait_ge(dve_.sem, dve_.at(name))
            dve.wait_ge(pe_.sem, pe_.at("z"))
            step("z", V.tensor_scalar(v3(z), acc, bf, None, ALU.add))
            dve.wait_ge(act_.sem, act_.at("l1"))
            step("lf", V.scalar_tensor_tensor(out=lf, in0=z, scalar=0.0, in1=e, op0=ALU.min, op1=ALU.subtract))
            need("lf")
            step("ones", V.memset(z[:, 0:NPROMPT], 1.0))
            need("ones")
            step("F0", V.memset(F[:], 0.0))
            need("F0")
            step("F", V.tensor_tensor_scan(F[0:8, :], z[:, 0:NPROMPT], lf[:, 0:NPROMPT], 0.0, ALU.mult, ALU.add))
            need("F")
            step("F2", V.tensor_copy(F[64:72, :], F[0:8, :]))
            for i in range(NC + 1):
                r = token_rows(i)
                dve.wait_ge(pe_.sem, pe_.at(("LT", NC)))
                step(("LT", i), V.tensor_copy(LT[0:r, i, :], bank(ps, 5)[0:r, 8 * i:8 * i + 8]))
            dve.wait_ge(pe_.sem, pe_.at("past"))
            step("past", V.tensor_copy(FN[:, 0:PAST], bank(ps, 4)[0:NS, 0:PAST]))
            step("one2", V.memset(W["one"][0:NS, :], 1.0))
            need("one2")
            dve.wait_ge(s["new"], 16 * NB)
            step("FS", V.tensor_tensor_scan(FS[:], W["one"][0:NS, :], FN, 0.0, ALU.mult, ALU.add))


def bias_tables(pr, I, C, B, Bc, Bs, Bcs, relx, oh, ps):
    nc = pr.nc
    with pr.stage("bias", steps=["pe", "act", "dve"], sems=["ld", "rows"]) as (block, s):
        pe_, act_, dve_ = s["pe"], s["act"], s["dve"]

        @block.sync
        def _(sp):
            sp.dma_start(relx[0:32, :], I["rel_bias"]).then_inc(s["ld"], 16)
            sp.dma_start(oh[:], I["c_onehot"]).then_inc(s["ld"], 16)
            sp.wait_ge(dve_.sem, dve_.at("B3"))
            for h in range(H):
                sp.dma_start(Bs[NT * h:NT * (h + 1), :], B[0:NT, h, 0:P + NT]).then_inc(s["rows"], 16)
                sp.dma_start(Bcs[NT * h:NT * (h + 1), :], Bc[0:NT, h, 0:8]).then_inc(s["rows"], 16)
            sp.wait_ge(s["rows"], 16 * 2 * H)

        @block.tensor
        def _(pe):
            pe.wait_ge(s["ld"], 32)
            pe.wait_ge(dve_.sem, dve_.at("neg"))
            for q in range(4):
                for j in range(64 * q, 64 * q + 64):
                    mm = pe.matmul(bank(ps, q)[:, 8 * (j % 64):8 * (j % 64) + 8], oh[:, 2 * P - j:3 * P - j], relx[:], start=True, stop=True)
                mm.then_inc(pe_.sem, pe_.mark(q))
            for n in range(16):
                c0 = 97 - 16 * (n - 9)
                mm = pe.matmul(bank(ps, 4)[:, 8 * n:8 * n + 8], oh[:, c0:c0 + P], relx[:], start=True, stop=True)
            mm.then_inc(pe_.sem, pe_.mark("c"))

        @block.vector
        def _(dve):
            nc.vector.memset(relx[32:33, :], NEG).then_inc(dve_.sem, dve_.mark("neg"))
            dve.wait_ge(pe_.sem, pe_.at("c"))
            nc.vector.tensor_copy(Bc[:], bank(ps, 4)[:, 0:P].rearrange("p (n h) -> p h n", h=8)).then_inc(dve_.sem, dve_.mark("Bc"))
            for q in range(4):
                nc.vector.tensor_copy(B[:, :, 64 * q:64 * q + 64], bank(ps, q).rearrange("p (j h) -> p h j", h=8)) \
                    .then_inc(dve_.sem, dve_.mark(f"B{q}"))


def compress(pr, I, O, C, W, kcD, kcS, vcP, vcS, arena, ps):
    nc = pr.nc
    X = [arena([P, 3072]) for _ in range(2)]
    w1 = [arena([P, 16, 256]) for _ in range(2)]
    w2 = [arena([P, 2, P]) for _ in range(2)]
    pos = [arena([P, 16]) for _ in range(2)]
    tin = arena([P, 2, 4, P])
    hid = [arena([P, 2, 366]) for _ in range(2)]
    pb = arena([P, 4])
    NU = 12
    with pr.stage("compress", steps=["pe", "act", "dve"], sems=["w", "t0", "t1"]) as (block, s):
        pe_, act_, dve_ = s["pe"], s["act"], s["dve"]

        @block.sync
        def _(sp):
            for kv in range(2):
                sp.dma_start(w1[kv], I["nsa_cmp_w1"][0, kv].rearrange("(a q) m -> q a m", q=P)).then_inc(s["w"], 16)
                for x in range(2):
                    sp.dma_start(w2[kv][:, :, 64 * x:64 * x + 64], I["nsa_cmp_w2"][0, kv].rearrange("(m q) d -> q m d", q=P)).then_inc(s["w"], 16)
                sp.dma_start(pos[kv], I["nsa_cmp_pos"][0, kv].rearrange("(a w) d -> (w d) a", w=2),
                             allow_slow_non_contiguous=True).then_inc(s["w"], 16)
            for u in range(NU):
                if u >= 2:
                    sp.wait_ge(pe_.sem, pe_.at(("X", u - 2)))
                st = s[f"t{u % 2}"]
                if u < 4:
                    src = O["p_nsa_kv"][0, 0, 256 * u:256 * (u + 1), 0:2].rearrange("(q w) a g d -> q (a g) w d", w=2)
                    for w in range(2):
                        sp.dma_start(tin[:, u % 2, :, 64 * w:64 * w + 64], src[:, :, w, :]).then_inc(st, 16)
                else:
                    for g in range(2):
                        page = sp.value_load(W["pages"][0:1, 2 * (u - 4) + g:2 * (u - 4) + g + 1], min_val=0, max_val=NPOOL - 1)
                        src = I["cache_nsa_kv"][0, bass.ds(page, 1), :, 0:2].rearrange("o (q w) a g d -> q w (o a g) d", w=2)
                        for w in range(2):
                            sp.dma_start(tin[64 * g:64 * g + 64, u % 2, :, 64 * w:64 * w + 64], src[:, w]).then_inc(st, 16)

        @block.tensor
        def _(pe):
            def need(st, name):
                pe.wait_ge(st.sem, st.at(name))
            for u in range(NU):
                pe.wait_ge(s[f"t{u % 2}"], 32 * (u // 2 + 1) if u < 4 else 64 + 64 * ((u - 4) // 2 + 1))
                if u >= 2:
                    need(act_, ("X", u - 2))
                for a in range(2):
                    for g in range(2):
                        t = pe.transpose(bank(ps, u % 2)[:, P * (2 * a + g):P * (2 * a + g + 1)],
                                         tin[:, u % 2, 2 * a + g, :], C["ident"][:])
                t.then_inc(pe_.sem, pe_.mark(("X", u)))
            pe.wait_ge(s["w"], 16 * 8)
            for kv in range(2):
                for m in range(2):
                    for a in range(16):
                        mm = pe.matmul(bank(ps, 2)[:, 2 * kv + m:2 * kv + m + 1], w1[kv][:, a, P * m:P * (m + 1)], pos[kv][:, a:a + 1],
                                       start=(a == 0), stop=(a == 15))
            mm.then_inc(pe_.sem, pe_.mark("pos"))
            need(act_, ("X", NU - 1))
            need(act_, ("X", NU - 2))
            for kv in range(2):
                xp = X[kv][:, 0:1024].rearrange("p (g n a) -> p g n a", g=2, a=8)
                xs = X[kv][:, 1024:3072].rearrange("p (b n a) -> p b n a", b=16, a=8)
                for m in range(2):
                    hb = bank(ps, 3 + 2 * kv + m)
                    for a in range(16):
                        n0 = a // 8
                        mm = pe.matmul(hb[:, 0:126].rearrange("p (g n) -> p g n", g=2), w1[kv][:, a, P * m:P * (m + 1)], xp[:, :, n0:n0 + 63, a % 8],
                                       start=(a == 0), stop=(a == 15))
                    for a in range(16):
                        n0 = a // 8
                        mm = pe.matmul(hb[:, 126:366].rearrange("p (b n) -> p b n", b=16), w1[kv][:, a, P * m:P * (m + 1)], xs[:, :, n0:n0 + 15, a % 8],
                                       start=(a == 0), stop=(a == 15))
                    mm.then_inc(pe_.sem, pe_.mark(("hid", kv, m)))
            need(act_, ("hid", 1, 1))
            for m in range(2):
                mm = pe.matmul(bank(ps, 0)[:, 0:366], w2[0][:, m, :], hid[0][:, m, :], start=(m == 0), stop=(m == 1))
            mm.then_inc(pe_.sem, pe_.mark("kc"))
            for g in range(2):
                for m in range(2):
                    mm = pe.matmul(bank(ps, 1)[0:63, 64 * g:64 * g + 64], hid[1][:, m, 63 * g:63 * g + 63], w2[1][:, m, 0:64], start=(m == 0), stop=(m == 1))
            for b in range(16):
                for m in range(2):
                    mm = pe.matmul(bank(ps, 6 + b // 8)[0:15, 64 * (b % 8):64 * (b % 8) + 64], hid[1][:, m, 126 + 15 * b:141 + 15 * b], w2[1][:, m, 0:64],
                                   start=(m == 0), stop=(m == 1))
            mm.then_inc(pe_.sem, pe_.mark("vc"))

        @block.scalar
        def _(act):
            for u in range(NU):
                act.wait_ge(pe_.sem, pe_.at(("X", u)))
                for kv in range(2):
                    src = bank(ps, u % 2)[:, 256 * kv:256 * kv + 256].rearrange("p (g n) -> p g n", g=2)
                    if u < 4:
                        dst = X[kv][:, 0:1024].rearrange("p (g n) -> p g n", g=2)[:, :, P * u:P * (u + 1)]
                    else:
                        dst = X[kv][:, 1024 + 256 * (u - 4):1024 + 256 * (u - 3)].rearrange("p (g n) -> p g n", g=2)
                    op = nc.scalar.activation(dst, src, ACT.Copy)
                op.then_inc(act_.sem, act_.mark(("X", u)))
            act.wait_ge(dve_.sem, dve_.at("pos"))
            for kv in range(2):
                for m in range(2):
                    act.wait_ge(pe_.sem, pe_.at(("hid", kv, m)))
                    nc.scalar.activation(hid[kv][:, m, :], bank(ps, 3 + 2 * kv + m)[:, 0:366], ACT.Silu, bias=pb[:, 2 * kv + m:2 * kv + m + 1]) \
                        .then_inc(act_.sem, act_.mark(("hid", kv, m)))

        @block.vector
        def _(dve):
            V = nc.vector

            def step(name, ins):
                ins.then_inc(dve_.sem, dve_.mark(name))
            dve.wait_ge(pe_.sem, pe_.at("pos"))
            step("pos", V.tensor_copy(pb, bank(ps, 2)[:, 0:4]))
            dve.wait_ge(pe_.sem, pe_.at("kc"))
            step("kc", V.tensor_copy(kcD[:], bank(ps, 0)[:, 0:126].rearrange("p (g n) -> p g n", g=2)))
            ks = bank(ps, 0)[:, 126:366].rearrange("p (b g n) -> p b g n", b=NB, g=2)
            for g in range(2):
                step(("kcS", g), V.tensor_copy(kcS[64 * g:64 * g + 64], ks[64 * g:64 * g + 64, :, g, :]))
            dve.wait_ge(pe_.sem, pe_.at("vc"))
            step("vcP", V.tensor_copy(vcP[:], bank(ps, 1)[0:63, 0:P].rearrange("p (g d) -> p g d", g=2)))
            for x in range(2):
                step(("vcS", x), V.tensor_copy(vcS[:, 4 * x:4 * x + 4], bank(ps, 6 + x)[0:15, :].rearrange("p (b v) -> p b v", b=4)))


def load_keys(pr, I, O, C, W, kv_sel, kv_win, fv, kselD, kwinD, kf, tk, ps):
    nc = pr.nc
    with pr.stage("keys", steps=["pe", "act", "dve"], sems=["v", "k0", "k1"]) as (block, s):
        pe_, act_, dve_ = s["pe"], s["act"], s["dve"]

        @block.sync
        def _(sp):
            sp.dma_start(kv_sel[:], O["p_nsa_kv"][0, 0].rearrange("(i t) a g d -> t i (a g d)", t=P)[:, :, 256:512]).then_inc(s["v"], 16)
            sp.dma_start(kv_win[:], W["win"][0:NPROMPT].rearrange("(i t) c -> t i c", t=P)).then_inc(s["v"], 16)
            sp.dma_start(fv[:], O["p_fox_kv"][0, 0, :, 1].rearrange("(i t) h d -> t i (h d)", t=P)).then_inc(s["v"], 16)
            for i in range(NC):
                if i >= 2:
                    sp.wait_ge(pe_.sem, pe_.at(("fox", i - 2)))
                sp.dma_start(tk[:, i % 2, 0:512], O["p_fox_kv"][0, 0, P * i:P * (i + 1), 0].rearrange("t h d -> t (h d)")).then_inc(s[f"k{i % 2}"], 16)
            sp.wait_ge(s["v"], 48)

        @block.tensor
        def _(pe):
            pe.wait_ge(s["v"], 48)
            for i in range(NC):
                if i >= 2:
                    pe.wait_ge(dve_.sem, dve_.at(("nsa", i - 2)))
                    pe.wait_ge(act_.sem, act_.at(("fox", i - 2)))
                pe.wait_ge(dve_.sem, dve_.at(("twice", i)))
                for n in range(4):
                    t = pe.transpose(bank(ps, i % 2)[:, P * n:P * (n + 1)], tk[:, i % 2, 512 + P * n:512 + P * (n + 1)], C["ident"][:])
                t.then_inc(pe_.sem, pe_.mark(("nsa", i)))
                pe.wait_ge(s[f"k{i % 2}"], 16 * (i // 2 + 1))
                for j in range(4):
                    t = pe.transpose(bank(ps, 2 + i % 2)[:, P * j:P * (j + 1)], tk[:, i % 2, P * j:P * (j + 1)], C["ident"][:])
                t.then_inc(pe_.sem, pe_.mark(("fox", i)))

        @block.scalar
        def _(act):
            for i in range(NC):
                act.wait_ge(pe_.sem, pe_.at(("fox", i)))
                nc.scalar.activation(kf[:, :, P * i:P * (i + 1)], bank(ps, 2 + i % 2).rearrange("p (j t) -> p j t", j=4), ACT.Copy) \
                    .then_inc(act_.sem, act_.mark(("fox", i)))

        @block.vector
        def _(dve):
            dve.wait_ge(s["v"], 48)

            def twice(i):
                if i >= 2:
                    dve.wait_ge(pe_.sem, pe_.at(("nsa", i - 2)))
                for n, kv in enumerate((kv_sel, kv_win)):
                    dst = tk[:, i % 2, 512 + 256 * n:768 + 256 * n].rearrange("p (g o d) -> p g o d", g=2, o=2)
                    for o in range(2):
                        ins = nc.vector.tensor_copy(dst[:, :, o, :], kv[:, i, 0:P].rearrange("p (g d) -> p g d", g=2))
                ins.then_inc(dve_.sem, dve_.mark(("twice", i)))
            twice(0)
            for i in range(NC):
                if i + 1 < NC:
                    twice(i + 1)
                dve.wait_ge(pe_.sem, pe_.at(("nsa", i)))
                src = bank(ps, i % 2).rearrange("p (n g t) -> p n g t", n=2, g=2)
                nc.vector.tensor_copy(kselD[:, :, P * i:P * (i + 1)], src[:, 0])
                nc.vector.tensor_copy(kwinD[:, :, P * i:P * (i + 1)], src[:, 1]).then_inc(dve_.sem, dve_.mark(("nsa", i)))


def prompt_attention(pr, C, T, mix, ps):
    nc = pr.nc
    Q, kselD, kwinD, kf, kcD, vcP = T["Q"], T["kselD"], T["kwinD"], T["kf"], T["kcD"], T["vcP"]
    prob, probT, oacc, gates, B, Bc, F = T["prob"], T["probT"], T["oacc"], T["gates"], T["B"], T["Bc"], T["F"]
    nmax, rsum, coef = T["nmax"], T["rsum"], T["coef"]
    units = []
    for i in range(NC):
        for h in range(H):
            units += [(i, "sel", h), (i, "win", h), (i, "cmp", h)]
        units += [(i, "fox", h) for h in range(H)]
    U = len(units)

    def span(u):
        i, kind, h = units[u]
        if kind == "cmp":
            return 0, 8 * i + 7
        k0 = P * max(0, i - 4) if kind == "win" else 0
        return k0, P * (i + 1) - k0

    def groups(u):
        nt = -(-span(u)[1] // P)
        return [(a, min(a + 4, nt)) for a in range(0, nt, 4)]
    first_group = np.cumsum([0] + [len(groups(u)) for u in range(U)]).tolist()
    with pr.stage("attend", steps=["pe", "act", "dve"]) as (block, s):
        pe_, act_, dve_ = s["pe"], s["act"], s["dve"]

        def emptier(gi):
            return act_ if gi % 2 == 0 else dve_

        def S(u):
            return ps[:, 1024 * (u % 2):1024 * (u % 2) + 1024]

        def turned(gi):
            return bank(ps, 4 + gi % 2)

        def O(u):
            return bank(ps, 6 + u % 2)[:, 0:HD]

        def qcol(i):
            return slice(P * i, P * (i + 1))

        @block.tensor
        def _(pe):
            def need(st, name):
                pe.wait_ge(st.sem, st.at(name))

            def scores(u):
                i, kind, h = units[u]
                k0, n = span(u)
                if u >= 2:
                    need(act_, ("exp", u - 2))
                half = slice(64 * (h % 2), 64 * (h % 2) + 64)
                q = Q[half, (4 if kind == "fox" else 0) + h // 2, qcol(i)]
                src = {"sel": kselD, "win": kwinD, "cmp": kcD}.get(kind)
                for a in range(0, n, 512):
                    w = min(512, n - a)
                    k = kf[half, h // 2, k0 + a:k0 + a + w] if kind == "fox" else src[half, h // 4, k0 + a:k0 + a + w]
                    mm = pe.matmul(S(u)[:, a:a + w], q, k, start=True, stop=kind != "fox")
                    if kind == "fox":
                        mm = pe.matmul(S(u)[:, a:a + w], C["headsel"][half, h, :], F[half, a:a + w], start=False, stop=True)
                mm.then_inc(pe_.sem, pe_.mark(("qk", u)))

            def turn_and_weigh(u):
                i, kind, h = units[u]
                k0, n = span(u)
                need(act_, ("exp", u))
                for x, (a, b) in enumerate(groups(u)):
                    gi = first_group[u] + x
                    if gi >= 2:
                        need(emptier(gi - 2), ("turned", gi - 2))
                    for t in range(a, b):
                        w = min(P, n - P * t)
                        mm = pe.transpose(turned(gi)[0:w, P * (t - a):P * (t - a + 1)], prob[:, u % 2, P * t:P * t + w], C["ident"][:])
                    mm.then_inc(pe_.sem, pe_.mark(("turn", gi)))
                if u >= 2:
                    need(dve_, ("o", u - 2))
                nt = -(-n // P)
                for x, (a, b) in enumerate(groups(u)):
                    gi = first_group[u] + x
                    need(emptier(gi), ("turned", gi))
                    for t in range(a, b):
                        w = min(P, n - P * t)
                        if kind == "fox":
                            v = T["fv"][:, t, HD * h:HD * (h + 1)]
                        elif kind == "cmp":
                            v = vcP[0:w, h // 4, :]
                        else:
                            kv = T["kv_sel"] if kind == "sel" else T["kv_win"]
                            v = kv[:, k0 // P + t, 128 + 64 * (h // 4):192 + 64 * (h // 4)]
                        mm = pe.matmul(O(u), probT[0:w, u % 2, t, :], v, start=(t == 0), stop=(t == nt - 1))
                mm.then_inc(pe_.sem, pe_.mark(("pv", u)))

            def rows_out(i):
                need(dve_, ("o", 32 * i + 31))
                if 32 * i + 32 < U:
                    need(act_, ("exp", 32 * i + 30))
                for j in range(8):
                    t = pe.transpose(bank(ps, 6 + j // 4)[:, P * (j % 4):P * (j % 4 + 1)], oacc[:, i % 2, 2 * j:2 * j + 2, :], C["ident"][:])
                t.then_inc(pe_.sem, pe_.mark(("rows", i)))
            scores(0)
            for u in range(U):
                if u + 1 < U:
                    scores(u + 1)
                if u % 32 == 0 and u:
                    need(dve_, ("rows", u // 32 - 1))
                turn_and_weigh(u)
                if u % 32 == 31:
                    rows_out(u // 32)

        @block.scalar
        def _(act):
            def need(st, name):
                act.wait_ge(st.sem, st.at(name))

            def empty(u):
                for x, (a, b) in enumerate(groups(u)):
                    gi = first_group[u] + x
                    if emptier(gi) is act_:
                        need(pe_, ("turn", gi))
                        if u >= 2:
                            need(pe_, ("pv", u - 2))
                        w = min(P, span(u)[1] - P * a)
                        nc.scalar.activation(probT[0:w, u % 2, a:b, :], turned(gi)[0:w, 0:P * (b - a)].rearrange("p (n t) -> p n t", t=P), ACT.Copy) \
                            .then_inc(act_.sem, act_.mark(("turned", gi)))
            for u in range(U):
                need(dve_, ("max", u))
                if u >= 2:
                    need(pe_, ("turn", first_group[u - 1] - 1))
                    need(dve_, ("o", u - 2))
                n = span(u)[1]
                nc.scalar.activation(prob[:, u % 2, 0:n], S(u)[:, 0:n], ACT.Exp, bias=nmax[:, u % 2:u % 2 + 1],
                                     accum_out=rsum[:, u % 2:u % 2 + 1]).then_inc(act_.sem, act_.mark(("exp", u)))
                if u >= 1:
                    empty(u - 1)
            empty(U - 1)

        @block.vector
        def _(dve):
            V = nc.vector

            def step(name, ins):
                ins.then_inc(dve_.sem, dve_.mark(name))

            def need(st, name):
                dve.wait_ge(st.sem, st.at(name))

            def top(u):
                i, kind, h = units[u]
                k0, n = span(u)
                need(pe_, ("qk", u))
                if kind == "cmp":
                    a = max(0, n - 16)
                    step(("bias", u), V.tensor_tensor(S(u)[:, a:n], S(u)[:, a:n], Bc[:, h, 16 - (n - a):16], ALU.add))
                elif kind == "fox":
                    step(("bias", u), V.tensor_tensor(S(u)[:, n - P:n], S(u)[:, n - P:n], C["causal"][:], ALU.add))
                else:
                    a = max(0, n - 2 * P)
                    if kind == "win" and i >= 4:
                        step(("far", u), V.tensor_tensor(S(u)[:, 0:P], S(u)[:, 0:P], C["farmask"][:], ALU.add))
                    step(("bias", u), V.tensor_tensor(S(u)[:, a:n], S(u)[:, a:n], B[:, h, 2 * P - (n - a):2 * P], ALU.add))
                need(dve_, ("bias", u))
                if u >= 2:
                    need(act_, ("exp", u - 2))
                step(("max", u), V.tensor_reduce(nmax[:, u % 2:u % 2 + 1], S(u)[:, 0:n], AX, ALU.max, negate=True))

            def finish(u):
                i, kind, h = units[u]
                for x, (a, b) in enumerate(groups(u)):
                    gi = first_group[u] + x
                    if emptier(gi) is dve_:
                        need(pe_, ("turn", gi))
                        if u >= 2:
                            need(pe_, ("pv", u - 2))
                        w = min(P, span(u)[1] - P * a)
                        step(("turned", gi), V.tensor_copy(probT[0:w, u % 2, a:b, :], turned(gi)[0:w, 0:P * (b - a)].rearrange("p (n t) -> p n t", t=P)))
                need(act_, ("exp", u))
                step(("rec", u), V.reciprocal(coef[:, u % 2:u % 2 + 1], rsum[:, u % 2:u % 2 + 1]))
                need(dve_, ("rec", u))
                col = coef[:, u % 2:u % 2 + 1]
                if kind != "fox":
                    g = 3 * h + {"cmp": 0, "sel": 1, "win": 2}[kind]
                    step(("coef", u), V.tensor_tensor(col, col, gates[:, i, g:g + 1], ALU.mult))
                    need(dve_, ("coef", u))
                need(pe_, ("pv", u))
                if i >= 2 and u % 32 == 0:
                    need(pe_, ("rows", i - 2))
                o = oacc[:, i % 2, (8 if kind == "fox" else 0) + h, :]
                if kind in ("fox", "sel"):
                    step(("o", u), V.tensor_scalar(o, O(u), col, None, ALU.mult))
                else:
                    step(("o", u), V.scalar_tensor_tensor(out=o, in0=O(u), scalar=col, in1=o, op0=ALU.mult, op1=ALU.add))
            for u in range(U):
                top(u)
                if u >= 1:
                    finish(u - 1)
                if u % 32 == 0 and u:
                    i = u // 32 - 1
                    need(pe_, ("rows", i))
                    for b in range(2):
                        ins = V.tensor_copy(mix[:, 4 * b:4 * b + 4, qcol(i)], bank(ps, 6 + b).rearrange("p (j t) -> p j t", j=4))
                    step(("rows", i), ins)
            finish(U - 1)
            need(pe_, ("rows", NC - 1))
            for b in range(2):
                ins = V.tensor_copy(mix[:, 4 * b:4 * b + 4, qcol(NC - 1)], bank(ps, 6 + b).rearrange("p (j t) -> p j t", j=4))
            step(("rows", NC - 1), ins)


def sample_attention(pr, I, O, C, W, T, mix, arena, ps):
    nc = pr.nc
    Q, gS, FS, Bs, Bcs, kcS, vcS = T["Q"], T["gS"], T["FS"], T["Bs"], T["Bcs"], T["kcS"], T["vcS"]
    Qn = arena([P, NB, NS])
    Qf = arena([P, 4, NB, NS])
    pages = [arena([P, 2, 256]) for _ in range(2)]
    wins = [arena([P, 2, 256]) for _ in range(2)]
    foxs = [arena([P, 2, 1024]) for _ in range(2)]
    new = [arena([NT, 1536]) for _ in range(2)]
    kT = arena([P, 6, TK])
    pr_ = arena([NS, 4, TK])
    pT = arena([P, 10, NS])
    nmx, rs, cf = arena([NS, 4]), arena([NS, 4]), arena([NS, 4])
    nk = [TK, TK, TK, 15]
    with pr.stage("sample", steps=["pe", "act", "dve"], sems=["in0", "in1"]) as (block, s):
        pe_, act_, dve_ = s["pe"], s["act"], s["dve"]
        OUTN = bank(ps, 6).rearrange("p (b c) -> p b c", b=NB)
        OUTF = bank(ps, 7).rearrange("p (j b c) -> p j b c", j=4, b=NB)

        @block.sync
        def _(sp):
            for b in range(NB):
                x, st = b % 2, s[f"in{b % 2}"]
                if b >= 2:
                    sp.wait_ge(pe_.sem, pe_.at(("pv", b - 2)))
                for g in range(2):
                    page = sp.value_load(W["pages"][0:1, 2 * b + g:2 * b + g + 1], min_val=0, max_val=NPOOL - 1)
                    sp.dma_start(pages[x][:, g], I["cache_nsa_kv"][0, bass.ds(page, 1), :, 2:4].rearrange("o t a g d -> t (o a g d)")).then_inc(st, 16)
                    sp.dma_start(foxs[x][:, g], I["cache_fox_kv"][0, bass.ds(page, 1)].rearrange("o t a h d -> t (o a h d)")).then_inc(st, 16)
                sp.dma_start(wins[x], I["state_nsa_win"][0, b].rearrange("(g t) a k d -> t g (a k d)", t=P)).then_inc(st, 16)
                sp.dma_start(new[x][:, 0:256], O["s_nsa_kv"][0, b, :, 2:4].rearrange("t a g d -> t (a g d)")).then_inc(st, 16)
                sp.dma_start(new[x][:, 256:512], W["win"][NPROMPT + NT * b:NPROMPT + NT * (b + 1)]).then_inc(st, 16)
                sp.dma_start(new[x][:, 512:1536], O["s_fox_kv"][0, b].rearrange("t a h d -> t (a h d)")).then_inc(st, 16)

        @block.tensor
        def _(pe):
            def need(st, name):
                pe.wait_ge(st.sem, st.at(name))
            for b in range(NB):
                x = b % 2
                pe.wait_ge(s[f"in{x}"], 128 * (b // 2 + 1))
                if b:
                    need(act_, ("pT", b - 1))
                    need(dve_, ("pT", b - 1))
                if b == 0:
                    need(dve_, ("zb", 5))
                for n in range(6):
                    for g in range(3):
                        w = P if g < 2 else NT
                        if n < 2:
                            src = (pages, wins)[n][x][:, g, 0:P] if g < 2 else new[x][:, 256 * n:256 * n + P]
                        else:
                            src = foxs[x][:, g, P * (n - 2):P * (n - 1)] if g < 2 else new[x][:, 512 + P * (n - 2):512 + P * (n - 1)]
                        t = pe.transpose(bank(ps, n)[:, P * g:P * g + w], src, C["ident"][0:w, 0:w])
                    t.then_inc(pe_.sem, pe_.mark(("kT", b, n)))
                for n in range(6):
                    e = act_ if n % 2 else dve_
                    need(e, ("kT", b, n))
                pe.matmul(bank(ps, 0)[0:NS, 0:TK], Qn[:, b, :], kT[:, 0, :], start=True, stop=True)
                pe.matmul(bank(ps, 1)[0:NS, 0:TK], Qn[:, b, :], kT[:, 1, :], start=True, stop=True)
                for j in range(4):
                    pe.matmul(bank(ps, 2)[0:NS, 0:TK], Qf[:, j, b, :], kT[:, 2 + j, :], start=(j == 0), stop=False)
                pe.matmul(bank(ps, 2)[0:NS, 0:TK], C["foxsel"][:, b, :], FS[:], start=False, stop=True)
                pe.matmul(bank(ps, 3)[0:NS, 0:15], Qn[:, b, :], kcS[:, b, :], start=True, stop=True).then_inc(pe_.sem, pe_.mark(("qk", b)))
                need(dve_, ("p", b))
                for n in range(10):
                    k, g = n // 3, n % 3
                    w = 15 if k == 3 else (P if g < 2 else NT)
                    t = pe.transpose(bank(ps, 4 + n // 5)[0:w, NS * (n % 5):NS * (n % 5 + 1)], pr_[:, k, P * g:P * g + w], C["ident"][0:NS, 0:NS])
                    if n % 5 == 4:
                        t.then_inc(pe_.sem, pe_.mark(("turn", b, n // 5)))
                need(act_, ("pT", b))
                need(dve_, ("pT", b))
                for n in range(6):
                    k, g = n // 3, n % 3
                    w = P if g < 2 else NT
                    v = (pages, wins)[k][x][:, g, P:2 * P] if g < 2 else new[x][:, 256 * k + P:256 * k + 2 * P]
                    pe.matmul(OUTN[:, b, :], v, pT[0:w, n, :], start=(n == 0), stop=False)
                pe.matmul(OUTN[:, b, :], vcS[:, b, :], pT[0:15, 9, :], start=False, stop=True)
                for j in range(4):
                    for g in range(3):
                        w = P if g < 2 else NT
                        v = foxs[x][:, g, 512 + P * j:512 + P * (j + 1)] if g < 2 else new[x][:, 1024 + P * j:1024 + P * (j + 1)]
                        mm = pe.matmul(OUTF[:, j, b, :], v, pT[0:w, 6 + g, 16 * j:16 * j + 16], start=(g == 0), stop=(g == 2))
                mm.then_inc(pe_.sem, pe_.mark(("pv", b)))

        @block.scalar
        def _(act):
            def need(st, name):
                act.wait_ge(st.sem, st.at(name))
            for b in range(NB):
                for n in (1, 3, 5):
                    need(pe_, ("kT", b, n))
                    nc.scalar.activation(kT[:, n, :], bank(ps, n)[:, 0:TK], ACT.Copy).then_inc(act_.sem, act_.mark(("kT", b, n)))
                need(dve_, ("max", b))
                for k in range(4):
                    ins = nc.scalar.activation(pr_[:, k, 0:nk[k]], bank(ps, k)[0:NS, 0:nk[k]], ACT.Exp, bias=nmx[:, k:k + 1], accum_out=rs[:, k:k + 1])
                ins.then_inc(act_.sem, act_.mark(("exp", b)))
                need(pe_, ("turn", b, 0))
                nc.scalar.activation(pT[:, 0:5, :], bank(ps, 4)[:, 0:5 * NS].rearrange("p (n c) -> p n c", n=5), ACT.Copy) \
                    .then_inc(act_.sem, act_.mark(("pT", b)))

        @block.vector
        def _(dve):
            V = nc.vector

            def step(name, ins):
                ins.then_inc(dve_.sem, dve_.mark(name))

            def need(st, name):
                dve.wait_ge(st.sem, st.at(name))
            step("z0", V.memset(Qn, 0.0))
            step("z1", V.memset(Qf, 0.0))
            for n in (4, 5):
                step(("zb", n), V.memset(bank(ps, n), 0.0))
            need(dve_, "z1")
            for h in range(H):
                g, x = h // 4, h % 2
                src = Q[64 * x:64 * x + 64, h // 2, NPROMPT:TOK].rearrange("p (b t) -> p b t", t=NT)
                step(("Qn", h), V.tensor_copy(Qn[64 * g:64 * g + 64, :, NT * h:NT * (h + 1)], src))
                src = Q[64 * x:64 * x + 64, 4 + h // 2, NPROMPT:TOK].rearrange("p (b t) -> p b t", t=NT)
                step(("Qf", h), V.tensor_copy(Qf[64 * x:64 * x + 64, h // 2, :, NT * h:NT * (h + 1)], src))
            for b in range(NB):
                for n in (0, 2, 4):
                    need(pe_, ("kT", b, n))
                    step(("kT", b, n), V.tensor_copy(kT[:, n, :], bank(ps, n)[:, 0:TK]))
                need(pe_, ("qk", b))
                for k in range(2):
                    v = bank(ps, k)[0:NS, P:TK]
                    step(("bias", b, k), V.tensor_tensor(v, v, Bs[:], ALU.add))
                v = bank(ps, 2)[0:NS, PAST:TK]
                step(("bias", b, 2), V.tensor_tensor(v, v, C["samplemask"][:], ALU.add))
                v = bank(ps, 3)[0:NS, 7:15]
                step(("bias", b, 3), V.tensor_tensor(v, v, Bcs[:], ALU.add))
                need(dve_, ("bias", b, 3))
                for k in range(4):
                    ins = V.tensor_reduce(nmx[:, k:k + 1], bank(ps, k)[0:NS, 0:nk[k]], AX, ALU.max, negate=True)
                step(("max", b), ins)
                need(act_, ("exp", b))
                step(("rec", b), V.reciprocal(cf, rs))
                need(dve_, ("rec", b))
                for k, c in ((0, 1), (1, 2), (3, 0)):
                    ins = V.tensor_tensor(cf[:, k:k + 1], cf[:, k:k + 1], gS[:, b, c:c + 1], ALU.mult)
                step(("cf", b), ins)
                need(dve_, ("cf", b))
                for k in range(4):
                    ins = V.tensor_scalar(pr_[:, k, 0:nk[k]], pr_[:, k, 0:nk[k]], cf[:, k:k + 1], None, ALU.mult)
                step(("p", b), ins)
                need(pe_, ("turn", b, 1))
                step(("pT", b), V.tensor_copy(pT[:, 5:10, :], bank(ps, 5)[:, 0:5 * NS].rearrange("p (n c) -> p n c", n=5)))
            need(pe_, ("pv", NB - 1))
            for h in range(H):
                g, x = h // 4, h % 2
                dst = mix[64 * x:64 * x + 64, h // 2, NPROMPT:TOK].rearrange("p (b t) -> p b t", t=NT)
                step(("on", h), V.tensor_copy(dst, OUTN[64 * g:64 * g + 64, :, NT * h:NT * (h + 1)]))
                dst = mix[64 * x:64 * x + 64, 4 + h // 2, NPROMPT:TOK].rearrange("p (b t) -> p b t", t=NT)
                step(("of", h), V.tensor_copy(dst, OUTF[64 * x:64 * x + 64, h // 2, :, NT * x:NT * (x + 1)]))
            step("pad", V.memset(mix[:, :, TOK:TP], 0.0))


def layer1(pr, I, O, C, xT, hn, wslots, ps):
    nc = pr.nc
    W = {"win": nc.dram_tensor("win_rows", [TOK, 256], F32).ap(), "gates": nc.dram_tensor("gate_rows", [NS, 24], F32).ap()}
    saved = nc.dram_tensor("x_saved1", [P, KT * TP], F32).ap()
    move(pr, "save_x1", saved, xT[:].rearrange("p k t -> p (k t)"))
    xflat, wflat = xT[:].rearrange("p k t -> p (k t)"), wslots[:].rearrange("p a k m -> p (a k m)")
    with ExitStack() as c:
        def sb(n, shape, dt=F32):
            return c.enter_context(nc.sbuf_tensor(n, shape, dt))
        T = {"Q": sb("Q", [P, 8, TP]), "gates": sb("gates", [P, NC + 1, 24]), "F": sb("F", [P, NPROMPT]), "FS": sb("FS", [NS, TK]),
             "gS": sb("gS", [NS, NB, 3]), "B": sb("B", [P, H, 256]), "Bc": sb("Bc", [P, H, 16]), "Bs": sb("Bs", [NS, P + NT]),
             "Bcs": sb("Bcs", [NS, 8]), "kcD": sb("kcD", [P, 2, 63]), "kcS": sb("kcS", [P, NB, 15]), "vcP": sb("vcP", [63, 2, HD]),
             "vcS": sb("vcS", [15, NB, P])}
        W["pages"] = sb("pages", [1, 2 * NB], I32)
        W["rowvalid"] = sb("rowvalid", [P, 1])
        W["one"] = sb("one", [NS, TK])
        with pr.stage("const1", sems=["ld"]) as (block, s):
            @block.sync
            def _(sp):
                sp.dma_start(W["pages"][:], I["page_table"].rearrange("b (g o) -> o (b g)", o=1)).then_inc(s["ld"], 16)
                sp.dma_start(W["rowvalid"][:], I["c_rowvalid"]).then_inc(s["ld"], 16)
                sp.wait_ge(s["ld"], 32)
        w = I["w_in_odd"][0]
        tiles = []
        for n in range(8):
            def epi(e, i, acc, n=n):
                dst = v3(T["Q"][:, n, :])
                return nc.vector.tensor_scalar(dst, acc, HD ** -0.5, None, ALU.mult) if n % 2 else \
                    nc.scalar.activation(dst, acc, ACT.Copy, scale=HD ** -0.5)
            c0 = P * n if n < 4 else FQ0 + P * (n - 4)
            tiles.append(dict(w=lambda i, c0=c0: w[:, c0:c0 + P], x=hn, epi=epi, by="dve" if n % 2 else "act"))
        stream(pr, "queries", ps, wslots, 1, tiles)
        with ExitStack() as c2:
            wide = c2.enter_context(nc.sbuf_tensor("wide", [P, KT, 512], F32))
            rows = c2.enter_context(nc.sbuf_tensor("rows", [P, 4, 512], F32))
            token_major(pr, I, O, W, hn, wslots, wide, rows, T["gates"], ps)
            fox_rows(pr, I, O, C, hn, T["F"], T["FS"], T["gS"], W, Arena(xflat, wflat), ps)
        with ExitStack() as c2:
            relx = c2.enter_context(nc.sbuf_tensor("relx", [33, 8], F32))
            oh = c2.enter_context(nc.sbuf_tensor("onehot", [33, 3 * P], F32))
            bias_tables(pr, I, C, T["B"], T["Bc"], T["Bs"], T["Bcs"], relx, oh, ps)
        with ExitStack() as c2:
            more = c2.enter_context(nc.sbuf_tensor("more", [P, 8000], F32))
            compress(pr, I, O, C, W, T["kcD"], T["kcS"], T["vcP"], T["vcS"], Arena(xflat, wflat, more[:]), ps)
        with ExitStack() as c2:
            more = c2.enter_context(nc.sbuf_tensor("more2", [P, 13000], F32))
            ar = Arena(xflat, wflat, more[:])
            for n, shape in (("kv_sel", [P, NC, 256]), ("kv_win", [P, NC, 256]), ("fv", [P, NC, 512]), ("kf", [P, 4, NPROMPT]),
                             ("kselD", [P, 2, NPROMPT]), ("kwinD", [P, 2, NPROMPT]), ("prob", [P, 2, NPROMPT])):
                T[n] = ar(shape)
            T["nmax"], T["rsum"], T["coef"] = ar([P, 2]), ar([P, 2]), ar([P, 2])
            T["oacc"] = ar([P, 2, 16, HD])
            load_keys(pr, I, O, C, W, T["kv_sel"], T["kv_win"], T["fv"], T["kselD"], T["kwinD"], T["kf"], T["prob"], ps)
            T["probT"] = ar([P, 2, NC, P])
            prompt_attention(pr, C, T, hn, ps)
        with ExitStack() as c2:
            more = c2.enter_context(nc.sbuf_tensor("more3", [P, 8000], F32))
            sample_attention(pr, I, O, C, W, T, hn, Arena(xflat, wflat, more[:]), ps)
    move(pr, "load_x1", xT[:].rearrange("p k t -> p (k t)"), saved)


def write_y(pr, O, C, hn, rows, ps):
    nc = pr.nc
    with pr.stage("writey", steps=["pe", "act", "dve"], sems=["y0", "y1"]) as (block, s):
        pe_, act_, dve_ = s["pe"], s["act"], s["dve"]

        @block.tensor
        def _(pe):
            for i in range(NC + 1):
                r = token_rows(i)
                if i >= 2:
                    pe.wait_ge(act_.sem, act_.at(i - 2))
                    pe.wait_ge(dve_.sem, dve_.at(i - 2))
                for k in range(KT):
                    t = pe.transpose(bank(ps, 2 * (i % 2) + k // 4)[0:r, P * (k % 4):P * (k % 4 + 1)], hn[:, k, P * i:P * i + r], C["ident"][:])
                t.then_inc(pe_.sem, pe_.mark(i))

        def half(e, st, b):
            for i in range(NC + 1):
                r = token_rows(i)
                e.wait_ge(pe_.sem, pe_.at(i))
                if i >= 2:
                    e.wait_ge(s[f"y{i % 2}"], 16 * (i // 2))
                dst, src = rows[0:r, i % 2, 512 * b:512 * (b + 1)], bank(ps, 2 * (i % 2) + b)[0:r]
                op = nc.vector.tensor_copy(dst, src) if b else nc.scalar.activation(dst, src, ACT.Copy)
                op.then_inc(st.sem, st.mark(i))

        @block.scalar
        def _(act):
            half(act, act_, 0)

        @block.vector
        def _(dve):
            half(dve, dve_, 1)

        @block.sync
        def _(sp):
            for i in range(NC + 1):
                sp.wait_ge(act_.sem, act_.at(i))
                sp.wait_ge(dve_.sem, dve_.at(i))
                dst = O["y_prompt"][0, P * i:P * (i + 1), :] if i < NC else O["y_sample"].rearrange("b t d -> (b t) d")
                sp.dma_start(dst, rows[0:token_rows(i), i % 2, :]).then_inc(s[f"y{i % 2}"], 16)
            sp.wait_ge(s["y0"], 16 * 5)
            sp.wait_ge(s["y1"], 16 * 4)


def t5_bucket(n):
    n = np.maximum(n, 0)
    nf = np.maximum(n, 1).astype(np.float32)
    large = 16 + (np.log(nf / np.float32(16)) / np.float32(np.log(8.0)) * np.float32(16)).astype(np.int32)
    return np.where(n < 16, n, np.minimum(large, 31))


def constants():
    f = np.float32
    t = np.arange(P)
    k = {"ident": np.eye(P, dtype=f), "ones": np.ones((P, P), f)}
    k["maskP"] = np.where(t[:, None] <= t[None, :], 0, NEG).astype(f)
    same = t[:, None] // NT == t[None, :] // NT
    k["maskS"] = np.where((t[:, None] <= t[None, :]) & same, 0, NEG).astype(f)
    lv = []
    for n in range(7):
        z = 1 << n
        lv.append((t[:, None] // (2 * z) == t[None, :] // (2 * z)) & (t[:, None] % (2 * z) < z) & (t[None, :] % (2 * z) >= z))
    k["level"] = np.stack(lv, 1).astype(f)
    sel = np.zeros((P, 16, P), f)
    for q in range(4):
        for h in range(4):
            sel[32 * q + h, 4 * q + h, :] = 1
    k["sel"] = sel
    keep = np.ones((4, TP), f)
    keep[:, 0:NPROMPT:P] = 0
    keep[:, NPROMPT::NT] = 0
    k["keep"] = keep
    d = np.arange(-P, 2 * P)
    oh = np.zeros((33, 3 * P), f)
    oh[t5_bucket(d), np.arange(3 * P)] += 1
    oh[31] -= 1
    oh[:, d < 0] = 0
    oh[32, d < 0] = 1
    k["onehot"] = oh
    k["causal"] = np.where(t[None, :] > t[:, None], NEG, 0).astype(f)
    k["farmask"] = np.where(t[None, :] <= t[:, None], NEG, 0).astype(f)
    k["rowvalid"] = (t >= 31).astype(f)[:, None]
    row = np.arange(NS)
    k["samplemask"] = np.where(np.arange(NT)[None, :] > (row % NT)[:, None], NEG, 0).astype(f)
    fs = np.zeros((NS, NB, NS), f)
    for b in range(NB):
        for r in range(NS):
            fs[NT * b + r // NT, b, r] = -1
    k["foxsel"] = fs
    hs = np.zeros((P, 8, P), f)
    for h in range(8):
        hs[h, h] = hs[64 + h, h] = -1
    k["headsel"] = hs
    return k


def load_constants(pr, I, names, tiles, stage="const"):
    with pr.stage(stage, sems=["ld"]) as (block, s):
        @block.sync
        def _(sp):
            for n in names:
                sp.dma_start(tiles[n][:], I["c_" + n]).then_inc(s["ld"], 16)
            sp.wait_ge(s["ld"], 16 * len(names))


def program(nc, I, O, values, dbg=None, only=None):
    pr = Program(nc, values)
    with ExitStack() as c:
        xT = c.enter_context(nc.sbuf_tensor("xT", [P, KT, TP], F32))
        C = {}
        for n in ("ident", "ones"):
            C[n] = c.enter_context(nc.sbuf_tensor("sb_" + n, list(I["c_" + n].shape), F32))
        ps = c.enter_context(nc.psum_tensor("ps", [P, 8 * 512], F32))
        load_constants(pr, I, list(C), C)
        load_x(pr, I, xT, C["ident"], ps)
        with ExitStack() as c2:
            hn = c2.enter_context(nc.sbuf_tensor("hn", [P, KT, TP], F32))
            wslots = c2.enter_context(nc.sbuf_tensor("wslots", [P, 4, KT, P], F32))
            C0 = dict(C)
            with ExitStack() as c3:
                for n in ("maskP", "maskS", "level", "sel", "keep"):
                    C0[n] = c3.enter_context(nc.sbuf_tensor("sb_" + n, list(I["c_" + n].shape), F32))
                load_constants(pr, I, ["maskP", "maskS", "level", "sel", "keep"], C0, "const0")
                layer0(pr, I, O, C0, xT, hn, wslots, ps, dbg and (lambda n, *a: dbg(pr, n, *a)))
            if dbg and dbg(pr, 5, xT): return pr.found
            with ExitStack() as c3:
                u = c3.enter_context(nc.sbuf_tensor("u", [P, KT, TP], F32))
                rt = c3.enter_context(nc.sbuf_tensor("rt", [P, 2, TP], F32))
                rmsnorm(pr, "norm1", xT, hn, rt[:, 0], rt[:, 1], I["norm_mlp"][0], C["ones"], ps)
                mlp(pr, I, 0, xT, hn, u, rt, wslots, ps)
            if dbg and dbg(pr, 6, xT): return pr.found
            with ExitStack() as c3:
                names1 = ["causal", "farmask", "samplemask", "foxsel", "headsel"]
                C1 = dict(C)
                for n in names1:
                    C1[n] = c3.enter_context(nc.sbuf_tensor("sb_" + n, list(I["c_" + n].shape), F32))
                load_constants(pr, I, names1, C1, "const2")
                with ExitStack() as c4:
                    rt = c4.enter_context(nc.sbuf_tensor("rt2", [P, 2, TP], F32))
                    rmsnorm(pr, "norm2", xT, hn, rt[:, 0], rt[:, 1], I["norm_mix"][1], C["ones"], ps)
                layer1(pr, I, O, C1, xT, hn, wslots, ps)
            if dbg and dbg(pr, 7, hn): return pr.found
            residual_product(pr, "wout1", I["w_out_odd"][0], hn, xT, wslots, ps)
            if dbg and dbg(pr, 8, xT): return pr.found
            with ExitStack() as c3:
                u = c3.enter_context(nc.sbuf_tensor("u1", [P, KT, TP], F32))
                rt = c3.enter_context(nc.sbuf_tensor("rt3", [P, 2, TP], F32))
                rmsnorm(pr, "norm3", xT, hn, rt[:, 0], rt[:, 1], I["norm_mlp"][1], C["ones"], ps)
                mlp(pr, I, 1, xT, hn, u, rt, wslots, ps)
                rmsnorm(pr, "norm4", xT, hn, rt[:, 0], rt[:, 1], I["norm_final"], C["ones"], ps)
                write_y(pr, O, C, hn, u[:].rearrange("p k t -> p (k t)")[:, 0:2 * DM].rearrange("p (a n) -> p a n", a=2), ps)
    return pr.found


_OUTS = [
    ("y_prompt", (1, 1024, 1024)), ("y_sample", (8, 8, 1024)),
    ("p_mlstm_c", (1, 1, 4, 64, 128)), ("p_mlstm_n", (1, 1, 4, 64)), ("p_mlstm_m", (1, 1, 4)), ("p_gdn_s", (1, 1, 4, 128, 128)),
    ("p_gdn_conv", (1, 1, 3, 1536)), ("p_nsa_kv", (1, 1, 1024, 4, 2, 64)), ("p_nsa_win", (1, 1, 256, 2, 2, 64)),
    ("p_fox_kv", (1, 1, 1024, 2, 8, 64)), ("p_fox_logf", (1, 1, 1024, 8)),
    ("s_mlstm_c", (1, 8, 4, 64, 128)), ("s_mlstm_n", (1, 8, 4, 64)), ("s_mlstm_m", (1, 8, 4)), ("s_gdn_s", (1, 8, 4, 128, 128)),
    ("s_gdn_conv", (1, 8, 3, 1536)), ("s_nsa_kv", (1, 8, 8, 4, 2, 64)), ("s_nsa_win", (1, 8, 256, 2, 2, 64)),
    ("s_fox_kv", (1, 8, 8, 2, 8, 64)), ("s_fox_logf", (1, 8, 8, 8)),
]


def kernel(**inputs):
    import concourse.bacc as _bacc
    from concourse.bass_utils import run_bass_kernel_spmd as _run

    arrays = {f"in_{k}": np.ascontiguousarray(v) for k, v in inputs.items()}
    arrays.update({f"in_c_{k}": np.ascontiguousarray(v) for k, v in constants().items()})

    def build(values):
        nc = _bacc.Bacc("TRN2", target_bir_lowering=False, num_devices=1)
        ins = {k[3:]: nc.dram_tensor(k, v.shape, mybir.dt.from_np(v.dtype), kind="ExternalInput").ap() for k, v in arrays.items()}
        outs = {k: nc.dram_tensor(f"out_{k}", s, F32, kind="ExternalOutput").ap() for k, s in _OUTS}
        return nc, program(nc, ins, outs, values)
    _, values = build({})
    nc, _ = build(values)
    r = _run(nc, [arrays], core_ids=[0])
    return tuple(r.results[0][f"out_{k}"] for k, _ in _OUTS)
```

```python
from contextlib import ExitStack, contextmanager

import numpy as np
import concourse.bass as bass
from concourse import mybir

F32 = mybir.dt.float32
F32R = mybir.dt.float32r
I32 = mybir.dt.int32
ALU = mybir.AluOpType
ACT = mybir.ActivationFunctionType
AX = mybir.AxisListType.X

P = 128
DM = 1024
KT = DM // P
NPROMPT = 1024
NB, NT = 8, 8
NS = NB * NT
TOK = NPROMPT + NS
CH = 364
TP = 3 * CH
NC = NPROMPT // P
DFF = 4 * DM
EPS = 1e-6
NEG = -1e30
PAST = 256
TK = PAST + NT
NPOOL = 20
WIN = 512
H = 8
HD = 64


class Steps:

    def __init__(self, handle, values):
        self.sem, self.values, self.count, self.first = handle, values, 0, not values
        self.seen = {}

    def mark(self, name, by=1):
        assert name not in self.seen, name
        self.count += by
        self.seen[name] = self.count
        return by

    def at(self, name):
        return 1 if self.first else self.values[name]


class Program:

    def __init__(self, nc, values):
        self.nc, self.values, self.found = nc, values, {}

    @contextmanager
    def stage(self, name, steps=(), sems=()):
        nc = self.nc
        all_ = {}
        for s in steps:
            all_[s] = Steps(nc.alloc_semaphore(name=f"{name}_{s}"), self.values.get((name, s), {}))
        for s in sems:
            all_[s] = nc.alloc_semaphore(name=f"{name}_{s}")
        with nc.Block(no_gpsimd_drain=False) as block:
            yield block, all_
        for s in steps:
            self.found[(name, s)] = all_[s].seen
        nc.clear_and_free_semaphores([v.sem if isinstance(v, Steps) else v for v in all_.values()])
        nc.all_engine_barrier()


class Arena:

    def __init__(self, *buffers):
        self.free = [[b, 0] for b in buffers]

    def __call__(self, shape):
        p, dims = shape[0], shape[1:]
        n = int(np.prod(dims))
        for f in self.free:
            if f[1] + n <= f[0].shape[1]:
                ap = f[0][0:p, f[1]:f[1] + n]
                f[1] += n + n % 2
                if len(dims) > 1:
                    names = " ".join("abc"[:len(dims)])
                    ap = ap.rearrange(f"p ({names}) -> p {names}", **dict(zip("abc", dims[:-1])))
                return ap
        raise ValueError(f"no room for {shape}")


def bank(ps, n):
    return ps[:, 512 * n:512 * (n + 1)]


ROUNDED = {}


def two_ways(nc, c, name, shape):
    with nc.sbuf_tensor(name + "_r32", shape, F32R) as rounded:
        ROUNDED[name] = rounded
    return c.enter_context(nc.sbuf_tensor(name, shape, F32))


def r32(ap):
    return bass.AP(tensor=ROUNDED[ap.tensor.name], offset=ap.offset, ap=ap.ap)


HALVES = ((1, 0), (0, 1), (0, 0))


def split(pr, name, tiles, copy=None):
    nc = pr.nc
    with pr.stage(name, sems=["high", "low_dve", "low_pool", "moved"]) as (block, s):
        def lows(e, E, which, done):
            for k in which:
                src, hi, lo = tiles[k]
                e.wait_ge(s["high"], k + 1)
                E.tensor_tensor(r32(lo), src, r32(hi), ALU.subtract).then_inc(s[done], 1)

        @block.sync
        def _(sp):
            if copy:
                sp.dma_start(*copy).then_inc(s["moved"], 16)
                sp.wait_ge(s["moved"], 16)

        @block.scalar
        def _(act):
            for src, hi, lo in tiles:
                nc.scalar.activation(r32(hi), src, ACT.Copy).then_inc(s["high"], 1)

        @block.vector
        def _(dve):
            lows(dve, nc.vector, [k for k in range(len(tiles)) if k % 3 != 1], "low_dve")

        @block.gpsimd
        def _(pool):
            lows(pool, nc.gpsimd, [k for k in range(len(tiles)) if k % 3 == 1], "low_pool")


def stream(pr, name, ps, W, iters, tiles):
    nc = pr.nc
    nb = len(tiles)
    assert nb % 2 == 0
    raw, half, one = W["raw"], W["half"], W["ones"][:].unsqueeze(1).to_broadcast([P, KT, P])
    deep = max(len(t["steps"]) for t in tiles)
    longer = [[n for n, t in enumerate(tiles) if len(t["steps"]) > j] for j in range(deep)]

    def over(e):
        class One:
            def __enter__(self):
                return 0

            def __exit__(self, *a):
                return False
        return e.Fori(0, iters) if iters > 1 else One()

    sems = ["w0", "w1", "high", "split", "product", "set0_free", "set1_free"] + [f"step{j}" for j in range(1, deep)]
    with pr.stage(name, sems=sems) as (block, s):
        view = [ps[:, 1536 * k:1536 * (k + 1)].rearrange("p (c n) -> p c n", n=512)[:, :, 0:CH] for k in (0, 1)]
        free = [s["set0_free"], s["set1_free"]]

        @block.sync
        def _(sp):
            with over(sp) as i:
                for n, t in enumerate(tiles):
                    sp.wait_ge(s["split"], i * nb + n + 1)
                    sp.dma_start(raw[:, n % 2], t["w"](i).rearrange("(k p) m -> p k m", p=P)).then_inc(s[f"w{n % 2}"], 16)

        @block.gpsimd
        def _(pool):
            pool.sem_inc(s["split"], 2)
            with over(pool) as i:
                for n, t in enumerate(tiles):
                    pool.wait_ge(s[f"w{n % 2}"], i * (8 * nb) + 16 * (n // 2 + 1))
                    pool.wait_ge(s["product"], i * nb + n + 1)
                    nc.gpsimd.tensor_tensor(r32(half[0][:, n % 2]), raw[:, n % 2], one, ALU.mult).then_inc(s["high"], 1)
                    pool.wait_ge(s["high"], i * nb + n + 1)
                    nc.gpsimd.tensor_tensor(r32(half[1][:, n % 2]), raw[:, n % 2], r32(half[0][:, n % 2]), ALU.subtract) \
                        .then_inc(s["split"], 1)

        @block.tensor
        def _(pe):
            pe.sem_inc(s["product"], 2)
            with over(pe) as i:
                for n, t in enumerate(tiles):
                    pe.wait_ge(s["split"], i * nb + n + 3)
                    pe.wait_ge(free[n % 2], i * (nb // 2) + n // 2 + 1)
                    if t.get("need"):
                        for k in (0, 1):
                            pe.wait_ge(free[k], i * (nb // 2) + (t["need"] + 1 - k) // 2 + 1)
                    for k in range(KT):
                        for a, b in HALVES:
                            for c in range(3):
                                mm = pe.matmul(view[n % 2][:, c, :], r32(half[a][:, n % 2, k, :]),
                                               r32(t["x"][b][:, k, CH * c:CH * (c + 1)]),
                                               start=(k == 0 and (a, b) == HALVES[0]), stop=(k == KT - 1 and (a, b) == HALVES[-1]))
                    mm.then_inc(s["product"], 1)

        def steps_of(who, e, E):
            with over(e) as i:
                for n, t in enumerate(tiles):
                    for j, (eng, f) in enumerate(t["steps"]):
                        if eng != who:
                            continue
                        if j == 0:
                            e.wait_ge(s["product"], i * nb + n + 3)
                        else:
                            e.wait_ge(s[f"step{j}"], i * len(longer[j]) + longer[j].index(n) + 1)
                        last = j == len(t["steps"]) - 1
                        f(E, i, view[n % 2]).then_inc(free[n % 2] if last else s[f"step{j + 1}"], 1)

        @block.scalar
        def _(act):
            act.sem_inc(s["set0_free"], 1)
            act.sem_inc(s["set1_free"], 1)
            steps_of("act", act, nc.scalar)

        @block.vector
        def _(dve):
            steps_of("dve", dve, nc.vector)


def v3(ap):
    return ap.rearrange("p (c n) -> p c n", n=CH)


def chunk_pieces():
    cuts = sorted({P * i for i in range(NC + 1)} | {CH * c for c in range(3)} | {TP})
    return [(a // P, a // CH, a, b) for a, b in zip(cuts, cuts[1:])]


def rmsnorm(pr, name, xT, hn, total, diag, g_dram, ident, ones, ps, low=None, save=None):
    nc = pr.nc
    with ExitStack() as c:
        gcol = c.enter_context(nc.sbuf_tensor(f"{name}_g", [P, KT], F32))
        r = c.enter_context(nc.sbuf_tensor(f"{name}_r", [P, NC + 1], F32))
        with pr.stage(name, steps=["pe", "act", "dve", "pool"], sems=["g", "saved"]) as (block, s):
            pe_, act_, dve_, pool_ = s["pe"], s["act"], s["dve"], s["pool"]
            spread = ps[:, 0:1536].rearrange("p (c n) -> p c n", n=512)[:, :, 0:CH]
            sums = bank(ps, 3)[:, 0:NC + 1]
            width = lambda i: min(P, TP - P * i)

            @block.sync
            def _(sp):
                sp.dma_start(gcol[:], g_dram.rearrange("(k p) -> p k", p=P),
                             allow_slow_non_contiguous=True).then_inc(s["g"], 16)
                if save is not None:
                    sp.dma_start(save, xT[:].rearrange("p k t -> p (k t)")).then_inc(s["saved"], 16)
                    sp.wait_ge(s["saved"], 16)

            @block.scalar
            def _(act):
                for k in range(KT):
                    nc.scalar.activation(hn[:, k, :], xT[:, k, :], ACT.Square).then_inc(act_.sem, act_.mark(("sq", k)))
                act.wait_ge(dve_.sem, dve_.at("mean"))
                nc.scalar.activation(r[:], r[:], ACT.Sqrt).then_inc(act_.sem, act_.mark("root"))
                if low is not None:
                    for k in range(KT):
                        act.wait_ge(dve_.sem, dve_.at(("hn", k)))
                        nc.scalar.activation(r32(hn[:, k, :]), low[:, k, :], ACT.Copy).then_inc(act_.sem, act_.mark(("high", k)))

            def lower(e, st, E, k):
                e.wait_ge(act_.sem, act_.at(("high", k)))
                E.tensor_tensor(r32(low[:, k, :]), low[:, k, :], r32(hn[:, k, :]), ALU.subtract).then_inc(st.sem, st.mark(("low", k)))

            @block.gpsimd
            def _(pool):
                if low is not None:
                    for k in (1, 3, 5):
                        lower(pool, pool_, nc.gpsimd, k)

            @block.tensor
            def _(pe):
                pe.wait_ge(dve_.sem, dve_.at(("sum", KT - 1)))
                for i in range(NC + 1):
                    mm = pe.matmul(sums[0:width(i), i:i + 1], total[:, P * i:P * i + width(i)], ones[:, 0:1], start=True, stop=True)
                mm.then_inc(pe_.sem, pe_.mark("sums"))
                pe.wait_ge(dve_.sem, dve_.at("diag"))
                for i, c_, t0, t1 in chunk_pieces():
                    mm = pe.matmul(spread[:, c_, t0 - CH * c_:t1 - CH * c_], ones[0:width(i)], diag[0:width(i), i, t0 - P * i:t1 - P * i],
                                   start=True, stop=True)
                mm.then_inc(pe_.sem, pe_.mark("spread"))

            @block.vector
            def _(dve):
                nc.vector.memset(r[:], 1.0).then_inc(dve_.sem, dve_.mark("r"))
                for k in range(1, KT):
                    dve.wait_ge(act_.sem, act_.at(("sq", k)))
                    if k > 1:
                        dve.wait_ge(dve_.sem, dve_.at(("sum", k - 1)))
                    nc.vector.tensor_tensor(total, hn[:, 0, :] if k == 1 else total, hn[:, k, :], ALU.add) \
                        .then_inc(dve_.sem, dve_.mark(("sum", k)))
                dve.wait_ge(pe_.sem, pe_.at("sums"))
                nc.vector.tensor_scalar(r[:, 0:NC], sums[:, 0:NC], 1.0 / DM, EPS, ALU.mult, ALU.add) \
                    .then_inc(dve_.sem, dve_.mark("mean0"))
                w = width(NC)
                nc.vector.tensor_scalar(r[0:w, NC:NC + 1], sums[0:w, NC:NC + 1], 1.0 / DM, EPS, ALU.mult, ALU.add) \
                    .then_inc(dve_.sem, dve_.mark("mean"))
                dve.wait_ge(act_.sem, act_.at("root"))
                nc.vector.reciprocal(r[:], r[:]).then_inc(dve_.sem, dve_.mark("rstd"))
                dve.wait_ge(dve_.sem, dve_.at("rstd"))
                nc.vector.tensor_tensor(diag, ident[:].unsqueeze(1).to_broadcast([P, NC + 1, P]),
                                        r[:].unsqueeze(2).to_broadcast([P, NC + 1, P]), ALU.mult) \
                    .then_inc(dve_.sem, dve_.mark("diag"))
                dve.wait_ge(pe_.sem, pe_.at("spread"))
                dve.wait_ge(s["g"], 16)
                if save is not None:
                    dve.wait_ge(s["saved"], 16)
                out = hn if low is None else low
                for k in range(KT):
                    nc.vector.scalar_tensor_tensor(out=v3(out[:, k, :]), in0=v3(xT[:, k, :]), scalar=gcol[:, k:k + 1],
                                                   in1=spread, op0=ALU.mult, op1=ALU.mult) \
                        .then_inc(dve_.sem, dve_.mark(("hn", k)))
                    if low is not None and k >= 2 and k % 2 == 0:
                        lower(dve, dve_, nc.vector, k - 2)
                if low is not None:
                    lower(dve, dve_, nc.vector, 6)
                    lower(dve, dve_, nc.vector, 7)


def token_rows(i):
    return P if i < NC else NS


def load_x(pr, I, xT, ident, ps):
    nc = pr.nc
    with ExitStack() as c:
        xin = c.enter_context(nc.sbuf_tensor("xin", [P, 2, DM], F32))
        with pr.stage("loadx", steps=["pe", "act", "dve"], sems=["x0", "x1"]) as (block, s):
            pe_, act_, dve_ = s["pe"], s["act"], s["dve"]

            @block.sync
            def _(sp):
                for i in range(NC + 1):
                    if i >= 2:
                        sp.wait_ge(pe_.sem, pe_.at(("turned", i - 2)))
                    src = I["x_prompt"][0, P * i:P * (i + 1), :] if i < NC else \
                        I["x_sample"].rearrange("b t d -> (b t) d")
                    sp.dma_start(xin[0:token_rows(i), i % 2, :], src).then_inc(s[f"x{i % 2}"], 16)

            @block.tensor
            def _(pe):
                for i in range(NC + 1):
                    r = token_rows(i)
                    pe.wait_ge(s[f"x{i % 2}"], 16 * (i // 2 + 1))
                    if i >= 2:
                        pe.wait_ge(act_.sem, act_.at(("x", i - 2)))
                        pe.wait_ge(dve_.sem, dve_.at(("x", i - 2)))
                    for k in range(KT):
                        t = pe.transpose(bank(ps, 2 * (i % 2) + k // 4)[:, P * (k % 4):P * (k % 4) + r],
                                         xin[0:r, i % 2, P * k:P * (k + 1)], ident[0:r, 0:r])
                    t.then_inc(pe_.sem, pe_.mark(("turned", i)))

            def half(e, st, b):
                if b:
                    nc.vector.memset(xT[:, :, TOK:TP], 0.0).then_inc(st.sem, st.mark("pad"))
                for i in range(NC + 1):
                    r = token_rows(i)
                    e.wait_ge(pe_.sem, pe_.at(("turned", i)))
                    src = bank(ps, 2 * (i % 2) + b).rearrange("p (k t) -> p k t", k=4)[:, :, 0:r]
                    dst = xT[:, 4 * b:4 * b + 4, P * i:P * i + r]
                    op = nc.vector.tensor_copy(dst, src) if b else nc.scalar.activation(dst, src, ACT.Copy)
                    op.then_inc(st.sem, st.mark(("x", i)))

            @block.scalar
            def _(act):
                half(act, act_, 0)

            @block.vector
            def _(dve):
                half(dve, dve_, 1)


def even_gates(pr, I, O, C, zg, GC, RT, arena, ps):
    nc = pr.nc
    Q = [slice(32 * q, 32 * q + 4) for q in range(4)]
    with ExitStack() as c:
        def sb(n, shape):
            return c.enter_context(nc.sbuf_tensor("eg_" + n, shape, F32))
        bias, al = sb("bias", [P, 1]), sb("al", [4, 1])
        z, l1, colr = zg, arena([P, TP]), arena([P, TP])
        rows = {n: arena([4, TP]) for n in ("li", "lf", "b", "m", "mp", "beta", "g", "gc", "t3", "t4")}
        rows["t1"], rows["t2"] = rows["mp"], rows["m"]
        m0 = sb("m0", [4, NB])
        mout = sb("mout", [4, 1 + NB])
        with pr.stage("evengates", steps=["pe", "act", "dve"], sems=["ld", "st"]) as (block, s):
            pe_, act_, dve_ = s["pe"], s["act"], s["dve"]

            @block.sync
            def _(sp):
                sp.wait_ge(dve_.sem, dve_.at("zero"))
                for q, n in ((0, "mi_b_i"), (1, "mi_b_f"), (3, "gd_dt_bias")):
                    sp.dma_start(bias[Q[q], :], I[n].rearrange("a h -> h a")).then_inc(s["ld"], 16)
                sp.dma_start(al[:], I["gd_a_log"].rearrange("a h -> h a")).then_inc(s["ld"], 16)
                sp.dma_start(m0[:], I["state_mlstm_m"][0].rearrange("b h -> h b"),
                             allow_slow_non_contiguous=True).then_inc(s["ld"], 16)
                sp.wait_ge(dve_.sem, dve_.at("m_out"))
                sp.dma_start(O["p_mlstm_m"].rearrange("a b h -> (b h) a"), mout[:, 0:1]).then_inc(s["st"], 16)
                sp.dma_start(O["s_mlstm_m"][0].rearrange("b h -> h b"), mout[:, 1:1 + NB],
                             allow_slow_non_contiguous=True).then_inc(s["st"], 16)
                sp.wait_ge(s["st"], 32)

            @block.scalar
            def _(act):
                act.wait_ge(dve_.sem, dve_.at("z"))
                nc.scalar.activation(l1[:], z[:], ACT.Abs).then_inc(act_.sem, act_.mark("abs"))
                act.wait_ge(act_.sem, act_.at("abs"))
                nc.scalar.activation(l1[:], l1[:], ACT.Exp, scale=-1.0).then_inc(act_.sem, act_.mark("e"))
                act.wait_ge(act_.sem, act_.at("e"))
                nc.scalar.activation(l1[:], l1[:], ACT.Ln, bias=1.0).then_inc(act_.sem, act_.mark("l1"))
                act.wait_ge(s["ld"], 80)
                nc.scalar.activation(al[:], al[:], ACT.Exp).then_inc(act_.sem, act_.mark("al"))
                nc.scalar.activation(rows["beta"][:], z[Q[2], :], ACT.Sigmoid).then_inc(act_.sem, act_.mark("beta"))
                act.wait_ge(dve_.sem, dve_.at("t3"))
                nc.scalar.activation(RT[Q[1], :], rows["t3"][:], ACT.Exp).then_inc(act_.sem, act_.mark("ainter"))
                nc.scalar.activation(RT[Q[2], :], rows["m"][:], ACT.Exp, scale=-1.0).then_inc(act_.sem, act_.mark("em"))
                act.wait_ge(dve_.sem, dve_.at("gc"))
                nc.scalar.activation(rows["t4"][:], rows["gc"][:], ACT.Exp).then_inc(act_.sem, act_.mark("egc"))

            @block.vector
            def _(dve):
                def step(name, ins):
                    ins.then_inc(dve_.sem, dve_.mark(name))

                def need(name):
                    dve.wait_ge(dve_.sem, dve_.at(name))
                V = nc.vector
                R = rows
                step("zero", V.memset(bias[:], 0.0))
                step("zero2", V.memset(RT[:], 0.0))
                step("zero3", V.memset(colr[:], 0.0))
                dve.wait_ge(s["ld"], 80)
                need("zero")
                step("z", V.tensor_scalar(z[:], zg[:], bias[:, 0:1], None, ALU.add))
                need("z")
                step("li", V.tensor_copy(R["li"][:], z[Q[0], :]))
                step("zf", V.tensor_copy(R["lf"][:], z[Q[1], :]))
                step("zg", V.tensor_copy(R["g"][:], z[Q[3], :]))
                dve.wait_ge(act_.sem, act_.at("l1"))
                step("l1f", V.tensor_copy(R["t1"][:], l1[Q[1], :]))
                step("l1g", V.tensor_copy(R["t2"][:], l1[Q[3], :]))
                need("l1g")
                step("lf", V.scalar_tensor_tensor(out=R["lf"][:], in0=R["lf"][:], scalar=0.0, in1=R["t1"][:],
                                                  op0=ALU.min, op1=ALU.subtract))
                step("sp", V.scalar_tensor_tensor(out=R["g"][:], in0=R["g"][:], scalar=0.0, in1=R["t2"][:],
                                                  op0=ALU.max, op1=ALU.add))
                dve.wait_ge(act_.sem, act_.at("al"))
                need("sp")
                step("g", V.tensor_scalar(R["g"][:], R["g"][:], al[:, 0:1], -1.0, ALU.mult, ALU.mult))
                need("lf")
                step("b", V.tensor_tensor_scan(R["b"][:], C["keep"][0:4, :], R["lf"][:], 0.0, ALU.mult, ALU.add))
                need("g")
                step("gc", V.tensor_tensor_scan(R["gc"][:], C["keep"][0:4, :], R["g"][:], 0.0, ALU.mult, ALU.add))
                step("m_p", V.tensor_tensor_scan(R["m"][:, 0:NPROMPT], R["lf"][:, 0:NPROMPT], R["li"][:, 0:NPROMPT],
                                                 0.0, ALU.add, ALU.max))
                for b in range(NB):
                    w = slice(NPROMPT + NT * b, NPROMPT + NT * (b + 1))
                    step(("m_s", b), V.tensor_tensor_scan(R["m"][:, w], R["lf"][:, w], R["li"][:, w],
                                                          m0[:, b:b + 1], ALU.add, ALU.max))
                step("m_pad", V.memset(R["m"][:, TOK:TP], 0.0))
                step("mp0", V.memset(R["mp"][:], 0.0))
                need("m_pad")
                need("mp0")
                ends = R["m"][:, P - 1:P * (NC - 1):P].rearrange("h (c o) -> h c o", o=1)
                step("mp1", V.tensor_copy(R["mp"][:, P:NPROMPT].rearrange("h (c t) -> h c t", t=P),
                                          ends.broadcast_to([4, NC - 1, P])))
                step("mp2", V.tensor_copy(R["mp"][:, NPROMPT:TOK].rearrange("h (b t) -> h b t", t=NT),
                                          m0[:].rearrange("h (b o) -> h b o", o=1).broadcast_to([4, NB, NT])))
                step("r1", V.tensor_tensor(RT[Q[0], :], R["b"][:], R["m"][:], ALU.subtract))
                step("r1b", V.tensor_tensor(R["t3"][:], R["b"][:], R["m"][:], ALU.subtract))
                need("r1b")
                step("t3", V.tensor_tensor(R["t3"][:], R["t3"][:], R["mp"][:], ALU.add))
                step("rgc", V.tensor_copy(RT[Q[3], :], R["gc"][:]))
                step("mo1", V.tensor_copy(mout[:, 0:1], R["m"][:, NPROMPT - 1:NPROMPT]))
                step("m_out", V.tensor_copy(mout[:, 1:1 + NB], R["m"][:, NPROMPT + NT - 1:TOK:NT]))
                step("c1", V.tensor_tensor(colr[Q[0], :], R["li"][:], R["b"][:], ALU.subtract))
                step("c2", V.tensor_scalar(colr[Q[1], :], R["gc"][:], -1.0, None, ALU.mult))
                dve.wait_ge(act_.sem, act_.at("egc"))
                step("c3", V.tensor_copy(colr[Q[2], :], R["beta"][:]))
                step("c4", V.tensor_tensor(colr[Q[3], :], R["beta"][:], R["t4"][:], ALU.mult))
                for i in range(NC + 1):
                    r = token_rows(i)
                    dve.wait_ge(pe_.sem, pe_.at(("turn", i)))
                    step(("GC", i), V.tensor_copy(GC[0:r, i, :], bank(ps, i % 8)[0:r, 0:P]))

            @block.tensor
            def _(pe):
                pe.wait_ge(dve_.sem, dve_.at("c4"))
                for i in range(NC + 1):
                    r = token_rows(i)
                    if i == 8:
                        pe.wait_ge(dve_.sem, dve_.at(("GC", 0)))
                    pe.transpose(bank(ps, i % 8)[0:r, 0:P], colr[:, P * i:P * i + r], C["ident"][:]) \
                        .then_inc(pe_.sem, pe_.mark(("turn", i)))


def gate_product(pr, I, hn, low, zg, W, save, ps):
    nc = pr.nc
    starts = [1536, 1540, 3592, 3596]
    raw, half = W["raw"][:, 0], [h[:, 0] for h in W["half"]]
    with pr.stage("gatemm", steps=["pe", "dve"], sems=["ld", "saved"]) as (block, s):
        pe_, dve_ = s["pe"], s["dve"]
        acc = ps[:, 0:1536].rearrange("p (c n) -> p c n", n=512)[:, :, 0:CH]

        @block.sync
        def _(sp):
            sp.wait_ge(dve_.sem, dve_.at("zero"))
            for q, c0 in enumerate(starts):
                sp.dma_start(raw[:, :, 32 * q:32 * q + 4],
                             I["w_in_even"][0, :, c0:c0 + 4].rearrange("(k p) m -> p k m", p=P),
                             allow_slow_non_contiguous=True).then_inc(s["ld"], 16)
            sp.dma_start(save, r32(low[:].rearrange("p k t -> p (k t)")).bitcast(F32)).then_inc(s["saved"], 16)
            sp.wait_ge(s["saved"], 16)

        @block.tensor
        def _(pe):
            pe.wait_ge(dve_.sem, dve_.at("w_low"))
            for k in range(KT):
                for a, b in HALVES:
                    for j in range(3):
                        mm = pe.matmul(acc[:, j, :], r32(half[a][:, k, :]), r32((hn, low)[b][:, k, CH * j:CH * (j + 1)]),
                                       start=(k == 0 and (a, b) == HALVES[0]), stop=(k == KT - 1 and (a, b) == HALVES[-1]))
            mm.then_inc(pe_.sem, pe_.mark("z"))

        @block.vector
        def _(dve):
            nc.vector.memset(raw, 0.0).then_inc(dve_.sem, dve_.mark("zero"))
            dve.wait_ge(s["ld"], 64)
            nc.vector.tensor_copy(r32(half[0]), raw).then_inc(dve_.sem, dve_.mark("w_high"))
            dve.wait_ge(dve_.sem, dve_.at("w_high"))
            nc.vector.tensor_tensor(r32(half[1]), raw, r32(half[0]), ALU.subtract).then_inc(dve_.sem, dve_.mark("w_low"))
            dve.wait_ge(pe_.sem, pe_.at("z"))
            nc.vector.tensor_copy(v3(zg[:]), acc).then_inc(dve_.sem, dve_.mark("zg"))


def conv(pr, I, O, C, Z, arena, ps):
    nc = pr.nc
    T = 12
    with ExitStack() as c:
        def sb(n, shape):
            return arena(shape)
        hist_in, hist, wrow, wcol = sb("hi", [24, T * P]), sb("h", [P, T, 24]), sb("wr", [4, T * P]), sb("wc", [P, T, 4])
        last, lastT = sb("last", [P, T, 27]), sb("lastT", [27, T * P])
        y, xs = sb("y", [P, 2, TP]), sb("xs", [P, 2, NB, 11])
        rr = sb("rr", [P, TP])
        with pr.stage("conv", steps=["pe", "act", "dve"], sems=["ld", "st"]) as (block, s):
            pe_, act_, dve_ = s["pe"], s["act"], s["dve"]
            hp = bank(ps, 0)[:, 0:T * 24].rearrange("p (j n) -> p j n", n=24)
            wp = bank(ps, 1)[:, 0:T * 4].rearrange("p (j n) -> p j n", n=4)
            lp = bank(ps, 2)
            acc = ps[:, 1536:3072].rearrange("p (c n) -> p c n", n=512)[:, :, 0:CH]

            @block.sync
            def _(sp):
                sp.dma_start(hist_in[:], I["state_gdn_conv"][0].rearrange("b j c -> (b j) c")).then_inc(s["ld"], 16)
                sp.dma_start(wrow[:], I["gd_conv_w"][0]).then_inc(s["ld"], 16)
                sp.wait_ge(dve_.sem, dve_.at(("lastT", 2)))
                sp.dma_start(O["p_gdn_conv"][0, 0], lastT[0:3, :]).then_inc(s["st"], 16)
                sp.dma_start(O["s_gdn_conv"][0].rearrange("b j c -> (b j) c"), lastT[3:27, :]).then_inc(s["st"], 16)
                sp.wait_ge(s["st"], 32)

            @block.tensor
            def _(pe):
                pe.wait_ge(s["ld"], 32)
                for j in range(T):
                    pe.transpose(hp[:, j, :], hist_in[:, P * j:P * (j + 1)], C["ident"][0:24, 0:24])
                    t = pe.transpose(wp[:, j, :], wrow[:, P * j:P * (j + 1)], C["ident"][0:4, 0:4])
                t.then_inc(pe_.sem, pe_.mark("hist"))
                pe.wait_ge(dve_.sem, dve_.at("last"))
                for q in range(3):
                    if q:
                        pe.wait_ge(dve_.sem, dve_.at(("lastT", q - 1)))
                    for j in range(4 * q, 4 * q + 4):
                        t = pe.transpose(lp[0:27, P * (j - 4 * q):P * (j - 4 * q + 1)], last[:, j, :], C["ident"][:])
                    t.then_inc(pe_.sem, pe_.mark(("lastT", q)))
            @block.vector
            def _(dve):
                V = nc.vector

                def step(name, ins):
                    ins.then_inc(dve_.sem, dve_.mark(name))

                def need(name):
                    dve.wait_ge(dve_.sem, dve_.at(name))
                dve.wait_ge(pe_.sem, pe_.at("hist"))
                step("hist", V.tensor_copy(hist[:], hp))
                step("wcol", V.tensor_copy(wcol[:], wp))
                step("last0", V.tensor_copy(last[:, :, 0:3], Z[:, 8:20, NPROMPT - 3:NPROMPT]))
                for j in range(3):
                    step(("last1", j), V.tensor_copy(last[:, :, 3 + j:27:3], Z[:, 8:20, NPROMPT + 5 + j:TOK:NT]))
                step("last", V.memset(rr[:, 0:1], 0.0))
                for q in range(3):
                    dve.wait_ge(pe_.sem, pe_.at(("lastT", q)))
                    step(("lastT", q), V.tensor_copy(lastT[:, 512 * q:512 * (q + 1)], lp[0:27, :]))
                need("wcol")
                for j in range(T):
                    z, b = Z[:, 8 + j, :], j % 2
                    ys = y[:, b, NPROMPT:TOK].rearrange("p (b t) -> p b t", t=NT)
                    zs = z[:, NPROMPT:TOK].rearrange("p (b t) -> p b t", t=NT)
                    step(("xs0", j), V.tensor_copy(xs[:, b, :, 0:3], hist[:, j, :].rearrange("p (b t) -> p b t", t=3)))
                    step(("xs1", j), V.tensor_copy(xs[:, b, :, 3:11], zs))
                    dve.wait_ge(act_.sem, act_.at(("tap", j)))
                    for d in (1, 2, 3):
                        need(("xs1", j) if d == 1 else (f"y{d - 1}s", j))
                        w = wcol[:, j, 3 - d:4 - d]
                        step((f"y{d}p", j), V.scalar_tensor_tensor(
                            out=y[:, b, d:NPROMPT], in0=z[:, 0:NPROMPT - d], scalar=w, in1=y[:, b, d:NPROMPT],
                            op0=ALU.mult, op1=ALU.add))
                        step((f"y{d}s", j), V.scalar_tensor_tensor(
                            out=ys, in0=xs[:, b, :, 3 - d:11 - d], scalar=w, in1=ys, op0=ALU.mult, op1=ALU.add))

            @block.scalar
            def _(act):
                def tap(j):
                    act.wait_ge(dve_.sem, dve_.at("wcol"))
                    if j >= 2:
                        act.wait_ge(act_.sem, act_.at(("silu", j - 2)))
                    nc.scalar.activation(y[:, j % 2, :], Z[:, 8 + j, :], ACT.Copy, scale=wcol[:, j, 3:4]).then_inc(act_.sem, act_.mark(("tap", j)))
                tap(0)
                tap(1)
                for j in range(T):
                    act.wait_ge(dve_.sem, dve_.at(("y3s", j)))
                    nc.scalar.activation(Z[:, 8 + j, :], y[:, j % 2, :], ACT.Silu).then_inc(act_.sem, act_.mark(("silu", j)))
                    if j + 2 < T:
                        tap(j + 2)


def mlstm(pr, I, O, C, Z, GC, RT, arena, ps):
    nc = pr.nc
    with ExitStack() as c:
        def sb(n, shape):
            return arena(shape)
        Cs = sb("C", [P, 2, 129])
        Cb = sb("Cb", [P, 1 + NB, 2, 129])
        nbc = sb("nbc", [P, 2, P])
        nbs = sb("nbs", [P, NB, 2, P])
        kt, vt = sb("kt", [P, 4, 64]), sb("vt", [P, 4, 129])
        dt, pt, kw, qa = sb("dt", [P, 4, P]), sb("pt", [P, 4, P]), sb("kw", [P, 4, 64]), sb("qa", [P, 4, P])
        qz = sb("qz", [P, 4, P])
        ab, den, eb = sb("ab", [P, 4, P]), sb("den", [P, 4, P]), sb("eb", [P, 4, P])
        kwb = sb("kwb", [NS, 2, 4, 64])

        def b4(n):
            return bank(ps, n).rearrange("p (h t) -> p h t", h=4)
        ST, RB, AB, EB, TR, NUM, DEN, CU = (b4(n) for n in range(8))
        with pr.stage("mlstm", steps=["pe", "act", "dve"], sems=["ld", "st"]) as (block, s):
            pe_, act_, dve_ = s["pe"], s["act"], s["dve"]

            def cols(i):
                return slice(P * i, P * i + token_rows(i))

            def hp(h):
                return slice(64 * (h % 2), 64 * (h % 2) + 64)

            @block.sync
            def _(sp):
                for x in range(2):
                    sl = slice(64 * x, 64 * x + 64)
                    for b in range(NB):
                        sp.dma_start(Cb[sl, 1 + b, :, 0:P], I["state_mlstm_c"][0, b].rearrange("(y x) d v -> x d y v", x=2)[x]) \
                            .then_inc(s["ld"], 16)
                    for y in range(2):
                        sp.dma_start(Cb[sl, 1:, y, P:P + 1], I["state_mlstm_n"][0, :, 2 * y + x, :].rearrange("b (d o) -> d b o", o=1),
                                     allow_slow_non_contiguous=True).then_inc(s["ld"], 16)
                sp.wait_ge(dve_.sem, dve_.at(("C", NC - 1, 3)))
                for x in range(2):
                    sl = slice(64 * x, 64 * x + 64)
                    sp.dma_start(O["p_mlstm_c"][0, 0].rearrange("(y x) d v -> x d y v", x=2)[x], Cs[sl, :, 0:P]).then_inc(s["st"], 16)
                    sp.dma_start(O["p_mlstm_n"][0, 0].rearrange("(y x) (d o) -> x d y o", x=2, o=1)[x], Cs[sl, :, P:P + 1],
                                 allow_slow_non_contiguous=True).then_inc(s["st"], 16)
                sp.wait_ge(dve_.sem, dve_.at(("Cb", NB - 1, 3)))
                for x in range(2):
                    sl = slice(64 * x, 64 * x + 64)
                    for b in range(NB):
                        sp.dma_start(O["s_mlstm_c"][0, b].rearrange("(y x) d v -> x d y v", x=2)[x], Cb[sl, 1 + b, :, 0:P]) \
                            .then_inc(s["st"], 16)
                    for y in range(2):
                        sp.dma_start(O["s_mlstm_n"][0, :, 2 * y + x, :].rearrange("b (d o) -> d b o", o=1), Cb[sl, 1:, y, P:P + 1],
                                     allow_slow_non_contiguous=True).then_inc(s["st"], 16)
                sp.wait_ge(s["st"], 16 * (4 + 20))

            @block.tensor
            def _(pe):
                def need(st, name):
                    pe.wait_ge(st.sem, st.at(name))

                def bcast(q, dst, i, r):
                    for h in range(4):
                        mm = pe.matmul(dst[:, h, 0:r], C["sel"][:, 4 * q + h, :], RT[:, cols(i)], start=True, stop=True)
                    return mm

                for i in range(NC + 1):
                    r = token_rows(i)
                    if i:
                        need(act_, ("kt", i - 1))
                        need(dve_, ("ab", i - 1))
                        need(dve_, ("pt", i - 1))
                        need(act_, ("eb", i - 1))
                        need(dve_, ("D", i - 1))
                        need(act_, ("vt", i - 1))
                        need(dve_, ("C", i - 1, 3))
                    need(dve_, ("qz", i))
                    for h in range(4):
                        if h % 2 == 0:
                            t = pe.transpose(TR.rearrange("p h t -> p (h t)")[0:r, 64 * h:64 * h + P], Z[:, 2 + h // 2, cols(i)], C["ident"][:])
                        pe.matmul(ST[0:r, h, 0:r], Z[:, 2 + h // 2, cols(i)], qz[:, h, 0:r], start=True, stop=True)
                    bcast(0, RB, i, r).then_inc(pe_.sem, pe_.mark(("RB", i)))
                    bcast(1, AB, i, r).then_inc(pe_.sem, pe_.mark(("AB", i)))
                    bcast(2, EB, i, r).then_inc(pe_.sem, pe_.mark(("EB", i)))
                    for h in range(4):
                        t = pe.transpose(CU[0:r, h, :], Z[:, 4 + h, cols(i)], C["ident"][:])
                    t.then_inc(pe_.sem, pe_.mark(("VT", i)))
                    need(dve_, ("pt", i))
                    need(act_, ("vt", i))
                    need(dve_, ("qa", i))
                    if i:
                        need(dve_, ("h", i - 1))
                        need(dve_, ("den", i - 1))
                    last = i == NC
                    need(dve_, "nbs" if last else ("nbc", i))
                    for h in range(4):
                        pe.matmul(NUM[:, h, 0:r], vt[0:r, h, 0:P], pt[0:r, h, 0:r], start=True, stop=(i == 0))
                        if not last and i:
                            pe.matmul(NUM[:, h, 0:r], Cs[:, h // 2, 0:P], qa[:, h, 0:r], start=False, stop=True)
                        for b in range(NB if last else 0):
                            w = slice(NT * b, NT * (b + 1))
                            pe.matmul(NUM[:, h, w], Cb[:, 1 + b, h // 2, 0:P], qa[:, h, w], start=False, stop=(b == NB - 1))
                    for h in range(4):
                        mm = pe.matmul(DEN[:, h, 0:r], C["ones"][0:r, :], pt[0:r, h, 0:r], start=True, stop=(i == 0))
                        if not last and i:
                            mm = pe.matmul(DEN[:, h, 0:r], nbc[:, h // 2, :], qa[:, h, 0:r], start=False, stop=True)
                        for b in range(NB if last else 0):
                            w = slice(NT * b, NT * (b + 1))
                            mm = pe.matmul(DEN[:, h, w], nbs[:, b, h // 2, :], qa[:, h, w], start=False, stop=(b == NB - 1))
                    mm.then_inc(pe_.sem, pe_.mark(("ND", i)))
                    if not last:
                        need(dve_, ("kw", i))
                        for h in range(4):
                            bk = CU if h < 2 else TR
                            mm = pe.matmul(bk.rearrange("p h t -> p (h t)")[hp(h), 0:129], kw[0:r, h, :], vt[0:r, h, :], start=True, stop=True)
                        mm.then_inc(pe_.sem, pe_.mark(("CU", i)))
                    for b in range(NB if last else 0):
                        need(dve_, ("kwb", b))
                        if b >= 2:
                            need(dve_, ("Cb", b - 2, 3))
                        for h in range(4):
                            bk = ((CU, TR), (ST, RB))[b % 2][h // 2]
                            mm = pe.matmul(bk.rearrange("p h t -> p (h t)")[hp(h), 0:129], kwb[:, b % 2, h, :], vt[0:NS, h, :], start=True, stop=True)
                        mm.then_inc(pe_.sem, pe_.mark(("CUb", b)))

            @block.scalar
            def _(act):
                def need(st, name):
                    act.wait_ge(st.sem, st.at(name))
                for i in range(NC + 1):
                    r = token_rows(i)
                    need(pe_, ("RB", i))
                    if i:
                        need(pe_, ("CU", i - 1))
                    nc.scalar.activation(kt[0:r], TR.rearrange("p h t -> p (h t)")[0:r, 0:256].rearrange("p (h d) -> p h d", h=4), ACT.Copy) \
                        .then_inc(act_.sem, act_.mark(("kt", i)))
                    need(dve_, ("D", i))
                    for h in range(4):
                        ins = nc.scalar.activation(dt[0:r, h, 0:r], dt[0:r, h, 0:r], ACT.Exp, bias=GC[0:r, i, h:h + 1])
                    ins.then_inc(act_.sem, act_.mark(("dt", i)))
                    need(pe_, ("VT", i))
                    if i == 0:
                        need(dve_, ("ones_col"))
                    nc.scalar.activation(vt[0:r, :, 0:P], CU[0:r], ACT.Copy).then_inc(act_.sem, act_.mark(("vt", i)))
                    need(pe_, ("EB", i))
                    nc.scalar.activation(eb[:, :, 0:r], EB[:, :, 0:r], ACT.Copy).then_inc(act_.sem, act_.mark(("eb", i)))
                    need(pe_, ("ND", i))
                    nc.scalar.activation(den[:, :, 0:r], DEN[:, :, 0:r], ACT.Abs).then_inc(act_.sem, act_.mark(("absden", i)))

            @block.vector
            def _(dve):
                V = nc.vector

                def step(name, ins):
                    ins.then_inc(dve_.sem, dve_.mark(name))

                def need(st, name):
                    dve.wait_ge(st.sem, st.at(name))
                step("ones_col", V.memset(vt[:, :, P:P + 1], 1.0))
                step("qz_zero", V.memset(qz[:], 0.0))
                step("qa_zero", V.memset(qa[:], 0.0))
                need(dve_, "qa_zero")
                for i in range(NC + 1):
                    r = token_rows(i)
                    last = i == NC
                    if i:
                        need(pe_, ("AB", i - 1))
                    for x in range(2):
                        sl = slice(64 * x, 64 * x + 64)
                        step(("qz0", i) if x == 0 else ("qz", i), V.tensor_copy(qz[sl, x:4:2, 0:r], Z[sl, 0:2, cols(i)]))
                    mask = (C["maskS"] if last else C["maskP"])
                    need(pe_, ("RB", i))
                    if i:
                        need(pe_, ("ND", i - 1))
                        need(dve_, ("kw", i - 1))
                    step(("D", i), V.tensor_tensor(dt[0:r, :, 0:r], RB[0:r, :, 0:r],
                                                   mask[0:r, 0:r].rearrange("p (o t) -> p o t", o=1).broadcast_to([r, 4, r]), ALU.add))
                    need(pe_, ("AB", i))
                    step(("ab", i), V.tensor_copy(ab[:, :, 0:r], AB[:, :, 0:r]))
                    need(dve_, ("ab", i))
                    if last:
                        dve.wait_ge(s["ld"], 16 * 20)
                        step("nbs", V.tensor_copy(nbs[:].rearrange("p b y v -> p (b y) v"),
                                                    Cb[:, 1:, :, P:P + 1].rearrange("p b y o -> p (b y) o").broadcast_to([P, 2 * NB, P])))
                    elif i:
                        need(dve_, ("C", i - 1, 3))
                        step(("nbc", i), V.tensor_copy(nbc[:], Cs[:, :, P:P + 1].broadcast_to([P, 2, P])))
                    else:
                        step(("nbc", i), V.memset(nbc[:], 0.0))
                    for x in range(2):
                        sl = slice(64 * x, 64 * x + 64)
                        ins = V.tensor_tensor(qa[sl, x:4:2, 0:r], Z[sl, 0:2, cols(i)], ab[sl, x:4:2, 0:r], ALU.mult)
                        step(("qa0", i) if x == 0 else ("qa", i), ins)
                    need(act_, ("dt", i))
                    step(("pt", i), V.scalar_tensor_tensor(out=pt[0:r, :, 0:r], in0=ST[0:r, :, 0:r], scalar=0.125,
                                                           in1=dt[0:r, :, 0:r], op0=ALU.mult, op1=ALU.mult))
                    if not last:
                        need(act_, ("kt", i))
                        for h in range(4):
                            ins = V.tensor_scalar(kw[0:r, h, :], kt[0:r, h, :], dt[0:r, h, P - 1:P], 0.125, ALU.mult, ALU.mult)
                        step(("kw", i), ins)
                    if not last:
                        need(pe_, ("CU", i))
                    for h in range(4 if not last else 0):
                        bk = (CU if h < 2 else TR).rearrange("p h t -> p (h t)")
                        if i == 0:
                            ins = V.tensor_copy(Cs[hp(h), h // 2, :], bk[hp(h), 0:129])
                        else:
                            ins = V.scalar_tensor_tensor(out=Cs[hp(h), h // 2, :], in0=Cs[hp(h), h // 2, :],
                                                         scalar=ab[hp(h), h, P - 1:P], in1=bk[hp(h), 0:129], op0=ALU.mult, op1=ALU.add)
                        step(("C", i, h), ins)
                    need(act_, ("absden", i))
                    need(act_, ("eb", i))
                    step(("den", i), V.tensor_tensor(den[:, :, 0:r], den[:, :, 0:r], eb[:, :, 0:r], ALU.max))
                    need(dve_, ("den", i))
                    step(("rden", i), V.reciprocal(den[:, :, 0:r], den[:, :, 0:r]))
                    need(dve_, ("rden", i))
                    step(("h", i), V.tensor_tensor(Z[:, 4:8, cols(i)], NUM[:, :, 0:r], den[:, :, 0:r], ALU.mult))
                    def weights(b):
                        e = NT * b + NT - 1
                        if b >= 2:
                            need(pe_, ("CUb", b - 2))
                        for h in range(4):
                            ins = V.tensor_scalar(kwb[:, b % 2, h, :], kt[0:r, h, :], dt[0:r, h, e:e + 1], 0.125, ALU.mult, ALU.mult)
                        step(("kwb", b), ins)
                    if last:
                        need(act_, ("kt", i))
                        weights(0)
                    for b in range(NB if last else 0):
                        e = NT * b + NT - 1
                        if b + 1 < NB:
                            weights(b + 1)
                        need(pe_, ("CUb", b))
                        for h in range(4):
                            bk = ((CU, TR), (ST, RB))[b % 2][h // 2].rearrange("p h t -> p (h t)")
                            step(("Cb", b, h), V.scalar_tensor_tensor(
                                out=Cb[hp(h), 1 + b, h // 2, :], in0=Cb[hp(h), 1 + b, h // 2, :],
                                scalar=ab[hp(h), h, e:e + 1], in1=bk[hp(h), 0:129], op0=ALU.mult, op1=ALU.add))


def deltanet(pr, I, O, C, Z, GC, RT, arena, ps):
    nc = pr.nc
    with ExitStack() as c:
        def sb(n, shape):
            return arena(shape)
        S = sb("S", [P, 4, P])
        Sb = sb("Sb", [P, NB * 4, P])
        names = ("dt", "mt", "at", "mm", "x", "xt", "t1", "bv", "kb", "kd", "nwt", "vn", "qd", "eg", "kk", "mm2")
        T = {n: sb(n, [P, 4, P]) for n in names}
        kdb = sb("kdb", [NS, 2, 4, P])

        def b4(n):
            return bank(ps, n).rearrange("p (h t) -> p h t", h=4)
        KKT, QKT, GB, TK, TV, A1, A2, A3 = (b4(n) for n in range(8))
        L1, L2, L3 = (A1, KKT), (A2, QKT), (A3, GB)
        pair = (slice(0, 2), slice(2, 4))
        level_part = (T["mm"], T["mm2"])
        with pr.stage("delta", steps=["pe", "act", "dve", "pool"], sems=["ld", "st"]) as (block, s):
            pe_, act_, dve_, pool_ = s["pe"], s["act"], s["dve"], s["pool"]

            def cols(i):
                return slice(P * i, P * i + token_rows(i))

            def levels(i):
                return 7 if i < NC else 3

            @block.sync
            def _(sp):
                sp.dma_start(Sb[:], I["state_gdn_s"][0].rearrange("b h k v -> k (b h) v")).then_inc(s["ld"], 16)
                sp.wait_ge(dve_.sem, dve_.at(("S", NC - 1)))
                sp.dma_start(O["p_gdn_s"][0, 0].rearrange("h k v -> k h v"), S[:]).then_inc(s["st"], 16)
                sp.wait_ge(dve_.sem, dve_.at(("Sb", NB - 1)))
                sp.dma_start(O["s_gdn_s"][0].rearrange("b h k v -> k (b h) v"), Sb[:]).then_inc(s["st"], 16)
                sp.wait_ge(s["st"], 32)

            @block.tensor
            def _(pe):
                def need(st, name):
                    pe.wait_ge(st.sem, st.at(name))

                for i in range(NC + 1):
                    r = token_rows(i)
                    last = i == NC
                    cc = cols(i)
                    if i:
                        need(dve_, ("O", i - 1))
                        need(dve_, ("S", i - 1))
                    for h in range(4):
                        pe.matmul(KKT[0:r, h, 0:r], Z[:, 12 + h, cc], Z[:, 12 + h, cc], start=True, stop=True)
                        pe.matmul(QKT[0:r, h, 0:r], Z[:, 12 + h, cc], Z[:, 8 + h, cc], start=True, stop=True)
                        pe.matmul(GB[:, h, 0:r], C["sel"][:, 12 + h, :], RT[:, cc], start=True, stop=True)
                        pe.transpose(TK[0:r, h, :], Z[:, 12 + h, cc], C["ident"][:])
                        mm = pe.transpose(TV[0:r, h, :], Z[:, 16 + h, cc], C["ident"][:])
                    mm.then_inc(pe_.sem, pe_.mark(("in", i)))
                    for l in range(levels(i)):
                        need(pool_, ("mm", i, l))
                        if l == 0:
                            need(dve_, ("at", i))
                            need(act_, ("eg", i))
                        for g in (0, 1):
                            if l:
                                need(dve_, ("x", i, l - 1, g))
                            for h in (2 * g, 2 * g + 1):
                                mm = pe.matmul(L1[g][0:r, h, 0:r], level_part[l % 2][0:r, h, 0:r], T["x"][0:r, h, 0:r], start=True, stop=True)
                            mm.then_inc(pe_.sem, pe_.mark(("t1", i, l, g)))
                        for g in (0, 1):
                            need(dve_, ("t1", i, l, g))
                            for h in (2 * g, 2 * g + 1):
                                mm = pe.matmul(L2[g][0:r, h, 0:r], T["xt"][0:r, h, 0:r], T["t1"][0:r, h, 0:r], start=True, stop=True) \
                                    if l < levels(i) - 1 else None
                            if mm is not None:
                                mm.then_inc(pe_.sem, pe_.mark(("x", i, l, g)))
                            for h in (2 * g, 2 * g + 1):
                                mm = pe.matmul(L3[g][0:r, h, 0:r], T["t1"][0:r, h, 0:r], T["xt"][0:r, h, 0:r], start=True, stop=True)
                            mm.then_inc(pe_.sem, pe_.mark(("xt", i, l, g)))
                    need(dve_, ("xt", i, levels(i) - 1, 1))
                    need(act_, ("kb", i))
                    for h in range(4):
                        mm = pe.matmul(A1[:, h, 0:r], T["kb"][0:r, h, :], T["xt"][0:r, h, 0:r], start=True, stop=True)
                    mm.then_inc(pe_.sem, pe_.mark(("wt", i)))
                    need(act_, ("nwt", i))
                    need(act_, ("bv", i))
                    if last:
                        pe.wait_ge(s["ld"], 16)
                        for h in range(4):
                            mm = pe.matmul(A2[:, h, 0:r], T["bv"][0:r, h, :], T["xt"][0:r, h, 0:r], start=True, stop=False)
                            for b in range(NB):
                                w = slice(NT * b, NT * (b + 1))
                                mm = pe.matmul(A2[:, h, w], Sb[:, 4 * b + h, :], T["nwt"][:, h, w], start=False, stop=(b == NB - 1))
                        mm.then_inc(pe_.sem, pe_.mark(("vnT", i)))
                        need(act_, ("vnT", i))
                        for h in range(4):
                            mm = pe.transpose(A1[0:r, h, :], T["mm"][:, h, 0:r], C["ident"][:])
                        mm.then_inc(pe_.sem, pe_.mark(("vn", i)))
                    else:
                        for h in range(4):
                            mm = pe.matmul(A2[0:r, h, :], T["xt"][0:r, h, 0:r], T["bv"][0:r, h, :], start=True, stop=(i == 0))
                            if i:
                                mm = pe.matmul(A2[0:r, h, :], T["nwt"][:, h, 0:r], S[:, h, :], start=False, stop=True)
                        mm.then_inc(pe_.sem, pe_.mark(("vn", i)))
                    need(act_, ("vn", i))
                    need(dve_, ("qd", i))
                    need(dve_, ("at", i))
                    for h in range(4):
                        mm = pe.matmul(A3[:, h, 0:r], T["vn"][0:r, h, :], T["at"][0:r, h, 0:r], start=True, stop=(i == 0))
                        if i and not last:
                            mm = pe.matmul(A3[:, h, 0:r], S[:, h, :], T["qd"][:, h, 0:r], start=False, stop=True)
                        for b in range(NB if last else 0):
                            w = slice(NT * b, NT * (b + 1))
                            mm = pe.matmul(A3[:, h, w], Sb[:, 4 * b + h, :], T["qd"][:, h, w], start=False, stop=(b == NB - 1))
                    mm.then_inc(pe_.sem, pe_.mark(("O", i)))
                    if not last:
                        need(dve_, ("kd", i))
                        for h in range(4):
                            mm = pe.matmul(A1[:, h, :], T["kd"][0:r, h, :], T["vn"][0:r, h, :], start=True, stop=True)
                        mm.then_inc(pe_.sem, pe_.mark(("SU", i)))
                    for b in range(NB if last else 0):
                        need(dve_, ("kdb", b))
                        if b >= 2:
                            need(dve_, ("Sb", b - 2))
                        for h in range(4):
                            mm = pe.matmul((A2, A1)[b % 2][:, h, :], kdb[:, b % 2, h, :], T["vn"][0:r, h, :], start=True, stop=True)
                        mm.then_inc(pe_.sem, pe_.mark(("SUb", b)))

            @block.scalar
            def _(act):
                A = nc.scalar

                def need(st, name):
                    act.wait_ge(st.sem, st.at(name))

                def step(name, ins):
                    ins.then_inc(act_.sem, act_.mark(name))
                for i in range(NC + 1):
                    r = token_rows(i)
                    need(dve_, ("D", i))
                    for h in range(4):
                        ins = A.activation(T["dt"][0:r, h, 0:r], T["dt"][0:r, h, 0:r], ACT.Exp, bias=GC[0:r, i, 32 + h:33 + h])
                    step(("dt", i), ins)
                    step(("eg", i), A.activation(T["eg"][:, :, 0:r], GB[:, :, 0:r], ACT.Exp))
                    step(("kk", i), A.activation(T["kk"][0:r], TK[0:r], ACT.Copy))
                    for h in range(4):
                        ins = A.activation(T["bv"][0:r, h, :], TV[0:r, h, :], ACT.Copy, scale=GC[0:r, i, 64 + h:65 + h])
                    step(("bv", i), ins)
                    for h in range(4):
                        ins = A.activation(T["kb"][0:r, h, :], TK[0:r, h, :], ACT.Copy, scale=GC[0:r, i, 96 + h:97 + h])
                    step(("kb", i), ins)
                    need(pe_, ("wt", i))
                    step(("nwt", i), A.activation(T["nwt"][:, :, 0:r], A1[:, :, 0:r], ACT.Copy, scale=-1.0))
                    if i == NC:
                        need(pe_, ("vnT", i))
                        step(("vnT", i), A.activation(T["mm"][:, :, 0:r], A2[:, :, 0:r], ACT.Copy))
                        need(pe_, ("vn", i))
                        step(("vn", i), A.activation(T["vn"][0:r], A1[0:r], ACT.Copy))
                    else:
                        need(pe_, ("vn", i))
                        step(("vn", i), A.activation(T["vn"][0:r], A2[0:r], ACT.Copy))

            @block.gpsimd
            def _(pool):
                for i in range(NC + 1):
                    r = token_rows(i)
                    pool.wait_ge(dve_.sem, dve_.at(("mt", i)))
                    for l in range(levels(i)):
                        if l >= 2:
                            pool.wait_ge(pe_.sem, pe_.at(("t1", i, l - 2, 1)))
                        mask = C["level"][0:r, l, 0:r].rearrange("p (o t) -> p o t", o=1).broadcast_to([r, 4, r])
                        nc.gpsimd.tensor_tensor(level_part[l % 2][0:r, :, 0:r], T["mt"][0:r, :, 0:r], mask, ALU.mult) \
                            .then_inc(pool_.sem, pool_.mark(("mm", i, l)))

            @block.vector
            def _(dve):
                V = nc.vector

                def step(name, ins):
                    ins.then_inc(dve_.sem, dve_.mark(name))

                def need(st, name):
                    dve.wait_ge(st.sem, st.at(name))

                def over_heads(m, r):
                    return m.rearrange("p (o t) -> p o t", o=1).broadcast_to([r, 4, r])
                for i in range(NC + 1):
                    r = token_rows(i)
                    last = i == NC
                    need(pe_, ("in", i))
                    if i:
                        need(pe_, ("SU", i - 1))
                    mask = C["maskS"] if last else C["maskP"]
                    step(("D", i), V.tensor_tensor(T["dt"][0:r, :, 0:r], GB[0:r, :, 0:r], over_heads(mask[0:r, 0:r], r), ALU.add))
                    idn = over_heads(C["ident"][0:r, 0:r], r)
                    step(("x0", i), V.tensor_copy(T["x"][0:r, :, 0:r], idn))
                    step(("xt0", i), V.tensor_copy(T["xt"][0:r, :, 0:r], idn))
                    need(act_, ("dt", i))
                    step(("mt", i), V.tensor_tensor(T["mt"][0:r, :, 0:r], KKT[0:r, :, 0:r], T["dt"][0:r, :, 0:r], ALU.mult))
                    step(("at", i), V.tensor_tensor(T["at"][0:r, :, 0:r], QKT[0:r, :, 0:r], T["dt"][0:r, :, 0:r], ALU.mult))
                    for l in range(levels(i)):
                        beta = GC[0:r, i, 64:68].rearrange("p (h o) -> p h o", o=1).broadcast_to([r, 4, r])
                        for g in (0, 1):
                            need(pe_, ("t1", i, l, g))
                            step(("t1", i, l, g), V.tensor_tensor(T["t1"][0:r, pair[g], 0:r], L1[g][0:r, pair[g], 0:r], beta[:, pair[g]], ALU.mult))
                        if l == 0:
                            need(act_, ("eg", i))
                            step(("qd", i), V.tensor_tensor(T["qd"][:, :, 0:r], Z[:, 8:12, cols(i)], T["eg"][:, :, 0:r], ALU.mult))
                            if not last:
                                need(act_, ("kk", i))
                                step(("kd", i), V.tensor_tensor(T["kd"][0:r], T["kk"][0:r],
                                                               T["dt"][0:r, :, P - 1:P].broadcast_to([r, 4, P]), ALU.mult))
                        for g in (0, 1):
                            need(pe_, ("xt", i, l, g))
                            step(("xt", i, l, g), V.tensor_tensor(T["xt"][0:r, pair[g], 0:r], T["xt"][0:r, pair[g], 0:r],
                                                                  L3[g][0:r, pair[g], 0:r], ALU.subtract))
                            if l < levels(i) - 1:
                                step(("x", i, l, g), V.tensor_tensor(T["x"][0:r, pair[g], 0:r], T["x"][0:r, pair[g], 0:r],
                                                                     L2[g][0:r, pair[g], 0:r], ALU.subtract))
                    need(pe_, ("O", i))
                    step(("O", i), V.tensor_copy(Z[:, 16:20, cols(i)], A3[:, :, 0:r]))
                    if not last:
                        need(pe_, ("SU", i))
                        if i == 0:
                            step(("S", i), V.tensor_copy(S[:], A1))
                        else:
                            for h in range(4):
                                ins = V.scalar_tensor_tensor(out=S[:, h, :], in0=S[:, h, :], scalar=T["eg"][:, h, P - 1:P],
                                                             in1=A1[:, h, :], op0=ALU.mult, op1=ALU.add)
                            step(("S", i), ins)
                    def weights(b):
                        e = NT * b + NT - 1
                        if b >= 2:
                            need(pe_, ("SUb", b - 2))
                        step(("kdb", b), V.tensor_tensor(kdb[:, b % 2], T["kk"][0:r],
                                                         T["dt"][0:r, :, e:e + 1].broadcast_to([r, 4, P]), ALU.mult))
                    if last:
                        weights(0)
                    for b in range(NB if last else 0):
                        e = NT * b + NT - 1
                        if b + 1 < NB:
                            weights(b + 1)
                        need(pe_, ("SUb", b))
                        for h in range(4):
                            ins = V.scalar_tensor_tensor(out=Sb[:, 4 * b + h, :], in0=Sb[:, 4 * b + h, :], scalar=T["eg"][:, h, e:e + 1],
                                                         in1=(A2, A1)[b % 2][:, h, :], op0=ALU.mult, op1=ALU.add)
                        step(("Sb", b), ins)


def tile_norms(pr, name, I, Z, tiles, which, gammas, beside, arena, ps):
    nc = pr.nc
    sumsel, rowsel, eps = arena([P, 8, 8]), arena([8, 8, P]), arena([8, 1])
    gam, sq, rows = arena([P, 5]), arena([P, 2, TP]), arena([8, TP])
    with pr.stage(name, steps=["pe", "act", "dve"], sems=["ld", "beside"]) as (block, s):
        pe_, act_, dve_ = s["pe"], s["act"], s["dve"]
        sets = [ps[:, 1536 * k:1536 * (k + 1)].rearrange("p (c n) -> p c n", n=512)[:, :, 0:CH] for k in (0, 1)]

        @block.sync
        def _(sp):
            if beside:
                sp.dma_start(*beside).then_inc(s["beside"], 16)
            sp.dma_start(sumsel, I["c_sumsel"][:, which]).then_inc(s["ld"], 16)
            sp.dma_start(rowsel, I["c_rowsel"]).then_inc(s["ld"], 16)
            sp.dma_start(eps, I["c_epsrow"][which]).then_inc(s["ld"], 16)
            if gammas:
                sp.dma_start(gam[:, 0:4], I["mi_norm"][0].rearrange("(h v) -> v h", v=P), allow_slow_non_contiguous=True).then_inc(s["ld"], 16)
                sp.dma_start(gam[:, 4:5], I["gd_norm"].rearrange("a v -> v a")).then_inc(s["ld"], 16)
            if beside:
                sp.wait_ge(s["beside"], 16)

        landed = 80 if gammas else 48

        @block.scalar
        def _(act):
            for j in range(8):
                if j >= 2:
                    act.wait_ge(pe_.sem, pe_.at(("sum", j - 2)))
                nc.scalar.activation(sq[:, j % 2, :], Z[:, tiles[j], :], ACT.Square).then_inc(act_.sem, act_.mark(("sq", j)))
            act.wait_ge(dve_.sem, dve_.at("mean"))
            nc.scalar.activation(rows, rows, ACT.Sqrt).then_inc(act_.sem, act_.mark("root"))

        @block.tensor
        def _(pe):
            pe.wait_ge(s["ld"], landed)
            for j in range(8):
                pe.wait_ge(act_.sem, act_.at(("sq", j)))
                for c in range(3):
                    mm = pe.matmul(sets[0][0:8, c, :], sumsel[:, j, :], sq[:, j % 2, CH * c:CH * (c + 1)], start=(j == 0), stop=(j == 7))
                mm.then_inc(pe_.sem, pe_.mark(("sum", j)))
            pe.wait_ge(dve_.sem, dve_.at("rec"))
            for j in range(8):
                if j >= 2:
                    pe.wait_ge(dve_.sem, dve_.at(("n", j - 2)))
                for c in range(3):
                    mm = pe.matmul(sets[j % 2][:, c, :], rowsel[:, j, :], rows[:, CH * c:CH * (c + 1)], start=True, stop=True)
                mm.then_inc(pe_.sem, pe_.mark(("spread", j)))

        @block.vector
        def _(dve):
            dve.wait_ge(pe_.sem, pe_.at(("sum", 7)))
            nc.vector.tensor_scalar(v3(rows), sets[0][0:8], eps, None, ALU.add).then_inc(dve_.sem, dve_.mark("mean"))
            dve.wait_ge(act_.sem, act_.at("root"))
            nc.vector.reciprocal(rows, rows).then_inc(dve_.sem, dve_.mark("rec"))
            for j in range(8):
                dve.wait_ge(pe_.sem, pe_.at(("spread", j)))
                z = v3(Z[:, tiles[j], :])
                if gammas:
                    g = gam[:, min(j, 4):min(j, 4) + 1]
                    op = nc.vector.scalar_tensor_tensor(out=z, in0=z, scalar=g, in1=sets[j % 2], op0=ALU.mult, op1=ALU.mult)
                else:
                    op = nc.vector.tensor_tensor(z, z, sets[j % 2], ALU.mult)
                op.then_inc(dve_.sem, dve_.mark(("n", j)))


def mlp(pr, I, layer, xT, hn, u, W, ps):
    nc = pr.nc
    wu, wd = I["w_up"][layer], I["w_down"][layer]
    tiles = []
    for n in range(8):
        def relu(e, i, acc, n=n):
            return e.activation(v3(u[1][:, n, :]), acc, ACT.Relu)

        def square(e, i, acc, n=n):
            return e.tensor_tensor(v3(u[1][:, n, :]), v3(u[1][:, n, :]), acc, ALU.mult)

        def high(e, i, acc, n=n):
            return e.activation(r32(u[0][:, n, :]), u[1][:, n, :], ACT.Copy)

        def low(e, i, acc, n=n):
            return e.tensor_tensor(r32(u[1][:, n, :]), u[1][:, n, :], r32(u[0][:, n, :]), ALU.subtract)
        tiles.append(dict(w=lambda i, n=n: wu[:, bass.ds(i * DM + P * n, P)], x=hn,
                          steps=[("act", relu), ("dve", square), ("act", high), ("dve", low)]))
    for n in range(8):
        def add(e, i, acc, n=n):
            return e.tensor_tensor(v3(xT[:, n, :]), v3(xT[:, n, :]), acc, ALU.add)
        tiles.append(dict(w=lambda i, n=n: wd[bass.ds(i * DM, DM), P * n:P * (n + 1)], x=u, steps=[("dve", add)],
                          need=8 if n == 0 else None))
    stream(pr, f"mlp{layer}", ps, W, DFF // DM, tiles)


def residual_product(pr, name, w, mix, xT, W, ps):
    tiles = []
    for n in range(8):
        def add(e, i, acc, n=n):
            return e.tensor_tensor(v3(xT[:, n, :]), v3(xT[:, n, :]), acc, ALU.add)
        tiles.append(dict(w=lambda i, n=n: w[:, P * n:P * (n + 1)], x=mix, steps=[("dve", add)]))
    stream(pr, name, ps, W, 1, tiles)


class Tiles:

    def __init__(self, z, which):
        self.z, self.which = z, which

    def __getitem__(self, key):
        p, k, t = key
        return self.z[p, self.which[k], t]


def layer0(pr, I, O, Cc, xT, hn, wslots, ps):
    nc = pr.nc
    flat = xT[:].rearrange("p k t -> p (k t)")
    which = [4, 5, 6, 7, 16, 17, 18, 19]
    half = [wslots[:, 0:2], wslots[:, 2:4]]
    w = I["w_in_even"][0]
    saved = nc.dram_tensor("x_saved", [P, KT * TP], F32).ap()
    saved_low = nc.dram_tensor("low_saved", [P, KT * TP], F32).ap()
    with ExitStack() as c:
        Z = two_ways(nc, c, "Z", [P, 20, TP])
        zg = c.enter_context(nc.sbuf_tensor("zg", [P, TP], F32))
        spare = c.enter_context(nc.sbuf_tensor("spare", [P, TP], F32))
        GC = c.enter_context(nc.sbuf_tensor("GC", [P, NC + 1, P], F32))
        RT = c.enter_context(nc.sbuf_tensor("RT", [P, TP], F32))
        with ExitStack() as c2:
            W = {"raw": c2.enter_context(nc.sbuf_tensor("raw0", [P, 2, KT, P], F32)), "half": half, "ones": Cc["ones"]}
            rmsnorm(pr, "norm0", xT, hn, zg[:], GC[:], I["norm_mix"][0], Cc["ident"], Cc["ones"], ps, low=xT, save=saved)
            for name, c0, t0, panels in (("in0a", 0, 0, 2), ("in0b", 1544, 8, 3)):
                tiles = []
                for n in range(4):
                    def out(e, i, acc, n=n, t0=t0):
                        dst = Z[:, bass.ds(4 * i + (t0 + n), 1), :].rearrange("p o (c n) -> p (o c) n", n=CH)
                        return e.tensor_copy(dst, acc) if n % 2 else e.activation(dst, acc, ACT.Copy)
                    tiles.append(dict(w=lambda i, n=n, c0=c0: w[:, bass.ds(i * 512 + (c0 + P * n), P)], x=(hn, xT),
                                      steps=[("dve" if n % 2 else "act", out)]))
                stream(pr, name, ps, W, panels, tiles)
            gate_product(pr, I, hn, xT, zg, W, saved_low, ps)

        def room():
            return Arena(flat, wslots[:].rearrange("p a k m -> p (a k m)"), spare[:])
        with ExitStack() as c2:
            C = dict(Cc)
            names = ["maskP", "maskS", "level", "sel", "keep"]
            for n in names:
                C[n] = c2.enter_context(nc.sbuf_tensor("sb_" + n, list(I["c_" + n].shape), F32))
            load_constants(pr, I, names, C, "const0")
            even_gates(pr, I, O, C, zg, GC, RT, room(), ps)
            conv(pr, I, O, C, Z, room(), ps)
            tile_norms(pr, "unit_qk", I, Z, list(range(8, 16)), 0, False, None, room(), ps)
            mlstm(pr, I, O, C, Z, GC, RT, room(), ps)
            deltanet(pr, I, O, C, Z, GC, RT, room(), ps)
        tile_norms(pr, "headnorm", I, Z, which, 1, True, (r32(flat).bitcast(F32), saved_low),
                   Arena(wslots[:].rearrange("p a k m -> p (a k m)"), spare[:], RT[:]), ps)
        with ExitStack() as c2:
            W = {"raw": c2.enter_context(nc.sbuf_tensor("raw1", [P, 2, KT, P], F32)), "half": half, "ones": Cc["ones"]}
            gt = [zg[:], spare[:]]
            tiles = []
            for n in range(8):
                def gate(e, i, acc, n=n):
                    return e.activation(v3(gt[n % 2]), acc, ACT.Sigmoid if n < 4 else ACT.Silu)

                def gated(e, i, acc, n=n):
                    z = Z[:, which[n], :]
                    return e.tensor_tensor(z, z, gt[n % 2], ALU.mult)
                c0 = (1024 if n < 4 else 3080 - 512) + P * n
                tiles.append(dict(w=lambda i, c0=c0: w[:, c0:c0 + P], x=(hn, xT), steps=[("act", gate), ("dve", gated)]))
            stream(pr, "outgates", ps, W, 1, tiles)
            split(pr, "mix_halves", [(Z[:, k, :], hn[:, n, :], Z[:, k, :]) for n, k in enumerate(which)], copy=(flat, saved))
            residual_product(pr, "wout0", I["w_out_even"][0], (hn, Tiles(Z, which)), xT, W, ps)


KV0, WIN0, FQ0, FK0, FF0 = 512, 1024, 1304, 1816, 2840


def token_major(pr, I, O, W, hn, wslots, wide, stage_buf, gates, ps):
    nc = pr.nc
    w = I["w_in_odd"][0]
    panels = [(KV0, 512), (WIN0, 280), (FK0, 512), (FK0 + 512, 512)]
    flat = wslots[:].rearrange("p a k m -> p (a k m)").rearrange("p (k m) -> p k m", k=KT)
    wb = [flat, wide[:]]
    units = [(n, i) for n in range(4) for i in range(NC + 1)]
    NSL = 4
    with pr.stage("tokmajor", steps=["pe", "act", "dve"], sems=["w0", "w1", "gs", "hist"] + [f"out{k}" for k in range(NSL)]) as (block, s):
        pe_, act_, dve_ = s["pe"], s["act"], s["dve"]
        eng = lambda u: act_ if u % 2 == 0 else dve_
        stores = [0] * NSL
        sent = {}
        for u, (n, i) in enumerate(units):
            stores[u % NSL] += 2 if n == 1 and i in (6, 7, 8) else 1
            sent[u] = stores[u % NSL]

        @block.sync
        def _(sp):
            sp.dma_start(O["s_nsa_win"][0, :, 0:PAST - NT].rearrange("b j a g d -> b j (a g d)"),
                         I["state_nsa_win"][0, :, NT:PAST].rearrange("b j a g d -> b j (a g d)")).then_inc(s["hist"], 16)
            for n in range(2):
                c0, m = panels[n]
                sp.dma_start(wb[n % 2][:, :, 0:m], w[:, c0:c0 + m].rearrange("(k p) m -> p k m", p=P)).then_inc(s[f"w{n % 2}"], 16)
            for u, (n, i) in enumerate(units):
                if n >= 1 and i == 0 and n + 1 < 4:
                    c0, m = panels[n + 1]
                    sp.wait_ge(pe_.sem, pe_.at((n - 1, NC)))
                    sp.dma_start(wb[(n + 1) % 2][:, :, 0:m], w[:, c0:c0 + m].rearrange("(k p) m -> p k m", p=P)) \
                        .then_inc(s[f"w{(n + 1) % 2}"], 16)
                e = eng(u)
                sp.wait_ge(e.sem, e.at(("row", u)))
                r = token_rows(i)
                src = stage_buf[0:r, u % NSL, 0:(256 if n == 1 else 512)]
                so = s[f"out{u % NSL}"]
                rows = slice(P * i, P * i + r)
                if n == 0:
                    dst = O["p_nsa_kv"][0, 0, rows].rearrange("t a g d -> t (a g d)") if i < NC else \
                        O["s_nsa_kv"][0].rearrange("b t a g d -> (b t) (a g d)")
                elif n == 1:
                    dst = W["win"][rows]
                else:
                    dst = O["p_fox_kv"][0, 0, rows, n - 2].rearrange("t h d -> t (h d)") if i < NC else \
                        O["s_fox_kv"][0, :, :, n - 2].rearrange("b t h d -> (b t) (h d)")
                sp.dma_start(dst, src).then_inc(so, 16)
                if n == 1 and i in (6, 7):
                    sp.dma_start(O["p_nsa_win"][0, 0, P * (i - 6):P * (i - 5)].rearrange("j a g d -> j (a g d)"), src).then_inc(so, 16)
                if n == 1 and i == NC:
                    sp.dma_start(O["s_nsa_win"][0, :, PAST - NT:PAST].rearrange("b j a g d -> b j (a g d)"), src).then_inc(so, 16)
            sp.wait_ge(dve_.sem, dve_.at("gates_done"))
            sp.dma_start(W["gates"], gates[0:NS, NC, :]).then_inc(s["gs"], 16)
            sp.wait_ge(s["gs"], 16)
            sp.wait_ge(s["hist"], 16)
            for k in range(NSL):
                sp.wait_ge(s[f"out{k}"], 16 * stores[k])

        @block.tensor
        def _(pe):
            for u, (n, i) in enumerate(units):
                r, m = token_rows(i), panels[n][1]
                if i == 0:
                    pe.wait_ge(s[f"w{n % 2}"], 16 * (n // 2 + 1))
                if u >= 4:
                    e = eng(u - 4)
                    pe.wait_ge(e.sem, e.at(("read", u - 4)))
                for k in range(KT):
                    mm = pe.matmul(bank(ps, u % 4)[0:r, 0:m], hn[:, k, P * i:P * i + r], wb[n % 2][:, k, 0:m],
                                   start=(k == 0), stop=(k == KT - 1))
                mm.then_inc(pe_.sem, pe_.mark((n, i)))

        def half(e, st, par):
            for u, (n, i) in enumerate(units):
                if u % 2 != par:
                    continue
                r, m = token_rows(i), 256 if n == 1 else 512
                e.wait_ge(pe_.sem, pe_.at((n, i)))
                if u >= NSL:
                    e.wait_ge(s[f"out{u % NSL}"], 16 * sent[u - NSL])
                src = bank(ps, u % 4)[0:r]
                dst = stage_buf[0:r, u % NSL, 0:m]
                op = nc.vector.tensor_copy(dst, src[:, 0:m]) if par else nc.scalar.activation(dst, src[:, 0:m], ACT.Copy)
                op.then_inc(st.sem, st.mark(("row", u)))
                if n == 1:
                    dst, g = gates[0:r, i, :], src[:, 256:280]
                    op = nc.vector.tensor_copy(dst, g) if par else nc.scalar.activation(dst, g, ACT.Copy)
                    op.then_inc(st.sem, st.mark(("read", u)))
                else:
                    st.seen[("read", u)] = st.count

        @block.scalar
        def _(act):
            half(act, act_, 0)
            act.wait_ge(dve_.sem, dve_.at(("read", 2 * NC + 1)))
            act.wait_ge(act_.sem, act_.at(("read", 2 * NC)))
            nc.scalar.activation(gates[:], gates[:], ACT.Sigmoid).then_inc(act_.sem, act_.mark("gates"))

        @block.vector
        def _(dve):
            nc.vector.memset(gates[:, NC, :], 0.0).then_inc(dve_.sem, dve_.mark("gate_zero"))
            dve.wait_ge(dve_.sem, dve_.at("gate_zero"))
            half(dve, dve_, 1)
            dve.wait_ge(act_.sem, act_.at("gates"))
            nc.vector.tensor_scalar(gates[:, 0, 0:24:3], gates[:, 0, 0:24:3], W["rowvalid"][:, 0:1], None, ALU.mult) \
                .then_inc(dve_.sem, dve_.mark("gates_done"))


def fox_rows(pr, I, O, C, hn, F, FS, gS, W, arena, ps):
    nc = pr.nc
    wf, bf = arena([P, KT, 8]), arena([8, 1])
    z, e, lf = arena([8, TP]), arena([8, TP]), arena([8, TP])
    LT = arena([P, NC + 1, 8])
    L = arena([P, 2, NB, 8])
    FN = arena([NS, TK])
    with pr.stage("foxrows", steps=["pe", "act", "dve"], sems=["ld", "pages", "st", "new", "gs"]) as (block, s):
        pe_, act_, dve_ = s["pe"], s["act"], s["dve"]
        acc = ps[:, 0:1536].rearrange("p (c n) -> p c n", n=512)[0:8, :, 0:CH]

        @block.sync
        def _(sp):
            sp.dma_start(wf, I["w_in_odd"][0, :, FF0:FF0 + 8].rearrange("(k p) m -> p k m", p=P),
                         allow_slow_non_contiguous=True).then_inc(s["ld"], 16)
            sp.dma_start(bf, I["fox_b_f"].rearrange("a h -> h a")).then_inc(s["ld"], 16)
            for b in range(NB):
                for g in range(2):
                    page = sp.value_load(W["pages"][0:1, 2 * b + g:2 * b + g + 1], min_val=0, max_val=NPOOL - 1)
                    sp.dma_start(L[:, g, b, :], I["cache_fox_logf"][0, bass.ds(page, 1)].rearrange("o t h -> t (o h)")) \
                        .then_inc(s["pages"], 16)
            for h in range(H):
                sp.dma_start(gS[NT * h:NT * (h + 1)], W["gates"].rearrange("(b t) (h c) -> h t b c", t=NT, c=3)[h],
                             allow_slow_non_contiguous=True).then_inc(s["gs"], 16)
            sp.wait_ge(dve_.sem, dve_.at(("LT", NC)))
            sp.dma_start(O["p_fox_logf"][0, 0].rearrange("(i t) h -> t i h", t=P), LT[:, 0:NC, :]).then_inc(s["st"], 16)
            sp.dma_start(O["s_fox_logf"][0].rearrange("b t h -> (b t) h"), LT[0:NS, NC, :]).then_inc(s["st"], 16)
            sp.wait_ge(s["st"], 32)
            for b in range(NB):
                sp.dma_start(FN[NT * b:NT * (b + 1), PAST:TK], O["s_fox_logf"][0, b].rearrange("t h -> h t"),
                             allow_slow_non_contiguous=True).then_inc(s["new"], 16)
            sp.wait_ge(s["gs"], 16 * H)

        @block.tensor
        def _(pe):
            pe.wait_ge(s["ld"], 32)
            for k in range(KT):
                for j in range(3):
                    mm = pe.matmul(acc[:, j, :], wf[:, k, :], hn[:, k, CH * j:CH * (j + 1)], start=(k == 0), stop=(k == KT - 1))
            mm.then_inc(pe_.sem, pe_.mark("z"))
            pe.wait_ge(s["pages"], 16 * 2 * NB)
            for g in range(2):
                t = pe.transpose(bank(ps, 4)[0:NS, P * g:P * (g + 1)], L[:, g].rearrange("p b h -> p (b h)"), C["ident"][:])
            t.then_inc(pe_.sem, pe_.mark("past"))
            pe.wait_ge(dve_.sem, dve_.at("lf"))
            for i in range(NC + 1):
                r = token_rows(i)
                pe.transpose(bank(ps, 5)[0:r, 8 * i:8 * i + 8], lf[:, P * i:P * i + r], C["ident"][0:8, 0:8]) \
                    .then_inc(pe_.sem, pe_.mark(("LT", i)))

        @block.scalar
        def _(act):
            act.wait_ge(dve_.sem, dve_.at("z"))
            nc.scalar.activation(e, z, ACT.Abs).then_inc(act_.sem, act_.mark("abs"))
            act.wait_ge(act_.sem, act_.at("abs"))
            nc.scalar.activation(e, e, ACT.Exp, scale=-1.0).then_inc(act_.sem, act_.mark("exp"))
            act.wait_ge(act_.sem, act_.at("exp"))
            nc.scalar.activation(e, e, ACT.Ln, bias=1.0).then_inc(act_.sem, act_.mark("l1"))

        @block.vector
        def _(dve):
            V = nc.vector

            def step(name, ins):
                ins.then_inc(dve_.sem, dve_.mark(name))

            def need(name):
                dve.wait_ge(dve_.sem, dve_.at(name))
            dve.wait_ge(pe_.sem, pe_.at("z"))
            step("z", V.tensor_scalar(v3(z), acc, bf, None, ALU.add))
            dve.wait_ge(act_.sem, act_.at("l1"))
            step("lf", V.scalar_tensor_tensor(out=lf, in0=z, scalar=0.0, in1=e, op0=ALU.min, op1=ALU.subtract))
            need("lf")
            step("ones", V.memset(z[:, 0:NPROMPT], 1.0))
            need("ones")
            step("F0", V.memset(F[:], 0.0))
            need("F0")
            step("F", V.tensor_tensor_scan(F[0:8, :], z[:, 0:NPROMPT], lf[:, 0:NPROMPT], 0.0, ALU.mult, ALU.add))
            need("F")
            step("F2", V.tensor_copy(F[64:72, :], F[0:8, :]))
            for i in range(NC + 1):
                r = token_rows(i)
                dve.wait_ge(pe_.sem, pe_.at(("LT", NC)))
                step(("LT", i), V.tensor_copy(LT[0:r, i, :], bank(ps, 5)[0:r, 8 * i:8 * i + 8]))
            dve.wait_ge(pe_.sem, pe_.at("past"))
            step("past", V.tensor_copy(FN[:, 0:PAST], bank(ps, 4)[0:NS, 0:PAST]))
            step("one2", V.memset(W["one"][0:NS, :], 1.0))
            need("one2")
            dve.wait_ge(s["new"], 16 * NB)
            step("FS", V.tensor_tensor_scan(FS[:], W["one"][0:NS, :], FN, 0.0, ALU.mult, ALU.add))


def bias_tables(pr, I, B, Bc, Bs, Bcs, relx, oh, rev, arena, ps):
    nc = pr.nc
    turn, rows, windows = arena([P, P]), arena([H, 3 * P]), arena([P, H, 256])
    byd = nc.dram_tensor("bias_by_distance", [H, 3 * P], F32).ap()
    with pr.stage("bias", steps=["pe", "act", "dve"], sems=["ld", "rows", "byd", "windows"]) as (block, s):
        pe_, act_, dve_ = s["pe"], s["act"], s["dve"]

        @block.sync
        def _(sp):
            sp.dma_start(relx[0:32, :], I["rel_bias"]).then_inc(s["ld"], 16)
            sp.dma_start(oh[:], I["c_onehot"]).then_inc(s["ld"], 16)
            sp.dma_start(rev[:], I["c_onehot_rev"]).then_inc(s["ld"], 16)
            sp.dma_start(turn, I["c_turnover"]).then_inc(s["ld"], 16)
            sp.wait_ge(dve_.sem, dve_.at("byd"))
            sp.dma_start(byd, rows).then_inc(s["byd"], 16)
            sp.wait_ge(s["byd"], 16)
            sp.dma_start(windows, bass.AP(tensor=byd.tensor, offset=0, ap=[[1, P], [3 * P, H], [1, 256]])).then_inc(s["windows"], 16)
            sp.wait_ge(dve_.sem, dve_.at("B3"))
            for h in range(H):
                sp.dma_start(Bs[NT * h:NT * (h + 1), :], B[0:NT, h, 0:P + NT]).then_inc(s["rows"], 16)
                sp.dma_start(Bcs[NT * h:NT * (h + 1), :], Bc[0:NT, h, 0:8]).then_inc(s["rows"], 16)
            sp.wait_ge(s["rows"], 16 * 2 * H)

        @block.tensor
        def _(pe):
            pe.wait_ge(s["ld"], 64)
            pe.wait_ge(dve_.sem, dve_.at("neg"))
            pe.matmul(bank(ps, 5)[0:H, 0:3 * P], relx[:], rev[:], start=True, stop=True).then_inc(pe_.sem, pe_.mark("byd"))
            for n in range(16):
                c0 = 97 - 16 * (n - 9)
                mm = pe.matmul(bank(ps, 4)[:, 8 * n:8 * n + 8], oh[:, c0:c0 + P], relx[:], start=True, stop=True)
            mm.then_inc(pe_.sem, pe_.mark("c"))
            pe.wait_ge(s["windows"], 16)
            for q in range(4):
                pe.matmul(bank(ps, q), turn, windows[:, 2 * q:2 * q + 2, :].rearrange("p h n -> p (h n)"), start=True, stop=True) \
                    .then_inc(pe_.sem, pe_.mark(q))

        @block.vector
        def _(dve):
            nc.vector.memset(relx[32:33, :], NEG).then_inc(dve_.sem, dve_.mark("neg"))
            dve.wait_ge(pe_.sem, pe_.at("byd"))
            nc.vector.tensor_copy(rows, bank(ps, 5)[0:H, 0:3 * P]).then_inc(dve_.sem, dve_.mark("byd"))
            dve.wait_ge(pe_.sem, pe_.at("c"))
            nc.vector.tensor_copy(Bc[:], bank(ps, 4)[:, 0:P].rearrange("p (n h) -> p h n", h=8)).then_inc(dve_.sem, dve_.mark("Bc"))
            for q in range(4):
                dve.wait_ge(pe_.sem, pe_.at(q))
                nc.vector.tensor_copy(B[:, 2 * q:2 * q + 2, :], bank(ps, q).rearrange("p (h j) -> p h j", h=2)) \
                    .then_inc(dve_.sem, dve_.mark(f"B{q}"))


def compress(pr, I, O, C, W, kcD, kcS, vcP, vcS, arena, ps):
    nc = pr.nc
    X = [arena([P, 3072]) for _ in range(2)]
    w1 = [arena([P, 16, 256]) for _ in range(2)]
    w2 = [arena([P, 2, P]) for _ in range(2)]
    pos = [arena([P, 16]) for _ in range(2)]
    NSL = 4
    tin = arena([P, NSL, 4, P])
    hid = [arena([P, 2, 366]) for _ in range(2)]
    pb = arena([P, 4])
    NU = 12
    landed = [16 * sum(2 if v < 4 else 4 for v in range(u % NSL, u + 1, NSL)) for u in range(NU)]
    with pr.stage("compress", steps=["pe", "act", "dve"], sems=["w"] + [f"t{k}" for k in range(NSL)]) as (block, s):
        pe_, act_, dve_ = s["pe"], s["act"], s["dve"]

        @block.sync
        def _(sp):
            for u in range(NU):
                if u >= NSL:
                    sp.wait_ge(pe_.sem, pe_.at(("X", u - NSL)))
                st = s[f"t{u % NSL}"]
                if u < 4:
                    src = O["p_nsa_kv"][0, 0, 256 * u:256 * (u + 1), 0:2].rearrange("(q w) a g d -> q (a g) w d", w=2)
                    for w in range(2):
                        sp.dma_start(tin[:, u % NSL, :, 64 * w:64 * w + 64], src[:, :, w, :]).then_inc(st, 16)
                else:
                    for g in range(2):
                        page = sp.value_load(W["pages"][0:1, 2 * (u - 4) + g:2 * (u - 4) + g + 1], min_val=0, max_val=NPOOL - 1)
                        src = I["cache_nsa_kv"][0, bass.ds(page, 1), :, 0:2].rearrange("o (q w) a g d -> q w (o a g) d", w=2)
                        for w in range(2):
                            sp.dma_start(tin[64 * g:64 * g + 64, u % NSL, :, 64 * w:64 * w + 64], src[:, w]).then_inc(st, 16)

        @block.tensor
        def _(pe):
            def need(st, name):
                pe.wait_ge(st.sem, st.at(name))
            for u in range(NU):
                pe.wait_ge(s[f"t{u % NSL}"], landed[u])
                if u >= 2:
                    need(act_, ("X", u - 2))
                for a in range(2):
                    for g in range(2):
                        t = pe.transpose(bank(ps, u % 2)[:, P * (2 * a + g):P * (2 * a + g + 1)],
                                         tin[:, u % NSL, 2 * a + g, :], C["ident"][:])
                t.then_inc(pe_.sem, pe_.mark(("X", u)))
            pe.wait_ge(s["w"], 16 * 8)
            for kv in range(2):
                for m in range(2):
                    for a in range(16):
                        mm = pe.matmul(bank(ps, 2)[:, 2 * kv + m:2 * kv + m + 1], w1[kv][:, a, P * m:P * (m + 1)], pos[kv][:, a:a + 1],
                                       start=(a == 0), stop=(a == 15))
            mm.then_inc(pe_.sem, pe_.mark("pos"))
            need(act_, ("X", NU - 1))
            need(act_, ("X", NU - 2))
            for kv in range(2):
                xp = X[kv][:, 0:1024].rearrange("p (g n a) -> p g n a", g=2, a=8)
                xs = X[kv][:, 1024:3072].rearrange("p (b n a) -> p b n a", b=16, a=8)
                for m in range(2):
                    hb = bank(ps, 3 + 2 * kv + m)
                    for a in range(16):
                        n0 = a // 8
                        mm = pe.matmul(hb[:, 0:126].rearrange("p (g n) -> p g n", g=2), w1[kv][:, a, P * m:P * (m + 1)], xp[:, :, n0:n0 + 63, a % 8],
                                       start=(a == 0), stop=(a == 15))
                    for a in range(16):
                        n0 = a // 8
                        mm = pe.matmul(hb[:, 126:366].rearrange("p (b n) -> p b n", b=16), w1[kv][:, a, P * m:P * (m + 1)], xs[:, :, n0:n0 + 15, a % 8],
                                       start=(a == 0), stop=(a == 15))
                    mm.then_inc(pe_.sem, pe_.mark(("hid", kv, m)))
            need(act_, ("hid", 1, 1))
            for m in range(2):
                mm = pe.matmul(bank(ps, 0)[:, 0:366], w2[0][:, m, :], hid[0][:, m, :], start=(m == 0), stop=(m == 1))
            mm.then_inc(pe_.sem, pe_.mark("kc"))
            for g in range(2):
                for m in range(2):
                    mm = pe.matmul(bank(ps, 1)[0:63, 64 * g:64 * g + 64], hid[1][:, m, 63 * g:63 * g + 63], w2[1][:, m, 0:64], start=(m == 0), stop=(m == 1))
            for b in range(16):
                for m in range(2):
                    mm = pe.matmul(bank(ps, 6 + b // 8)[0:15, 64 * (b % 8):64 * (b % 8) + 64], hid[1][:, m, 126 + 15 * b:141 + 15 * b], w2[1][:, m, 0:64],
                                   start=(m == 0), stop=(m == 1))
            mm.then_inc(pe_.sem, pe_.mark("vc"))

        @block.scalar
        def _(act):
            for kv in range(2):
                act.dma_start(w1[kv], I["nsa_cmp_w1"][0, kv].rearrange("(a q) m -> q a m", q=P)).then_inc(s["w"], 16)
                for x in range(2):
                    act.dma_start(w2[kv][:, :, 64 * x:64 * x + 64], I["nsa_cmp_w2"][0, kv].rearrange("(m q) d -> q m d", q=P)).then_inc(s["w"], 16)
                act.dma_start(pos[kv], I["nsa_cmp_pos"][0, kv].rearrange("(a w) d -> (w d) a", w=2),
                             allow_slow_non_contiguous=True).then_inc(s["w"], 16)
            for u in range(NU):
                act.wait_ge(pe_.sem, pe_.at(("X", u)))
                for kv in range(2):
                    src = bank(ps, u % 2)[:, 256 * kv:256 * kv + 256].rearrange("p (g n) -> p g n", g=2)
                    if u < 4:
                        dst = X[kv][:, 0:1024].rearrange("p (g n) -> p g n", g=2)[:, :, P * u:P * (u + 1)]
                    else:
                        dst = X[kv][:, 1024 + 256 * (u - 4):1024 + 256 * (u - 3)].rearrange("p (g n) -> p g n", g=2)
                    op = nc.scalar.activation(dst, src, ACT.Copy)
                op.then_inc(act_.sem, act_.mark(("X", u)))
            act.wait_ge(dve_.sem, dve_.at("pos"))
            for kv in range(2):
                for m in range(2):
                    act.wait_ge(pe_.sem, pe_.at(("hid", kv, m)))
                    nc.scalar.activation(hid[kv][:, m, :], bank(ps, 3 + 2 * kv + m)[:, 0:366], ACT.Silu, bias=pb[:, 2 * kv + m:2 * kv + m + 1]) \
                        .then_inc(act_.sem, act_.mark(("hid", kv, m)))

        @block.vector
        def _(dve):
            V = nc.vector

            def step(name, ins):
                ins.then_inc(dve_.sem, dve_.mark(name))
            dve.wait_ge(pe_.sem, pe_.at("pos"))
            step("pos", V.tensor_copy(pb, bank(ps, 2)[:, 0:4]))
            dve.wait_ge(pe_.sem, pe_.at("kc"))
            step("kc", V.tensor_copy(kcD[:], bank(ps, 0)[:, 0:126].rearrange("p (g n) -> p g n", g=2)))
            ks = bank(ps, 0)[:, 126:366].rearrange("p (b g n) -> p b g n", b=NB, g=2)
            for g in range(2):
                step(("kcS", g), V.tensor_copy(kcS[64 * g:64 * g + 64], ks[64 * g:64 * g + 64, :, g, :]))
            dve.wait_ge(pe_.sem, pe_.at("vc"))
            step("vcP", V.tensor_copy(vcP[:], bank(ps, 1)[0:63, 0:P].rearrange("p (g d) -> p g d", g=2)))
            for x in range(2):
                step(("vcS", x), V.tensor_copy(vcS[:, 4 * x:4 * x + 4], bank(ps, 6 + x)[0:15, :].rearrange("p (b v) -> p b v", b=4)))


def load_keys(pr, I, O, C, W, kv_sel, kv_win, fv, kselD, kwinD, kf, tk, ps):
    nc = pr.nc
    with pr.stage("keys", steps=["pe", "act", "dve"], sems=["v", "k0", "k1"]) as (block, s):
        pe_, act_, dve_ = s["pe"], s["act"], s["dve"]

        @block.sync
        def _(sp):
            sp.dma_start(kv_sel[:], O["p_nsa_kv"][0, 0].rearrange("(i t) a g d -> t i (a g d)", t=P)[:, :, 256:512]).then_inc(s["v"], 16)
            sp.dma_start(kv_win[:], W["win"][0:NPROMPT].rearrange("(i t) c -> t i c", t=P)).then_inc(s["v"], 16)
            sp.dma_start(fv[:], O["p_fox_kv"][0, 0, :, 1].rearrange("(i t) h d -> t i (h d)", t=P)).then_inc(s["v"], 16)
            for i in range(NC):
                if i >= 2:
                    sp.wait_ge(pe_.sem, pe_.at(("fox", i - 2)))
                sp.dma_start(tk[:, i % 2, 0:512], O["p_fox_kv"][0, 0, P * i:P * (i + 1), 0].rearrange("t h d -> t (h d)")).then_inc(s[f"k{i % 2}"], 16)
            sp.wait_ge(s["v"], 48)

        @block.tensor
        def _(pe):
            pe.wait_ge(s["v"], 48)
            for i in range(NC):
                if i >= 2:
                    pe.wait_ge(dve_.sem, dve_.at(("nsa", i - 2)))
                    pe.wait_ge(act_.sem, act_.at(("fox", i - 2)))
                pe.wait_ge(dve_.sem, dve_.at(("twice", i)))
                for n in range(4):
                    t = pe.transpose(bank(ps, i % 2)[:, P * n:P * (n + 1)], tk[:, i % 2, 512 + P * n:512 + P * (n + 1)], C["ident"][:])
                t.then_inc(pe_.sem, pe_.mark(("nsa", i)))
                pe.wait_ge(s[f"k{i % 2}"], 16 * (i // 2 + 1))
                for j in range(4):
                    t = pe.transpose(bank(ps, 2 + i % 2)[:, P * j:P * (j + 1)], tk[:, i % 2, P * j:P * (j + 1)], C["ident"][:])
                t.then_inc(pe_.sem, pe_.mark(("fox", i)))

        @block.scalar
        def _(act):
            for i in range(NC):
                act.wait_ge(pe_.sem, pe_.at(("fox", i)))
                nc.scalar.activation(kf[:, :, P * i:P * (i + 1)], bank(ps, 2 + i % 2).rearrange("p (j t) -> p j t", j=4), ACT.Copy) \
                    .then_inc(act_.sem, act_.mark(("fox", i)))

        @block.vector
        def _(dve):
            dve.wait_ge(s["v"], 48)

            def twice(i):
                if i >= 2:
                    dve.wait_ge(pe_.sem, pe_.at(("nsa", i - 2)))
                for n, kv in enumerate((kv_sel, kv_win)):
                    dst = tk[:, i % 2, 512 + 256 * n:768 + 256 * n].rearrange("p (g o d) -> p g o d", g=2, o=2)
                    for o in range(2):
                        ins = nc.vector.tensor_copy(dst[:, :, o, :], kv[:, i, 0:P].rearrange("p (g d) -> p g d", g=2))
                ins.then_inc(dve_.sem, dve_.mark(("twice", i)))
            twice(0)
            for i in range(NC):
                if i + 1 < NC:
                    twice(i + 1)
                dve.wait_ge(pe_.sem, pe_.at(("nsa", i)))
                src = bank(ps, i % 2).rearrange("p (n g t) -> p n g t", n=2, g=2)
                nc.vector.tensor_copy(kselD[:, :, P * i:P * (i + 1)], src[:, 0])
                nc.vector.tensor_copy(kwinD[:, :, P * i:P * (i + 1)], src[:, 1]).then_inc(dve_.sem, dve_.mark(("nsa", i)))


def prompt_attention(pr, C, T, mix, ps):
    nc = pr.nc
    Q, kselD, kwinD, kf, kcD, vcP = T["Q"], T["kselD"], T["kwinD"], T["kf"], T["kcD"], T["vcP"]
    prob, probT, diag, gates, B, Bc, F = T["prob"], T["probT"], T["diag"], T["gates"], T["B"], T["Bc"], T["F"]
    nmax, rsum, coef = T["nmax"], T["rsum"], T["coef"]
    units = []
    for i in range(NC):
        for h in range(H):
            units += [(i, "sel", h), (i, "win", h), (i, "cmp", h)]
        units += [(i, "fox", h) for h in range(H)]
    U = len(units)
    head = [16 * i + (8 if kind == "fox" else 0) + h for i, kind, h in units]
    opens = [kind in ("sel", "fox") for _, kind, _ in units]
    closes = [kind in ("cmp", "fox") for _, kind, _ in units]

    def span(u):
        i, kind, h = units[u]
        if kind == "cmp":
            return 0, 8 * i + 7
        k0 = P * max(0, i - 4) if kind == "win" else 0
        return k0, P * (i + 1) - k0

    def groups(u):
        nt = -(-span(u)[1] // P)
        return [(a, min(a + 4, nt)) for a in range(0, nt, 4)]
    first_group = np.cumsum([0] + [len(groups(u)) for u in range(U)]).tolist()
    with pr.stage("attend", steps=["pe", "act", "dve"]) as (block, s):
        pe_, act_, dve_ = s["pe"], s["act"], s["dve"]

        def emptier(gi):
            return act_ if gi % 2 == 0 else dve_

        def S(u):
            return ps[:, 1024 * (u % 2):1024 * (u % 2) + 1024]

        def turned(gi):
            return bank(ps, 4 + gi % 2)

        def out(u):
            h = units[u][2]
            return bank(ps, 6 + head[u] % 2)[64 * (h % 2):64 * (h % 2) + 64, 0:P]

        def qcol(i):
            return slice(P * i, P * (i + 1))

        def empty(u, st, e):
            for x, (a, b) in enumerate(groups(u)):
                gi = first_group[u] + x
                if emptier(gi) is not st:
                    continue
                e.wait_ge(pe_.sem, pe_.at(("turn", gi)))
                if u >= 2:
                    e.wait_ge(pe_.sem, pe_.at(("pv", u - 2)))
                w = min(P, span(u)[1] - P * a)
                dst, src = probT[0:w, u % 2, a:b, :], turned(gi)[0:w, 0:P * (b - a)].rearrange("p (n t) -> p n t", t=P)
                op = nc.scalar.activation(dst, src, ACT.Copy) if st is act_ else nc.vector.tensor_copy(dst, src)
                op.then_inc(st.sem, st.mark(("turned", gi)))

        @block.tensor
        def _(pe):
            def need(st, name):
                pe.wait_ge(st.sem, st.at(name))

            def scores(u):
                i, kind, h = units[u]
                k0, n = span(u)
                if u >= 2:
                    need(act_, ("exp", u - 2))
                half = slice(64 * (h % 2), 64 * (h % 2) + 64)
                q = Q[half, (4 if kind == "fox" else 0) + h // 2, qcol(i)]
                src = {"sel": kselD, "win": kwinD, "cmp": kcD}.get(kind)
                for a in range(0, n, 512):
                    w = min(512, n - a)
                    k = kf[half, h // 2, k0 + a:k0 + a + w] if kind == "fox" else src[half, h // 4, k0 + a:k0 + a + w]
                    mm = pe.matmul(S(u)[:, a:a + w], q, k, start=True, stop=kind != "fox")
                    if kind == "fox":
                        mm = pe.matmul(S(u)[:, a:a + w], C["headsel"][half, h, :], F[half, a:a + w], start=False, stop=True)
                mm.then_inc(pe_.sem, pe_.mark(("qk", u)))

            def turn(u):
                n = span(u)[1]
                need(dve_, ("diag", u))
                for x, (a, b) in enumerate(groups(u)):
                    gi = first_group[u] + x
                    if gi >= 2:
                        need(emptier(gi - 2), ("turned", gi - 2))
                    for t in range(a, b):
                        w = min(P, n - P * t)
                        mm = pe.matmul(turned(gi)[0:w, P * (t - a):P * (t - a + 1)], prob[:, u % 2, P * t:P * t + w], diag[:, u % 2, :],
                                       start=True, stop=True)
                    mm.then_inc(pe_.sem, pe_.mark(("turn", gi)))

            def values(u):
                i, kind, h = units[u]
                k0, n = span(u)
                nt = -(-n // P)
                if opens[u] and head[u] >= 2:
                    need(act_, ("out", head[u] - 2))
                for x, (a, b) in enumerate(groups(u)):
                    gi = first_group[u] + x
                    need(emptier(gi), ("turned", gi))
                    for t in range(a, b):
                        w = min(P, n - P * t)
                        if kind == "fox":
                            v = T["fv"][:, t, HD * h:HD * (h + 1)]
                        elif kind == "cmp":
                            v = vcP[0:w, h // 4, :]
                        else:
                            kv = T["kv_sel"] if kind == "sel" else T["kv_win"]
                            v = kv[:, k0 // P + t, 128 + 64 * (h // 4):192 + 64 * (h // 4)]
                        mm = pe.matmul(out(u), v, probT[0:w, u % 2, t, :], start=(opens[u] and t == 0), stop=(closes[u] and t == nt - 1))
                mm.then_inc(pe_.sem, pe_.mark(("pv", u)))
            scores(0)
            scores(1)
            for u in range(U):
                turn(u)
                if u + 2 < U:
                    scores(u + 2)
                if u >= 1:
                    values(u - 1)
            values(U - 1)

        @block.scalar
        def _(act):
            def need(st, name):
                act.wait_ge(st.sem, st.at(name))

            def exp(u):
                need(dve_, ("max", u))
                if u >= 2:
                    need(pe_, ("turn", first_group[u - 1] - 1))
                    need(dve_, ("rec", u - 2))
                n = span(u)[1]
                nc.scalar.activation(prob[:, u % 2, 0:n], S(u)[:, 0:n], ACT.Exp, bias=nmax[:, u % 2:u % 2 + 1],
                                     accum_out=rsum[:, u % 2:u % 2 + 1]).then_inc(act_.sem, act_.mark(("exp", u)))

            def finish(u):
                if closes[u]:
                    i, kind, h = units[u]
                    need(pe_, ("pv", u))
                    nc.scalar.activation(mix[64 * (h % 2):64 * (h % 2) + 64, (4 if kind == "fox" else 0) + h // 2, qcol(i)], out(u), ACT.Copy) \
                        .then_inc(act_.sem, act_.mark(("out", head[u])))
            exp(0)
            exp(1)
            for u in range(U):
                empty(u, act_, act)
                if u + 2 < U:
                    exp(u + 2)
                if u >= 1:
                    finish(u - 1)
            finish(U - 1)

        @block.vector
        def _(dve):
            V = nc.vector

            def step(name, ins):
                ins.then_inc(dve_.sem, dve_.mark(name))

            def need(st, name):
                dve.wait_ge(st.sem, st.at(name))

            def top(u):
                i, kind, h = units[u]
                k0, n = span(u)
                need(pe_, ("qk", u))
                if kind == "cmp":
                    a = max(0, n - 16)
                    step(("bias", u), V.tensor_tensor(S(u)[:, a:n], S(u)[:, a:n], Bc[:, h, 16 - (n - a):16], ALU.add))
                elif kind == "fox":
                    step(("bias", u), V.tensor_tensor(S(u)[:, n - P:n], S(u)[:, n - P:n], C["causal"][:], ALU.add))
                else:
                    a = max(0, n - 2 * P)
                    if kind == "win" and i >= 4:
                        step(("far", u), V.tensor_tensor(S(u)[:, 0:P], S(u)[:, 0:P], C["farmask"][:], ALU.add))
                    step(("bias", u), V.tensor_tensor(S(u)[:, a:n], S(u)[:, a:n], B[:, h, 2 * P - (n - a):2 * P], ALU.add))
                need(dve_, ("bias", u))
                if u >= 2:
                    need(act_, ("exp", u - 2))
                step(("max", u), V.tensor_reduce(nmax[:, u % 2:u % 2 + 1], S(u)[:, 0:n], AX, ALU.max, negate=True))

            def scale(u):
                i, kind, h = units[u]
                need(act_, ("exp", u))
                step(("rec", u), V.reciprocal(coef[:, u % 2:u % 2 + 1], rsum[:, u % 2:u % 2 + 1]))
                need(dve_, ("rec", u))
                if u >= 2:
                    need(pe_, ("turn", first_group[u - 1] - 1))
                col = coef[:, u % 2:u % 2 + 1]
                if kind == "fox":
                    step(("diag", u), V.tensor_scalar(diag[:, u % 2, :], C["ident"][:], col, None, ALU.mult))
                else:
                    g = 3 * h + {"cmp": 0, "sel": 1, "win": 2}[kind]
                    step(("diag", u), V.tensor_scalar(diag[:, u % 2, :], C["ident"][:], col, gates[:, i, g:g + 1], ALU.mult, ALU.mult))
            top(0)
            top(1)
            scale(0)
            for u in range(U):
                if u + 1 < U:
                    scale(u + 1)
                empty(u, dve_, dve)
                if u + 2 < U:
                    top(u + 2)


def sample_attention(pr, I, O, C, W, T, mix, arena, ps):
    nc = pr.nc
    Q, gS, FS, Bs, Bcs, kcS, vcS = T["Q"], T["gS"], T["FS"], T["Bs"], T["Bcs"], T["kcS"], T["vcS"]
    Qn = arena([P, NB, NS])
    Qf = arena([P, 4, NB, NS])
    pages = [arena([P, 2, 256]) for _ in range(2)]
    wins = [arena([P, 2, 256]) for _ in range(2)]
    foxs = [arena([P, 2, 1024]) for _ in range(2)]
    new = [arena([NT, 1536]) for _ in range(2)]
    kT = arena([P, 6, TK])
    pr_ = arena([NS, 4, TK])
    pT = arena([P, 10, NS])
    nmx, rs, cf = arena([NS, 4]), arena([NS, 4]), arena([NS, 4])
    nk = [TK, TK, TK, 15]
    with pr.stage("sample", steps=["pe", "act", "dve"], sems=["in0", "in1"]) as (block, s):
        pe_, act_, dve_ = s["pe"], s["act"], s["dve"]
        OUTN = bank(ps, 6).rearrange("p (b c) -> p b c", b=NB)
        OUTF = bank(ps, 7).rearrange("p (j b c) -> p j b c", j=4, b=NB)

        @block.sync
        def _(sp):
            for b in range(NB):
                x, st = b % 2, s[f"in{b % 2}"]
                if b >= 2:
                    sp.wait_ge(pe_.sem, pe_.at(("pv", b - 2)))
                for g in range(2):
                    page = sp.value_load(W["pages"][0:1, 2 * b + g:2 * b + g + 1], min_val=0, max_val=NPOOL - 1)
                    sp.dma_start(pages[x][:, g], I["cache_nsa_kv"][0, bass.ds(page, 1), :, 2:4].rearrange("o t a g d -> t (o a g d)")).then_inc(st, 16)
                    sp.dma_start(foxs[x][:, g], I["cache_fox_kv"][0, bass.ds(page, 1)].rearrange("o t a h d -> t (o a h d)")).then_inc(st, 16)
                sp.dma_start(wins[x], I["state_nsa_win"][0, b].rearrange("(g t) a k d -> t g (a k d)", t=P)).then_inc(st, 16)
                sp.dma_start(new[x][:, 0:256], O["s_nsa_kv"][0, b, :, 2:4].rearrange("t a g d -> t (a g d)")).then_inc(st, 16)
                sp.dma_start(new[x][:, 256:512], W["win"][NPROMPT + NT * b:NPROMPT + NT * (b + 1)]).then_inc(st, 16)
                sp.dma_start(new[x][:, 512:1536], O["s_fox_kv"][0, b].rearrange("t a h d -> t (a h d)")).then_inc(st, 16)

        @block.tensor
        def _(pe):
            def need(st, name):
                pe.wait_ge(st.sem, st.at(name))
            for b in range(NB):
                x = b % 2
                pe.wait_ge(s[f"in{x}"], 128 * (b // 2 + 1))
                if b:
                    need(act_, ("pT", b - 1))
                    need(dve_, ("pT", b - 1))
                if b == 0:
                    need(dve_, ("zb", 5))
                for n in range(6):
                    for g in range(3):
                        w = P if g < 2 else NT
                        if n < 2:
                            src = (pages, wins)[n][x][:, g, 0:P] if g < 2 else new[x][:, 256 * n:256 * n + P]
                        else:
                            src = foxs[x][:, g, P * (n - 2):P * (n - 1)] if g < 2 else new[x][:, 512 + P * (n - 2):512 + P * (n - 1)]
                        t = pe.transpose(bank(ps, n)[:, P * g:P * g + w], src, C["ident"][0:w, 0:w])
                    t.then_inc(pe_.sem, pe_.mark(("kT", b, n)))
                for n in range(6):
                    e = act_ if n % 2 else dve_
                    need(e, ("kT", b, n))
                pe.matmul(bank(ps, 0)[0:NS, 0:TK], Qn[:, b, :], kT[:, 0, :], start=True, stop=True)
                pe.matmul(bank(ps, 1)[0:NS, 0:TK], Qn[:, b, :], kT[:, 1, :], start=True, stop=True)
                for j in range(4):
                    pe.matmul(bank(ps, 2)[0:NS, 0:TK], Qf[:, j, b, :], kT[:, 2 + j, :], start=(j == 0), stop=False)
                pe.matmul(bank(ps, 2)[0:NS, 0:TK], C["foxsel"][:, b, :], FS[:], start=False, stop=True)
                pe.matmul(bank(ps, 3)[0:NS, 0:15], Qn[:, b, :], kcS[:, b, :], start=True, stop=True).then_inc(pe_.sem, pe_.mark(("qk", b)))
                need(dve_, ("p", b))
                for n in range(10):
                    k, g = n // 3, n % 3
                    w = 15 if k == 3 else (P if g < 2 else NT)
                    t = pe.transpose(bank(ps, 4 + n // 5)[0:w, NS * (n % 5):NS * (n % 5 + 1)], pr_[:, k, P * g:P * g + w], C["ident"][0:NS, 0:NS])
                    if n % 5 == 4:
                        t.then_inc(pe_.sem, pe_.mark(("turn", b, n // 5)))
                need(act_, ("pT", b))
                need(dve_, ("pT", b))
                for n in range(6):
                    k, g = n // 3, n % 3
                    w = P if g < 2 else NT
                    v = (pages, wins)[k][x][:, g, P:2 * P] if g < 2 else new[x][:, 256 * k + P:256 * k + 2 * P]
                    pe.matmul(OUTN[:, b, :], v, pT[0:w, n, :], start=(n == 0), stop=False)
                pe.matmul(OUTN[:, b, :], vcS[:, b, :], pT[0:15, 9, :], start=False, stop=True)
                for j in range(4):
                    for g in range(3):
                        w = P if g < 2 else NT
                        v = foxs[x][:, g, 512 + P * j:512 + P * (j + 1)] if g < 2 else new[x][:, 1024 + P * j:1024 + P * (j + 1)]
                        mm = pe.matmul(OUTF[:, j, b, :], v, pT[0:w, 6 + g, 16 * j:16 * j + 16], start=(g == 0), stop=(g == 2))
                mm.then_inc(pe_.sem, pe_.mark(("pv", b)))

        @block.scalar
        def _(act):
            def need(st, name):
                act.wait_ge(st.sem, st.at(name))
            for b in range(NB):
                for n in (1, 3, 5):
                    need(pe_, ("kT", b, n))
                    nc.scalar.activation(kT[:, n, :], bank(ps, n)[:, 0:TK], ACT.Copy).then_inc(act_.sem, act_.mark(("kT", b, n)))
                need(dve_, ("max", b))
                for k in range(4):
                    ins = nc.scalar.activation(pr_[:, k, 0:nk[k]], bank(ps, k)[0:NS, 0:nk[k]], ACT.Exp, bias=nmx[:, k:k + 1], accum_out=rs[:, k:k + 1])
                ins.then_inc(act_.sem, act_.mark(("exp", b)))
                need(pe_, ("turn", b, 0))
                nc.scalar.activation(pT[:, 0:5, :], bank(ps, 4)[:, 0:5 * NS].rearrange("p (n c) -> p n c", n=5), ACT.Copy) \
                    .then_inc(act_.sem, act_.mark(("pT", b)))

        @block.vector
        def _(dve):
            V = nc.vector

            def step(name, ins):
                ins.then_inc(dve_.sem, dve_.mark(name))

            def need(st, name):
                dve.wait_ge(st.sem, st.at(name))
            step("z0", V.memset(Qn, 0.0))
            step("z1", V.memset(Qf, 0.0))
            for n in (4, 5):
                step(("zb", n), V.memset(bank(ps, n), 0.0))
            need(dve_, "z1")
            for h in range(H):
                g, x = h // 4, h % 2
                src = Q[64 * x:64 * x + 64, h // 2, NPROMPT:TOK].rearrange("p (b t) -> p b t", t=NT)
                step(("Qn", h), V.tensor_copy(Qn[64 * g:64 * g + 64, :, NT * h:NT * (h + 1)], src))
                src = Q[64 * x:64 * x + 64, 4 + h // 2, NPROMPT:TOK].rearrange("p (b t) -> p b t", t=NT)
                step(("Qf", h), V.tensor_copy(Qf[64 * x:64 * x + 64, h // 2, :, NT * h:NT * (h + 1)], src))
            for b in range(NB):
                for n in (0, 2, 4):
                    need(pe_, ("kT", b, n))
                    step(("kT", b, n), V.tensor_copy(kT[:, n, :], bank(ps, n)[:, 0:TK]))
                need(pe_, ("qk", b))
                for k in range(2):
                    v = bank(ps, k)[0:NS, P:TK]
                    step(("bias", b, k), V.tensor_tensor(v, v, Bs[:], ALU.add))
                v = bank(ps, 2)[0:NS, PAST:TK]
                step(("bias", b, 2), V.tensor_tensor(v, v, C["samplemask"][:], ALU.add))
                v = bank(ps, 3)[0:NS, 7:15]
                step(("bias", b, 3), V.tensor_tensor(v, v, Bcs[:], ALU.add))
                need(dve_, ("bias", b, 3))
                for k in range(4):
                    ins = V.tensor_reduce(nmx[:, k:k + 1], bank(ps, k)[0:NS, 0:nk[k]], AX, ALU.max, negate=True)
                step(("max", b), ins)
                need(act_, ("exp", b))
                step(("rec", b), V.reciprocal(cf, rs))
                need(dve_, ("rec", b))
                for k, c in ((0, 1), (1, 2), (3, 0)):
                    ins = V.tensor_tensor(cf[:, k:k + 1], cf[:, k:k + 1], gS[:, b, c:c + 1], ALU.mult)
                step(("cf", b), ins)
                need(dve_, ("cf", b))
                for k in range(4):
                    ins = V.tensor_scalar(pr_[:, k, 0:nk[k]], pr_[:, k, 0:nk[k]], cf[:, k:k + 1], None, ALU.mult)
                step(("p", b), ins)
                need(pe_, ("turn", b, 1))
                step(("pT", b), V.tensor_copy(pT[:, 5:10, :], bank(ps, 5)[:, 0:5 * NS].rearrange("p (n c) -> p n c", n=5)))
            need(pe_, ("pv", NB - 1))
            for h in range(H):
                g, x = h // 4, h % 2
                dst = mix[64 * x:64 * x + 64, h // 2, NPROMPT:TOK].rearrange("p (b t) -> p b t", t=NT)
                step(("on", h), V.tensor_copy(dst, OUTN[64 * g:64 * g + 64, :, NT * h:NT * (h + 1)]))
                dst = mix[64 * x:64 * x + 64, 4 + h // 2, NPROMPT:TOK].rearrange("p (b t) -> p b t", t=NT)
                step(("of", h), V.tensor_copy(dst, OUTF[64 * x:64 * x + 64, h // 2, :, NT * x:NT * (x + 1)]))
            step("pad", V.memset(mix[:, :, TOK:TP], 0.0))


def layer1(pr, I, O, C, xT, hn, wslots, ps):
    nc = pr.nc
    W = {"win": nc.dram_tensor("win_rows", [TOK, 256], F32).ap(), "gates": nc.dram_tensor("gate_rows", [NS, 24], F32).ap()}
    xflat, wflat = xT[:].rearrange("p k t -> p (k t)"), wslots[:].rearrange("p a k m -> p (a k m)")
    with ExitStack() as c:
        def sb(n, shape, dt=F32):
            return c.enter_context(nc.sbuf_tensor(n, shape, dt))
        T = {"Q": sb("Q", [P, 8, TP]), "gates": sb("gates", [P, NC + 1, 24]), "F": sb("F", [P, NPROMPT]), "FS": sb("FS", [NS, TK]),
             "gS": sb("gS", [NS, NB, 3]), "B": sb("B", [P, H, 256]), "Bc": sb("Bc", [P, H, 16]), "Bs": sb("Bs", [NS, P + NT]),
             "Bcs": sb("Bcs", [NS, 8]), "kcD": sb("kcD", [P, 2, 63]), "kcS": sb("kcS", [P, NB, 15]), "vcP": sb("vcP", [63, 2, HD]),
             "vcS": sb("vcS", [15, NB, P])}
        W["pages"] = sb("pages", [1, 2 * NB], I32)
        W["rowvalid"] = sb("rowvalid", [P, 1])
        W["one"] = sb("one", [NS, TK])
        with pr.stage("const1", sems=["ld"]) as (block, s):
            @block.sync
            def _(sp):
                sp.dma_start(W["pages"][:], I["page_table"].rearrange("b (g o) -> o (b g)", o=1)).then_inc(s["ld"], 16)
                sp.dma_start(W["rowvalid"][:], I["c_rowvalid"]).then_inc(s["ld"], 16)
                sp.wait_ge(s["ld"], 32)
        w = I["w_in_odd"][0]
        with ExitStack() as c2:
            wide = c2.enter_context(nc.sbuf_tensor("wide", [P, KT, 512], F32))
            rows = c2.enter_context(nc.sbuf_tensor("rows", [P, 4, 512], F32))
            token_major(pr, I, O, W, hn, wslots, wide, rows, T["gates"], ps)
            fox_rows(pr, I, O, C, hn, T["F"], T["FS"], T["gS"], W, Arena(xflat, wflat), ps)
        split(pr, "query_halves", [(hn[:, k, :], xT[:, k, :], hn[:, k, :]) for k in range(KT)])
        tiles = []
        for n in range(8):
            def scaled(e, i, acc, n=n):
                dst = v3(T["Q"][:, n, :])
                return e.tensor_scalar(dst, acc, HD ** -0.5, None, ALU.mult) if n % 2 else \
                    e.activation(dst, acc, ACT.Copy, scale=HD ** -0.5)
            c0 = P * n if n < 4 else FQ0 + P * (n - 4)
            tiles.append(dict(w=lambda i, c0=c0: w[:, c0:c0 + P], x=(xT, hn), steps=[("dve" if n % 2 else "act", scaled)]))
        with ExitStack() as c2:
            raw = c2.enter_context(nc.sbuf_tensor("raw2", [P, 2, KT, P], F32))
            stream(pr, "queries", ps, {"raw": raw, "half": [wslots[:, 0:2], wslots[:, 2:4]], "ones": C["ones"]}, 1, tiles)
        with ExitStack() as c2:
            relx = c2.enter_context(nc.sbuf_tensor("relx", [33, 8], F32))
            oh = c2.enter_context(nc.sbuf_tensor("onehot", [33, 3 * P], F32))
            rev = c2.enter_context(nc.sbuf_tensor("onehot_rev", [33, 3 * P], F32))
            bias_tables(pr, I, T["B"], T["Bc"], T["Bs"], T["Bcs"], relx, oh, rev, Arena(xflat), ps)
        with ExitStack() as c2:
            more = c2.enter_context(nc.sbuf_tensor("more", [P, 8000], F32))
            compress(pr, I, O, C, W, T["kcD"], T["kcS"], T["vcP"], T["vcS"], Arena(xflat, wflat, more[:]), ps)
        with ExitStack() as c2:
            more = c2.enter_context(nc.sbuf_tensor("more2", [P, 13000], F32))
            ar = Arena(xflat, wflat, more[:])
            for n, shape in (("kv_sel", [P, NC, 256]), ("kv_win", [P, NC, 256]), ("fv", [P, NC, 512]), ("kf", [P, 4, NPROMPT]),
                             ("kselD", [P, 2, NPROMPT]), ("kwinD", [P, 2, NPROMPT]), ("prob", [P, 2, NPROMPT])):
                T[n] = ar(shape)
            T["nmax"], T["rsum"], T["coef"] = ar([P, 2]), ar([P, 2]), ar([P, 2])
            T["diag"] = ar([P, 2, P])
            load_keys(pr, I, O, C, W, T["kv_sel"], T["kv_win"], T["fv"], T["kselD"], T["kwinD"], T["kf"], T["prob"], ps)
            T["probT"] = ar([P, 2, NC, P])
            prompt_attention(pr, C, T, hn, ps)
        with ExitStack() as c2:
            more = c2.enter_context(nc.sbuf_tensor("more3", [P, 8000], F32))
            sample_attention(pr, I, O, C, W, T, hn, Arena(xflat, wflat, more[:]), ps)


def write_y(pr, O, C, hn, rows, ps):
    nc = pr.nc
    with pr.stage("writey", steps=["pe", "act", "dve"], sems=["y0", "y1"]) as (block, s):
        pe_, act_, dve_ = s["pe"], s["act"], s["dve"]

        @block.tensor
        def _(pe):
            for i in range(NC + 1):
                r = token_rows(i)
                if i >= 2:
                    pe.wait_ge(act_.sem, act_.at(i - 2))
                    pe.wait_ge(dve_.sem, dve_.at(i - 2))
                for k in range(KT):
                    t = pe.transpose(bank(ps, 2 * (i % 2) + k // 4)[0:r, P * (k % 4):P * (k % 4 + 1)], hn[:, k, P * i:P * i + r], C["ident"][:])
                t.then_inc(pe_.sem, pe_.mark(i))

        def half(e, st, b):
            for i in range(NC + 1):
                r = token_rows(i)
                e.wait_ge(pe_.sem, pe_.at(i))
                if i >= 2:
                    e.wait_ge(s[f"y{i % 2}"], 16 * (i // 2))
                dst, src = rows[0:r, i % 2, 512 * b:512 * (b + 1)], bank(ps, 2 * (i % 2) + b)[0:r]
                op = nc.vector.tensor_copy(dst, src) if b else nc.scalar.activation(dst, src, ACT.Copy)
                op.then_inc(st.sem, st.mark(i))

        @block.scalar
        def _(act):
            half(act, act_, 0)

        @block.vector
        def _(dve):
            half(dve, dve_, 1)

        @block.sync
        def _(sp):
            for i in range(NC + 1):
                sp.wait_ge(act_.sem, act_.at(i))
                sp.wait_ge(dve_.sem, dve_.at(i))
                dst = O["y_prompt"][0, P * i:P * (i + 1), :] if i < NC else O["y_sample"].rearrange("b t d -> (b t) d")
                sp.dma_start(dst, rows[0:token_rows(i), i % 2, :]).then_inc(s[f"y{i % 2}"], 16)
            sp.wait_ge(s["y0"], 16 * 5)
            sp.wait_ge(s["y1"], 16 * 4)


def t5_bucket(n):
    n = np.maximum(n, 0)
    nf = np.maximum(n, 1).astype(np.float32)
    large = 16 + (np.log(nf / np.float32(16)) / np.float32(np.log(8.0)) * np.float32(16)).astype(np.int32)
    return np.where(n < 16, n, np.minimum(large, 31))


def constants():
    f = np.float32
    t = np.arange(P)
    k = {"ident": np.eye(P, dtype=f), "ones": np.ones((P, P), f)}
    k["maskP"] = np.where(t[:, None] <= t[None, :], 0, NEG).astype(f)
    same = t[:, None] // NT == t[None, :] // NT
    k["maskS"] = np.where((t[:, None] <= t[None, :]) & same, 0, NEG).astype(f)
    lv = []
    for n in range(7):
        z = 1 << n
        lv.append((t[:, None] // (2 * z) == t[None, :] // (2 * z)) & (t[:, None] % (2 * z) < z) & (t[None, :] % (2 * z) >= z))
    k["level"] = np.stack(lv, 1).astype(f)
    sel = np.zeros((P, 16, P), f)
    for q in range(4):
        for h in range(4):
            sel[32 * q + h, 4 * q + h, :] = 1
    k["sel"] = sel
    keep = np.ones((4, TP), f)
    keep[:, 0:NPROMPT:P] = 0
    keep[:, NPROMPT::NT] = 0
    k["keep"] = keep
    d = np.arange(-P, 2 * P)
    oh = np.zeros((33, 3 * P), f)
    oh[t5_bucket(d), np.arange(3 * P)] += 1
    oh[31] -= 1
    oh[:, d < 0] = 0
    oh[32, d < 0] = 1
    k["onehot"] = oh
    k["onehot_rev"] = oh[:, ::-1].copy()
    k["turnover"] = np.eye(P, dtype=f)[::-1].copy()
    scale = np.array([[P] * 4 + [1] * 4, [1 / P] * 8])
    k["sumsel"] = np.broadcast_to(scale[:, :, None] * np.eye(8), (P, 2, 8, 8)).astype(f)
    k["epsrow"] = np.array([[P * EPS] * 4 + [EPS] * 4, [EPS] * 8])[:, :, None].astype(f)
    k["rowsel"] = np.broadcast_to(np.eye(8)[:, :, None], (8, 8, P)).astype(f)
    k["causal"] = np.where(t[None, :] > t[:, None], NEG, 0).astype(f)
    k["farmask"] = np.where(t[None, :] <= t[:, None], NEG, 0).astype(f)
    k["rowvalid"] = (t >= 31).astype(f)[:, None]
    row = np.arange(NS)
    k["samplemask"] = np.where(np.arange(NT)[None, :] > (row % NT)[:, None], NEG, 0).astype(f)
    fs = np.zeros((NS, NB, NS), f)
    for b in range(NB):
        for r in range(NS):
            fs[NT * b + r // NT, b, r] = -1
    k["foxsel"] = fs
    hs = np.zeros((P, 8, P), f)
    for h in range(8):
        hs[h, h] = hs[64 + h, h] = -1
    k["headsel"] = hs
    return k


def load_constants(pr, I, names, tiles, stage="const"):
    with pr.stage(stage, sems=["ld"]) as (block, s):
        @block.sync
        def _(sp):
            for n in names:
                sp.dma_start(tiles[n][:], I["c_" + n]).then_inc(s["ld"], 16)
            sp.wait_ge(s["ld"], 16 * len(names))


def diag_in(t):
    return t[:].rearrange("p k t -> p (k t)")[:, 0:(NC + 1) * P].rearrange("p (i n) -> p i n", n=P)


def program(nc, I, O, values):
    pr = Program(nc, values)
    with ExitStack() as c:
        xT = two_ways(nc, c, "xT", [P, KT, TP])
        C = {}
        for n in ("ident", "ones"):
            C[n] = c.enter_context(nc.sbuf_tensor("sb_" + n, list(I["c_" + n].shape), F32))
        ps = c.enter_context(nc.psum_tensor("ps", [P, 8 * 512], F32))
        load_constants(pr, I, list(C), C)
        load_x(pr, I, xT, C["ident"], ps)
        with ExitStack() as c2:
            hn = two_ways(nc, c2, "hn", [P, KT, TP])
            wslots = two_ways(nc, c2, "wslots", [P, 4, KT, P])
            layer0(pr, I, O, C, xT, hn, wslots, ps)
            half = [wslots[:, 0:2], wslots[:, 2:4]]
            flat = xT[:].rearrange("p k t -> p (k t)")
            saved = nc.dram_tensor("x_saved1", [P, KT * TP], F32).ap()
            for layer in (0, 1):
                with ExitStack() as c3:
                    low = two_ways(nc, c3, f"low{layer}", [P, KT, TP])
                    raw = c3.enter_context(nc.sbuf_tensor(f"rawm{layer}", [P, 2, KT, P], F32))
                    W = {"raw": raw, "half": half, "ones": C["ones"]}
                    if layer:
                        split(pr, "mixed_halves", [(hn[:, k, :], low[:, k, :], hn[:, k, :]) for k in range(KT)], copy=(flat, saved))
                        residual_product(pr, "wout1", I["w_out_odd"][0], (low, hn), xT, W, ps)
                    u = [two_ways(nc, c3, f"u{layer}{n}", [P, KT, TP]) for n in (0, 1)]
                    rmsnorm(pr, f"norm_mlp{layer}", xT, hn, u[0][:, 0], diag_in(u[1]), I["norm_mlp"][layer], C["ident"], C["ones"], ps, low=low)
                    mlp(pr, I, layer, xT, (hn, low), u, W, ps)
                    if layer:
                        rmsnorm(pr, "norm4", xT, hn, u[0][:, 0], diag_in(u[1]), I["norm_final"], C["ident"], C["ones"], ps)
                        write_y(pr, O, C, hn, low[:].rearrange("p k t -> p (k t)")[:, 0:2 * DM].rearrange("p (a n) -> p a n", a=2), ps)
                        continue
                with ExitStack() as c3:
                    names1 = ["causal", "farmask", "samplemask", "foxsel", "headsel"]
                    C1 = dict(C)
                    for n in names1:
                        C1[n] = c3.enter_context(nc.sbuf_tensor("sb_" + n, list(I["c_" + n].shape), F32))
                    load_constants(pr, I, names1, C1, "const2")
                    with ExitStack() as c4:
                        total = c4.enter_context(nc.sbuf_tensor("total", [P, TP], F32))
                        diag = c4.enter_context(nc.sbuf_tensor("diag", [P, NC + 1, P], F32))
                        rmsnorm(pr, "norm2", xT, hn, total[:], diag[:], I["norm_mix"][1], C["ident"], C["ones"], ps, save=saved)
                    layer1(pr, I, O, C1, xT, hn, wslots, ps)
    return pr.found


_OUTS = [
    ("y_prompt", (1, 1024, 1024)), ("y_sample", (8, 8, 1024)),
    ("p_mlstm_c", (1, 1, 4, 64, 128)), ("p_mlstm_n", (1, 1, 4, 64)), ("p_mlstm_m", (1, 1, 4)), ("p_gdn_s", (1, 1, 4, 128, 128)),
    ("p_gdn_conv", (1, 1, 3, 1536)), ("p_nsa_kv", (1, 1, 1024, 4, 2, 64)), ("p_nsa_win", (1, 1, 256, 2, 2, 64)),
    ("p_fox_kv", (1, 1, 1024, 2, 8, 64)), ("p_fox_logf", (1, 1, 1024, 8)),
    ("s_mlstm_c", (1, 8, 4, 64, 128)), ("s_mlstm_n", (1, 8, 4, 64)), ("s_mlstm_m", (1, 8, 4)), ("s_gdn_s", (1, 8, 4, 128, 128)),
    ("s_gdn_conv", (1, 8, 3, 1536)), ("s_nsa_kv", (1, 8, 8, 4, 2, 64)), ("s_nsa_win", (1, 8, 256, 2, 2, 64)),
    ("s_fox_kv", (1, 8, 8, 2, 8, 64)), ("s_fox_logf", (1, 8, 8, 8)),
]


def kernel(**inputs):
    import concourse.bacc as _bacc
    from concourse.bass_utils import run_bass_kernel_spmd as _run

    arrays = {f"in_{k}": np.ascontiguousarray(v) for k, v in inputs.items()}
    arrays.update({f"in_c_{k}": np.ascontiguousarray(v) for k, v in constants().items()})

    def build(values):
        nc = _bacc.Bacc("TRN2", target_bir_lowering=False, num_devices=1)
        ins = {k[3:]: nc.dram_tensor(k, v.shape, mybir.dt.from_np(v.dtype), kind="ExternalInput").ap() for k, v in arrays.items()}
        outs = {k: nc.dram_tensor(f"out_{k}", s, F32, kind="ExternalOutput").ap() for k, s in _OUTS}
        return nc, program(nc, ins, outs, values)
    _, values = build({})
    nc, _ = build(values)
    r = _run(nc, [arrays], core_ids=[0])
    return tuple(r.results[0][f"out_{k}"] for k, _ in _OUTS)
```
